# Optimizing a Trainium2 kernel written in Bass

```python
import math
import jax, jax.numpy as jnp
from jax import lax
import numpy as np

D_MODEL = 1024
BATCH = 1
SEQ = 256
DEPTH = 1

M_HEADS = 4
M_V_WIDTH = 2 * D_MODEL
M_QK_WIDTH = D_MODEL
M_DV = M_V_WIDTH // M_HEADS
M_DK = M_QK_WIDTH // M_HEADS
M_CHUNK = 128
CONV_K = 4
A_HEADS = D_MODEL // 128
A_DH = 64
A_QK_WIDTH = A_HEADS * 2 * A_DH
A_V_WIDTH = A_HEADS * 2 * A_DH
Q_BLOCK = 128
REL_BUCKETS = 32
REL_MAX_DIST = 128
EPS = 1e-6

SPLITS = (M_QK_WIDTH, M_QK_WIDTH, M_V_WIDTH, M_V_WIDTH, M_V_WIDTH, M_HEADS, M_HEADS,
          A_QK_WIDTH, A_QK_WIDTH, A_V_WIDTH, A_V_WIDTH, D_MODEL, D_MODEL)
N_IN = 3 * M_QK_WIDTH - M_QK_WIDTH + 3 * M_V_WIDTH + 2 * M_HEADS + 2 * A_QK_WIDTH + 2 * A_V_WIDTH + 2 * D_MODEL


def rmsnorm(x, g):
    xf = x.astype(jnp.float32)
    y = xf * lax.rsqrt(jnp.mean(xf * xf, axis=-1, keepdims=True) + EPS)
    return (y * g.astype(jnp.float32)).astype(x.dtype)

def head_rmsnorm(x, n_heads, g):
    B, S, W = x.shape
    xf = x.astype(jnp.float32).reshape(B, S, n_heads, W // n_heads)
    xf = xf * lax.rsqrt(jnp.mean(xf * xf, axis=-1, keepdims=True) + EPS)
    return (xf.reshape(B, S, W) * g.astype(jnp.float32)).astype(x.dtype)

def causal_dwconv(x, w, b):
    S = x.shape[1]
    xp = jnp.pad(x, ((0, 0), (CONV_K - 1, 0), (0, 0)))
    y = xp[:, CONV_K - 1:CONV_K - 1 + S] * w[CONV_K - 1] + b
    for j in range(CONV_K - 1):
        y = y + xp[:, j:j + S] * w[j]
    return y

def t5_bucket(n):
    max_exact = REL_BUCKETS // 2
    nf = jnp.maximum(n, 1).astype(jnp.float32)
    large = max_exact + (jnp.log(nf / max_exact) / math.log(REL_MAX_DIST / max_exact)
                         * (REL_BUCKETS - max_exact)).astype(jnp.int32)
    large = jnp.minimum(large, REL_BUCKETS - 1)
    return jnp.where(n < max_exact, n, large)

def mlstm_chunkwise(q, k, v, i_pre, f_pre):
    in_dtype = v.dtype
    B, S, H, dk = q.shape
    dv = v.shape[-1]
    nc = S // M_CHUNK
    L = M_CHUNK
    f32 = jnp.float32

    def chunks4(t):
        return t.astype(f32).reshape(B, nc, L, H, t.shape[-1]).transpose(1, 0, 3, 2, 4)

    def chunks3(t):
        return t.astype(f32).reshape(B, nc, L, H).transpose(1, 0, 3, 2)

    qc = chunks4(q)
    kc = chunks4(k) * (dk ** -0.5)
    vc = chunks4(v)
    ic = chunks3(i_pre)
    lfc = jax.nn.log_sigmoid(chunks3(f_pre))
    causal = jnp.tril(jnp.ones((L, L), dtype=bool))

    def step(carry, xs):
        C, n, m = carry
        qx, kx, vx, ix, lfx = xs
        b = jnp.cumsum(lfx, axis=-1)
        D = b[..., :, None] - b[..., None, :] + ix[..., None, :]
        D = jnp.where(causal, D, -jnp.inf)
        inter = b + m[..., None]
        m_t = jnp.maximum(inter, jnp.max(D, axis=-1))
        w_inter = jnp.exp(inter - m_t)
        s = jnp.einsum('bhtd,bhsd->bhts', qx, kx) * jnp.exp(D - m_t[..., None])
        num = (w_inter[..., None] * jnp.einsum('bhvd,bhtd->bhtv', C, qx)
               + jnp.einsum('bhts,bhsv->bhtv', s, vx))
        den = w_inter * jnp.einsum('bhd,bhtd->bht', n, qx) + jnp.sum(s, axis=-1)
        h = num / jnp.maximum(jnp.abs(den), jnp.exp(-m_t))[..., None]
        bL = b[..., -1]
        g = bL[..., None] - b + ix
        m_new = jnp.maximum(bL + m, jnp.max(g, axis=-1))
        decay = jnp.exp(bL + m - m_new)
        wk = jnp.exp(g - m_new[..., None])
        C_new = decay[..., None, None] * C + jnp.einsum('bhsv,bhsd->bhvd', vx * wk[..., None], kx)
        n_new = decay[..., None] * n + jnp.einsum('bhs,bhsd->bhd', wk, kx)
        return (C_new, n_new, m_new), h

    init = (jnp.zeros((B, H, dv, dk), f32), jnp.zeros((B, H, dk), f32), jnp.zeros((B, H), f32))
    _, hs = lax.scan(step, init, (qc, kc, vc, ic, lfc))
    return hs.transpose(1, 0, 3, 2, 4).reshape(B, S, H, dv).astype(in_dtype)

def diff_attention(q, k, v, lam, rel_bias):
    in_dtype = v.dtype
    f32 = jnp.float32
    S = q.shape[1]
    qh = q.astype(f32).transpose(0, 2, 3, 1, 4) * (A_DH ** -0.5)
    kh = k.astype(f32).transpose(0, 2, 3, 1, 4)
    vh = v.astype(f32).transpose(0, 2, 1, 3)
    table = rel_bias.astype(f32)
    outs = []
    for blk in range(S // Q_BLOCK):
        q0 = blk * Q_BLOCK
        end = q0 + Q_BLOCK
        rel = jnp.arange(q0, end)[:, None] - jnp.arange(end)[None, :]
        bias = table[t5_bucket(jnp.maximum(rel, 0))]
        bias = jnp.where((rel >= 0)[..., None], bias, -jnp.inf).transpose(2, 0, 1)
        logits = jnp.einsum('bhmqd,bhmkd->bhmqk', qh[:, :, :, q0:end], kh[:, :, :, :end])
        p = jax.nn.softmax(logits + bias[None, :, None], axis=-1)
        a = p[:, :, 0] - lam * p[:, :, 1]
        outs.append(jnp.einsum('bhqk,bhkd->bhqd', a, vh[:, :, :end]))
    o = jnp.concatenate(outs, axis=2)
    return o.transpose(0, 2, 1, 3).astype(in_dtype)

def first_inputs(seed: int = 0) -> dict:
    key = jax.random.key(seed)
    ks = jax.random.split(key, 24)
    nrm = jax.random.normal
    f32 = jnp.float32
    x = nrm(ks[0], (BATCH, SEQ, D_MODEL), f32)
    c = nrm(ks[1], (BATCH, D_MODEL), f32)
    norm_g = 1.0 + 0.05 * nrm(ks[2], (DEPTH, D_MODEL), f32)
    w_ada = 0.5 * D_MODEL ** -0.5 * nrm(ks[3], (DEPTH, D_MODEL, 3 * D_MODEL), f32)
    b_ada = 0.02 * nrm(ks[4], (DEPTH, 3 * D_MODEL), f32)
    w_in = D_MODEL ** -0.5 * nrm(ks[5], (DEPTH, D_MODEL, N_IN), f32)
    b_i = 0.1 * nrm(ks[6], (DEPTH, M_HEADS), f32)
    b_f = jnp.linspace(3.0, 6.0, M_HEADS, dtype=f32)[None] + 0.1 * nrm(ks[7], (DEPTH, M_HEADS), f32)
    b_if = jnp.concatenate([b_i, b_f], axis=-1)
    conv_w = CONV_K ** -0.5 * nrm(ks[8], (DEPTH, CONV_K, 2 * M_QK_WIDTH), f32)
    conv_b = 0.02 * nrm(ks[9], (DEPTH, 2 * M_QK_WIDTH), f32)
    mnorm_g = 1.0 + 0.05 * nrm(ks[10], (DEPTH, M_V_WIDTH), f32)
    w_proj_m = M_V_WIDTH ** -0.5 * nrm(ks[11], (DEPTH, M_V_WIDTH, D_MODEL), f32)
    lam_q1 = 0.1 * nrm(ks[12], (DEPTH, A_DH), f32)
    lam_k1 = 0.1 * nrm(ks[13], (DEPTH, A_DH), f32)
    lam_q2 = 0.1 * nrm(ks[14], (DEPTH, A_DH), f32)
    lam_k2 = 0.1 * nrm(ks[15], (DEPTH, A_DH), f32)
    anorm_g = 1.0 + 0.05 * nrm(ks[16], (DEPTH, A_V_WIDTH), f32)
    w_proj_a = A_V_WIDTH ** -0.5 * nrm(ks[17], (DEPTH, A_V_WIDTH, D_MODEL), f32)
    w_out = D_MODEL ** -0.5 * nrm(ks[18], (DEPTH, D_MODEL, D_MODEL), f32)
    rel_bias = 0.5 * nrm(ks[19], (REL_BUCKETS, A_HEADS), f32)
    final_g = 1.0 + 0.05 * nrm(ks[20], (D_MODEL,), f32)
    return {"x": x, "c": c, "norm_g": norm_g, "w_ada": w_ada, "b_ada": b_ada, "w_in": w_in,
            "b_if": b_if, "conv_w": conv_w, "conv_b": conv_b, "mnorm_g": mnorm_g, "w_proj_m": w_proj_m,
            "lam_q1": lam_q1, "lam_k1": lam_k1, "lam_q2": lam_q2, "lam_k2": lam_k2, "anorm_g": anorm_g,
            "w_proj_a": w_proj_a, "w_out": w_out, "rel_bias": rel_bias, "final_g": final_g}

def first_block(x, c, norm_g, w_ada, b_ada, w_in, b_if, conv_w, conv_b, mnorm_g, w_proj_m,
              lam_q1, lam_k1, lam_q2, lam_k2, anorm_g, w_proj_a, w_out, rel_bias, final_g):
    B, S, _ = x.shape
    split_idx = np.cumsum(np.array(SPLITS))[:-1].tolist()
    c_act = jax.nn.silu(c)
    for l in range(DEPTH):
        mod = c_act @ w_ada[l] + b_ada[l]
        shift, scale, gate = jnp.split(mod, 3, axis=-1)
        h = rmsnorm(x, norm_g[l]) * (1.0 + scale[:, None]) + shift[:, None]

        proj = h @ w_in[l]
        (qm, km, vm, om, zm, im, fm, qa, ka, va, za, gm, ga) = jnp.split(proj, split_idx, axis=-1)

        qk = jax.nn.silu(causal_dwconv(jnp.concatenate([qm, km], axis=-1), conv_w[l], conv_b[l]))
        qm, km = jnp.split(qk, 2, axis=-1)
        im = im + b_if[l, :M_HEADS]
        fm = fm + b_if[l, M_HEADS:]
        hm = mlstm_chunkwise(qm.reshape(B, S, M_HEADS, M_DK), km.reshape(B, S, M_HEADS, M_DK),
                             vm.reshape(B, S, M_HEADS, M_DV), im, fm)
        hm = jax.nn.sigmoid(om) * hm.reshape(B, S, M_V_WIDTH)
        hm = head_rmsnorm(hm, M_HEADS, mnorm_g[l]) * jax.nn.silu(zm)
        ym = hm @ w_proj_m[l]

        lam_init = 0.8 - 0.6 * math.exp(-0.3 * l)
        lam = (jnp.exp(jnp.sum(lam_q1[l].astype(jnp.float32) * lam_k1[l].astype(jnp.float32)))
               - jnp.exp(jnp.sum(lam_q2[l].astype(jnp.float32) * lam_k2[l].astype(jnp.float32)))
               + lam_init)
        ha = diff_attention(qa.reshape(B, S, A_HEADS, 2, A_DH), ka.reshape(B, S, A_HEADS, 2, A_DH),
                            va.reshape(B, S, A_HEADS, 2 * A_DH), lam, rel_bias)
        ha = head_rmsnorm(ha.reshape(B, S, A_V_WIDTH), A_HEADS, anorm_g[l]) * (1.0 - lam_init)
        ha = ha * jax.nn.silu(za)
        ya = ha @ w_proj_a[l]

        y = jax.nn.sigmoid(gm) * ym + jax.nn.sigmoid(ga) * ya
        x = x + gate[:, None] * (y @ w_out[l])
    return rmsnorm(x, final_g)


GRID_W = 64
CTX_LEN = 256
CONV_WIDTH = D_MODEL // 2
RET_HEADS = 4
RET_HEAD_DIM = (D_MODEL - CONV_WIDTH) // RET_HEADS
RET_WIDTH = RET_HEADS * RET_HEAD_DIM
MIX_WIDTH = CONV_WIDTH + RET_WIDTH
RET_CHUNK = 128
ROPE_BASE = 10000.0
N_EXPERTS = 16
EC_CAPACITY_FACTOR = 2
D_EXPERT = 2 * D_MODEL
RMS_EPS = 1e-6
GN_EPS = 1e-6
SPLITS_2 = (CONV_WIDTH, CONV_WIDTH, CONV_WIDTH, RET_WIDTH, RET_WIDTH, RET_WIDTH, RET_WIDTH)
IN_COLS = sum(SPLITS_2)
SPLIT_IDX = tuple(int(s) for s in np.cumsum(SPLITS_2)[:-1])


def _rms_norm(x, g):
    xf = x.astype(jnp.float32)
    y = xf * lax.rsqrt(jnp.mean(xf * xf, axis=-1, keepdims=True) + RMS_EPS)
    return (y * g.astype(jnp.float32)).astype(x.dtype)

def _modulation(cond, w_ada, b_ada):
    m = jax.nn.silu(cond) @ w_ada + b_ada
    return jnp.split(m[:, None, :], 6, axis=-1)

def _rotary(t, pos):
    half = t.shape[-1] // 2
    inv = 1.0 / (ROPE_BASE ** (jnp.arange(half, dtype=jnp.float32) / half))
    ang = pos[:, None] * inv[None, :]
    cos = jnp.cos(ang)[None, :, None, :]
    sin = jnp.sin(ang)[None, :, None, :]
    t1, t2 = t[..., :half], t[..., half:]
    return jnp.concatenate([t1 * cos - t2 * sin, t1 * sin + t2 * cos], axis=-1)

def _ret_qkv(q, k, v, pos):
    b, n, _ = q.shape
    shp = (b, n, RET_HEADS, RET_HEAD_DIM)
    q = _rotary(q.reshape(shp).astype(jnp.float32), pos)
    k = _rotary(k.reshape(shp).astype(jnp.float32), pos) * (RET_HEAD_DIM ** -0.5)
    v = v.reshape(shp).astype(jnp.float32)
    return q, k, v

def _retention_scan(q, k, v, log_g, s0, include_self):
    b, n, h, d = q.shape
    nc = n // RET_CHUNK
    qc = q.reshape(b, nc, RET_CHUNK, h, d)
    kc = k.reshape(b, nc, RET_CHUNK, h, d)
    vc = v.reshape(b, nc, RET_CHUNK, h, d)
    idx = jnp.arange(RET_CHUNK, dtype=jnp.float32)
    rel = idx[:, None] - idx[None, :]
    mask = (rel >= 0) if include_self else (rel > 0)
    decay = jnp.where(mask[None], jnp.exp(log_g[:, None, None] * jnp.where(mask, rel, 0.0)[None]), 0.0)
    scores = jnp.einsum('bcihd,bcjhd->bchij', qc, kc) * decay[None, None]
    intra = jnp.einsum('bchij,bcjhd->bcihd', scores, vc)
    zeta = jnp.exp(log_g[None, :] * (RET_CHUNK - 1.0 - idx)[:, None])
    u = jnp.einsum('bcjhd,bcjhe->bchde', kc * zeta[None, None, :, :, None], vc)
    g_chunk = jnp.exp(log_g * RET_CHUNK)[None, :, None, None]

    def step(s, u_c):
        return g_chunk * s + u_c, s

    s_final, s_prev = lax.scan(step, s0, jnp.moveaxis(u, 1, 0))
    s_prev = jnp.moveaxis(s_prev, 0, 1)
    xi = jnp.exp(log_g[None, :] * (idx + 1.0)[:, None])
    inter = jnp.einsum('bcihd,bchde->bcihe', qc, s_prev) * xi[None, None, :, :, None]
    return (intra + inter).reshape(b, n, h, d), s_final

def _bidir_retention(q, k, v, log_gf, log_gb, s0_f, s0_b):
    y_f, s_f = _retention_scan(q, k, v, log_gf, s0_f, True)
    flip = lambda t: jnp.flip(t, axis=1)
    y_b, s_b = _retention_scan(flip(q), flip(k), flip(v), log_gb, s0_b, False)
    return y_f + flip(y_b), s_f, s_b

def _context_states(k, v, log_gf, log_gb):
    n = k.shape[1]
    pos = jnp.arange(n, dtype=jnp.float32)
    wf = jnp.exp(log_gf[None, :] * (n - 1.0 - pos)[:, None])
    wb = jnp.exp(log_gb[None, :] * pos[:, None])
    s_f = jnp.einsum('bnhd,nh,bnhe->bhde', k, wf, v)
    s_b = jnp.einsum('bnhd,nh,bnhe->bhde', k, wb, v)
    return s_f, s_b

def _ret_out(y, g, norm_g):
    b, n, _, _ = y.shape
    mu = jnp.mean(y, axis=-1, keepdims=True)
    var = jnp.mean(jnp.square(y - mu), axis=-1, keepdims=True)
    yn = ((y - mu) * lax.rsqrt(var + GN_EPS)).reshape(b, n, RET_WIDTH) * norm_g.astype(jnp.float32)
    return (jax.nn.silu(g.astype(jnp.float32)) * yn).astype(g.dtype)

def _conv_branch(gate_b, gate_c, u_in, w, bias, rows, width):
    bsz, n, ch = u_in.shape
    u = (gate_c * u_in).reshape(bsz, rows, width, ch)
    up = jnp.pad(u, ((0, 0), (0, 0), (1, 1), (0, 0)))
    y = up[:, :, :-2] * w[0] + up[:, :, 1:-1] * w[1] + up[:, :, 2:] * w[2] + bias
    return gate_b * y.reshape(bsz, n, ch)

def _expert_choice_ffn(h, w_router, b_router, w_gate, w_up, w_down):
    b, n, d = h.shape
    cap = max(1, EC_CAPACITY_FACTOR * n // N_EXPERTS)
    logits = h.astype(jnp.float32) @ w_router.astype(jnp.float32) + b_router.astype(jnp.float32)
    aff = jax.nn.softmax(logits, axis=-1)
    gate, idx = lax.top_k(jnp.swapaxes(aff, 1, 2), cap)
    xs = jax.vmap(lambda hb, ib: hb[ib])(h, idx)
    a = jnp.einsum('becd,edf->becf', xs, w_gate)
    u = jnp.einsum('becd,edf->becf', xs, w_up)
    y = jnp.einsum('becf,efd->becd', jax.nn.silu(a) * u, w_down) * gate[..., None].astype(h.dtype)
    return jax.vmap(lambda yb, ib: jnp.zeros((n, d), yb.dtype).at[ib.reshape(-1)].add(yb.reshape(-1, d)))(y, idx)

def second_inputs(seed: int = 0) -> dict:
    key = jax.random.key(seed)
    ks = jax.random.split(key, 22)
    f32 = jnp.float32

    def nrm(k, shape, scale):
        return jax.random.normal(k, shape, f32) * scale

    decay_base = jnp.log(2.0 ** (5.0 + jnp.arange(RET_HEADS, dtype=f32)) - 1.0)
    return {
        "x": nrm(ks[0], (BATCH, SEQ, D_MODEL), 1.0),
        "c": nrm(ks[1], (BATCH, D_MODEL), 1.0),
        "ctx": nrm(ks[2], (BATCH, CTX_LEN, D_MODEL), 1.0),
        "c_ctx": nrm(ks[3], (D_MODEL,), 1.0),
        "w_ada": nrm(ks[4], (DEPTH, D_MODEL, 6 * D_MODEL), 0.5 * D_MODEL ** -0.5),
        "b_ada": nrm(ks[5], (DEPTH, 6 * D_MODEL), 0.02),
        "pre_mix_g": 1.0 + nrm(ks[6], (DEPTH, D_MODEL), 0.05),
        "post_mix_g": 1.0 + nrm(ks[7], (DEPTH, D_MODEL), 0.05),
        "pre_ffn_g": 1.0 + nrm(ks[8], (DEPTH, D_MODEL), 0.05),
        "post_ffn_g": 1.0 + nrm(ks[9], (DEPTH, D_MODEL), 0.05),
        "w_in": nrm(ks[10], (DEPTH, D_MODEL, IN_COLS), D_MODEL ** -0.5),
        "conv_w": nrm(ks[11], (DEPTH, 3, CONV_WIDTH), 3.0 ** -0.5),
        "conv_b": nrm(ks[12], (DEPTH, CONV_WIDTH), 0.02),
        "ret_decay_logit": decay_base[None, None, :] + nrm(ks[13], (DEPTH, 2, RET_HEADS), 0.1),
        "ret_norm_g": 1.0 + nrm(ks[14], (DEPTH, RET_WIDTH), 0.05),
        "w_out": nrm(ks[15], (DEPTH, MIX_WIDTH, D_MODEL), MIX_WIDTH ** -0.5),
        "w_router": nrm(ks[16], (DEPTH, D_MODEL, N_EXPERTS), D_MODEL ** -0.5),
        "b_router": nrm(ks[17], (DEPTH, N_EXPERTS), 0.01),
        "w_gate": nrm(ks[18], (DEPTH, N_EXPERTS, D_MODEL, D_EXPERT), D_MODEL ** -0.5),
        "w_up": nrm(ks[19], (DEPTH, N_EXPERTS, D_MODEL, D_EXPERT), D_MODEL ** -0.5),
        "w_down": nrm(ks[20], (DEPTH, N_EXPERTS, D_EXPERT, D_MODEL), D_EXPERT ** -0.5),
    }

def second_block(x, c, ctx, c_ctx, w_ada, b_ada, pre_mix_g, post_mix_g, pre_ffn_g, post_ffn_g,
              w_in, conv_w, conv_b, ret_decay_logit, ret_norm_g, w_out,
              w_router, b_router, w_gate, w_up, w_down):
    n_lat = x.shape[1]
    ctx_len = ctx.shape[1]
    rows = n_lat // GRID_W
    pos_ctx = jnp.arange(ctx_len, dtype=jnp.float32)
    pos_lat = ctx_len + jnp.arange(n_lat, dtype=jnp.float32)
    bsz = x.shape[0]
    zero_state = jnp.zeros((bsz, RET_HEADS, RET_HEAD_DIM, RET_HEAD_DIM), jnp.float32)

    for i in range(DEPTH):
        last = i == DEPTH - 1
        sh1, sc1, g1, sh2, sc2, g2 = _modulation(c, w_ada[i], b_ada[i])
        csh1, csc1, cg1, csh2, csc2, cg2 = _modulation(c_ctx[None, :], w_ada[i], b_ada[i])
        log_gf = jax.nn.log_sigmoid(ret_decay_logit[i, 0].astype(jnp.float32))
        log_gb = jax.nn.log_sigmoid(ret_decay_logit[i, 1].astype(jnp.float32))

        hc = _rms_norm(ctx, pre_mix_g[i]) * (1.0 + csc1) + csh1
        c_b, c_c, c_x, c_q, c_k, c_v, c_g = jnp.split(hc @ w_in[i], SPLIT_IDX, axis=-1)
        qc, kc, vc = _ret_qkv(c_q, c_k, c_v, pos_ctx)
        if last:
            s_f, s_b = _context_states(kc, vc, log_gf, log_gb)
            ctx_next = ctx
        else:
            yc, s_f, s_b = _bidir_retention(qc, kc, vc, log_gf, log_gb, zero_state, zero_state)
            mix_c = jnp.concatenate([
                _conv_branch(c_b, c_c, c_x, conv_w[i], conv_b[i], 1, ctx_len),
                _ret_out(yc, c_g, ret_norm_g[i])], axis=-1) @ w_out[i]
            ctx_mid = ctx + cg1 * _rms_norm(mix_c, post_mix_g[i])
            hc2 = _rms_norm(ctx_mid, pre_ffn_g[i]) * (1.0 + csc2) + csh2
            ffn_c = _expert_choice_ffn(hc2, w_router[i], b_router[i], w_gate[i], w_up[i], w_down[i])
            ctx_next = ctx_mid + cg2 * _rms_norm(ffn_c, post_ffn_g[i])

        hx = _rms_norm(x, pre_mix_g[i]) * (1.0 + sc1) + sh1
        x_b, x_c, x_x, x_q, x_k, x_v, x_g = jnp.split(hx @ w_in[i], SPLIT_IDX, axis=-1)
        qx, kx, vx = _ret_qkv(x_q, x_k, x_v, pos_lat)
        yx, _, _ = _bidir_retention(qx, kx, vx, log_gf, log_gb, s_f, s_b)
        mix_x = jnp.concatenate([
            _conv_branch(x_b, x_c, x_x, conv_w[i], conv_b[i], rows, GRID_W),
            _ret_out(yx, x_g, ret_norm_g[i])], axis=-1) @ w_out[i]
        x = x + g1 * _rms_norm(mix_x, post_mix_g[i])
        hx2 = _rms_norm(x, pre_ffn_g[i]) * (1.0 + sc2) + sh2
        ffn_x = _expert_choice_ffn(hx2, w_router[i], b_router[i], w_gate[i], w_up[i], w_down[i])
        x = x + g2 * _rms_norm(ffn_x, post_ffn_g[i])
        ctx = ctx_next
    return x


def setup_inputs(seed=0):
    out = dict(first_inputs(seed))
    for name, value in second_inputs(seed + 1).items():
        if name != "x":
            out[name + "_2"] = value
    return out


def reference(
    x, c, norm_g, w_ada, b_ada, w_in, b_if, conv_w, conv_b, mnorm_g, w_proj_m, lam_q1, lam_k1,
    lam_q2, lam_k2, anorm_g, w_proj_a, w_out, rel_bias, final_g, c_2, ctx_2, c_ctx_2, w_ada_2,
    b_ada_2, pre_mix_g_2, post_mix_g_2, pre_ffn_g_2, post_ffn_g_2, w_in_2, conv_w_2, conv_b_2,
    ret_decay_logit_2, ret_norm_g_2, w_out_2, w_router_2, b_router_2, w_gate_2, w_up_2,
    w_down_2,
):
    x = first_block(
        x, c, norm_g, w_ada, b_ada, w_in, b_if, conv_w, conv_b, mnorm_g, w_proj_m, lam_q1,
        lam_k1, lam_q2, lam_k2, anorm_g, w_proj_a, w_out, rel_bias, final_g,
    )
    return second_block(
        x, c_2, ctx_2, c_ctx_2, w_ada_2, b_ada_2, pre_mix_g_2, post_mix_g_2, pre_ffn_g_2,
        post_ffn_g_2, w_in_2, conv_w_2, conv_b_2, ret_decay_logit_2, ret_norm_g_2, w_out_2,
        w_router_2, b_router_2, w_gate_2, w_up_2, w_down_2,
    )


_drawn_inputs = setup_inputs


def setup_inputs(seed=0):
    import zlib

    import numpy as np

    out = dict(_drawn_inputs(seed))
    spreads = {}
    factors = {'conv_b': 8.0,
     'lam_q1': 8.0,
     'lam_q2': 8.0,
     'anorm_g': 3.077,
     'post_ffn_g_2': 4.016,
     'conv_b_2': 3.101,
     'ret_norm_g_2': 2.87,
     'b_router_2': 8.0}
    for name, (base, spread) in spreads.items():
        noise = np.random.default_rng([zlib.crc32(name.encode()), seed]).standard_normal(out[name].shape)
        drawn = base * np.exp(spread * noise) if base else spread * noise
        out[name] = __import__('jax').numpy.asarray(drawn.astype(out[name].dtype))
    for name, factor in factors.items():
        out[name] = (out[name] * factor).astype(out[name].dtype)
    return out
```

```python
from contextlib import ExitStack
import math

import numpy as np
import concourse.bass as bass
from concourse import mybir

F32 = mybir.dt.float32
ALU = mybir.AluOpType
ACT = mybir.ActivationFunctionType
AX = mybir.AxisListType.X

P = 128
T = 256
NT = T // P
D = 1024
KD = D // P
W = 512
MH, MDV, MDK = 4, 512, 256
AH, ADH = 8, 64
RH, RD = 4, 128
NBUCKET, MAXDIST = 32, 128
NE, CAP, DE = 16, 32, 2048
EPS = 1e-6
NEG = -1e30
LAM_INIT = 0.8 - 0.6 * math.exp(0.0)
GRID_W = 64
SLOT = 2048
RING = 8

SPLITS = (1024, 1024, 2048, 2048, 2048, MH, MH, 1024, 1024, 1024, 1024, 1024, 1024)
QM, KM, VM, OM, ZM, IM, FM, QA, KA, VA, ZA, GM, GA = (sum(SPLITS[:i]) for i in range(13))
CB2, CC2, CX2, Q2, K2, V2, G2 = (W * i for i in range(7))

ROWS, COLS, CONST, EARLY, LATE = {}, {}, {}, {}, {}


def _lay(table, *items):
    at = 0
    for name, n in items:
        table[name] = (at, n)
        at += n
    table["all"] = (0, at)


_lay(ROWS, ("b_ada", 3 * D), ("b_ada_2", 6 * D), ("final_g", D), ("post_mix_g", D), ("pre_ffn_g", D),
     ("post_ffn_g", D), ("ret_norm_g", W), ("b_router", NE), ("decay", 2 * RH), ("lam", 4 * ADH))
_lay(COLS, ("c", KD), ("c_2", KD), ("c_ctx", KD), ("conv_w", 4 * 16), ("conv_b", 16), ("norm_g", KD),
     ("mnorm_g", 16), ("anorm_g", KD), ("pre_mix_g", KD), ("conv_w_2", 3 * 4), ("conv_b_2", 4), ("b_if", 2))
_lay(CONST, ("ident", P), ("iota", P), ("causal", P), ("sel32", 4 * P))
_lay(EARLY, ("selh", MH * P), ("onehot", 2 * T), ("future", 2 * T), ("mirror", P))
_lay(LATE, ("ahead", NT * T), ("behind", NT * T), ("before", NT * T), ("n1", T), ("n2", T),
     ("cosx", NT * 64), ("sinx", NT * 64), ("cosc", NT * 64), ("sinc", NT * 64), ("wn", 2 * NT))


def constants():
    one = np.zeros((P, CONST["all"][1]), np.float32)

    def put(a, table, name, v):
        s, n = table[name]
        a[:v.shape[0], s:s + n] = v.reshape(v.shape[0], n)

    p, j = np.arange(P)[:, None], np.arange(P)[None, :]
    put(one, CONST, "ident", (p == j).astype(np.float32))
    put(one, CONST, "iota", np.broadcast_to(j % CAP, (P, P)).astype(np.float32))
    put(one, CONST, "causal", np.where(p <= j, 0.0, NEG).astype(np.float32))
    sel = np.zeros((P, 4, P), np.float32)
    for n in range(4):
        sel[32 * n, n] = 1.0
    put(one, CONST, "sel32", sel)
    early = np.zeros((P, EARLY["all"][1]), np.float32)
    selh = np.zeros((MH, MH, P), np.float32)
    for h in range(MH):
        selh[h, h] = 1.0
    put(early, EARLY, "selh", selh)
    dist = T - 1 - np.arange(2 * T)
    exact = NBUCKET // 2
    nf = np.maximum(dist, 1).astype(np.float32)
    large = exact + (np.log(nf / np.float32(exact)) / np.float32(math.log(MAXDIST / exact))
                     * np.float32(NBUCKET - exact)).astype(np.int32)
    bucket = np.where(dist < exact, dist, np.minimum(large, NBUCKET - 1))
    put(early, EARLY, "onehot", ((bucket[None, :] == np.arange(NBUCKET)[:, None]) & (dist >= 0)).astype(np.float32))
    put(early, EARLY, "future", np.broadcast_to(np.where(dist >= 0, 0.0, NEG), (AH, 2 * T)).astype(np.float32))
    put(early, EARLY, "mirror", (p + j == P - 1).astype(np.float32))
    late = np.zeros((P, LATE["all"][1]), np.float32)
    m = (np.arange(NT)[None, :, None] * P + np.arange(P)[:, None, None])
    n = np.arange(T)[None, None, :]
    put(late, LATE, "ahead", np.maximum(n - m, 0).astype(np.float32))
    put(late, LATE, "behind", np.maximum(m - n, 0).astype(np.float32))
    put(late, LATE, "before", (n < m).astype(np.float32))
    put(late, LATE, "n1", np.broadcast_to(np.arange(T) + 1.0, (P, T)).astype(np.float32))
    put(late, LATE, "n2", np.broadcast_to(T - np.arange(T), (P, T)).astype(np.float32))
    half = RD // 2
    inv = (np.float32(1.0) / (np.float32(10000.0) ** (np.arange(half, dtype=np.float32) / np.float32(half)))).astype(np.float32)
    tok = (np.arange(NT)[None, :, None] * P + np.arange(P)[:, None, None]).astype(np.float32)
    for base, c, s in ((T, "cosx", "sinx"), (0, "cosc", "sinc")):
        ang = ((tok + np.float32(base)) * inv[None, None, :]).astype(np.float32)
        put(late, LATE, c, np.cos(ang.astype(np.float64)).astype(np.float32))
        put(late, LATE, s, np.sin(ang.astype(np.float64)).astype(np.float32))
    put(late, LATE, "wn", np.concatenate([T - 1 - tok[:, :, 0], tok[:, :, 0]], axis=1))
    return {"const": one, "early": early, "late": late}


class Queue:

    def __init__(self, sem, chained):
        self.sem, self.chained = sem, chained
        self.items, self.count, self.seen = [], 0, {}

    def wait(self, *marks):
        for mark in marks:
            if mark is None:
                continue
            sem, value = mark
            if self.seen.get(sem.name, 0) < value:
                self.seen[sem.name] = value
                self.items.append(lambda e, s=sem, v=value: e.wait_ge(s, v))

    def do(self, issue, after=(), signal=True):
        self.wait(*after)
        if self.chained and self.count:
            self.wait((self.sem, self.count))
        if not signal:
            self.items.append(issue)
            return None
        self.count += 1
        self.items.append(lambda e: issue(e).then_inc(self.sem, 1))
        return (self.sem, self.count)


def build(nc, dram, out, tap=None):
    ctx = ExitStack()
    with ctx:
        def sem(name):
            return ctx.enter_context(nc.semaphore(name))

        ring = ctx.enter_context(nc.sbuf_tensor("ring", [P, RING, SLOT], F32))
        KB = 256
        arena = ctx.enter_context(nc.sbuf_tensor("arena", [P, 136 * KB], F32))
        keep = ctx.enter_context(nc.sbuf_tensor("keep", [P, 1990], F32))
        ps = ctx.enter_context(nc.psum_tensor("ps", [P, 8, W], F32))

        def at(kb, *shape):
            n = int(np.prod(shape))
            v = arena[:, int(kb * KB):int(kb * KB) + n]
            if len(shape) == 2:
                return v.rearrange("p (a b) -> p a b", a=shape[0])
            if len(shape) == 3:
                return v.rearrange("p (a b c) -> p a b c", a=shape[0], b=shape[1])
            return v

        used = [0]

        def small(*shape):
            n = int(np.prod(shape))
            v = keep[:, used[0]:used[0] + n]
            used[0] += n
            assert used[0] <= 1990
            if len(shape) == 2:
                return v.rearrange("p (a b) -> p a b", a=shape[0])
            if len(shape) == 3:
                return v.rearrange("p (a b c) -> p a b c", a=shape[0], b=shape[1])
            return v

        const, cols = small(CONST["all"][1]), small(COLS["all"][1])
        wr = small(KD, NE)
        early, late = at(118, EARLY["all"][1]), at(62, LATE["all"][1])

        def part(v, table, name, rows=P):
            s, n = table[name]
            return v[0:rows, s:s + n]

        ident, iota = part(const, CONST, "ident"), part(const, CONST, "iota")
        causal = part(const, CONST, "causal")
        sel32 = part(const, CONST, "sel32").rearrange("p (n m) -> p n m", n=4)

        PE, V, A, G, SP = (Queue(sem(n), c) for n, c in
                           (("pe", False), ("dve", True), ("act", True), ("pool", True), ("sp", False)))

        def mm(out_, lhsT, rhs, start, stop, after=(), signal=False):
            return PE.do(lambda e: e.matmul(out_, lhsT, rhs, start=start, stop=stop, skip_group_check=True),
                         after, signal)

        def flip(out_, in_, after=(), signal=False):
            k = in_.shape[0]
            return PE.do(lambda e: e.transpose(out_, in_, ident[0:k, 0:k]), after, signal)

        def tt(o, a, b, op, after=()):
            return V.do(lambda e: e.tensor_tensor(o, a, b, op), after)

        def ts(o, a, s1, s2, op0, op1=None, after=()):
            if op1 is None:
                return V.do(lambda e: e.tensor_scalar(o, a, s1, None, op0), after)
            return V.do(lambda e: e.tensor_scalar(o, a, s1, s2, op0, op1), after)

        def stt(o, a, s, b, op0, op1, after=()):
            return V.do(lambda e: e.scalar_tensor_tensor(out=o, in0=a, scalar=s, in1=b, op0=op0, op1=op1), after)

        def recip(o, a, after=()):
            return V.do(lambda e: e.reciprocal(o, a), after)

        def vcopy(o, a, after=()):
            return V.do(lambda e: e.tensor_copy(o, a), after)

        def reduce(o, a, op, after=()):
            return V.do(lambda e: e.tensor_reduce(o, a, AX, op), after)

        def act(o, a, func, scale=1.0, bias=0.0, accum=None, after=()):
            if accum is None:
                return A.do(lambda e: e.activation(o, a, func, bias=bias, scale=scale), after)
            return A.do(lambda e: e.activation(o, a, func, bias=bias, scale=scale, accum_out=accum), after)

        def acopy(o, a, after=()):
            return act(o, a, ACT.Copy, after=after)

        def now(q):
            return (q.sem, q.count)

        loads = [0]

        def load(dst, src, after=(), queue=None):
            s = sem(f"load{loads[0]}")
            loads[0] += 1
            q = queue or G
            q.wait(*after)
            q.items.append(lambda e: e.dma_start(dst, src).then_inc(s, 16))
            return (s, 16)

        landed = [sem(f"landed{i}") for i in range(RING)]
        chunks, freed = [0], [None] * RING

        def take(src, shape):
            s = chunks[0] % RING
            chunks[0] += 1
            dst = ring[:, s, 0:int(np.prod(shape))]
            if len(shape) == 2:
                dst = dst.rearrange("p (a b) -> p a b", a=shape[0])
            SP.wait(freed[s])
            SP.items.append(lambda e: e.dma_start(dst, src).then_inc(landed[s], 16))
            return dst, (landed[s], 16 * ((chunks[0] - 1) // RING + 1)), s

        bank_free = [None] * 8

        rows = dram["rows"]

        def row(name, s=0, n=None):
            a, m = ROWS[name]
            return rows[a + s:a + s + (m if n is None else n)]

        X = at(0, NT, D)
        x_in = load(X, dram["x"].rearrange("(t p) d -> p t d", p=P), queue=A)
        cols_in = load(cols, dram["cols"], queue=A)
        const_in = load(const, dram["const"], queue=A)
        early_in = load(early, dram["early"])
        table = small(AH)
        table_in = load(table[0:NBUCKET, :], dram["rel_bias"])
        wif = at(126, KD, 2 * MH)
        wif_in = load(wif, dram["w_in"][:, IM:IM + 2 * MH].rearrange("(k p) n -> p k n", p=P))
        lam4 = at(127, 4 * ADH)
        lam_in = load(lam4, row("lam").partition_broadcast(P))
        wr_in = load(wr, dram["w_router"].rearrange("(k p) n -> p k n", p=P))
        brt = small(NE)
        brt_in = load(brt, row("b_router").partition_broadcast(P))
        lg = small(2 * RH)
        lg_in = load(lg, row("decay").partition_broadcast(P))
        gate_pow = small(16)
        pow_in = G.do(lambda e: e.memset(gate_pow, -0.5))
        ones = small(2)
        ones_in = G.do(lambda e: e.memset(ones, 1.0))

        TA = at(128, 2, W)

        def sigmoid_into(o, pre, after=()):
            e = act(o, pre, ACT.Exp, scale=-1.0, after=(*after, now(V)))
            ts(o, o, 1.0, None, ALU.add, after=(e,))
            return recip(o, o)

        def log1p_exp_neg_abs(o, x, t1, t2):
            m = stt(t1, x, -1.0, x, ALU.mult, ALU.max)
            m = act(t1, t1, ACT.Exp, scale=-1.0, after=(m,))
            ts(t2, t1, 2.0, None, ALU.add, after=(m,))
            recip(t2, t2)
            tt(t1, t1, t2, ALU.mult)
            tt(t2, t1, t1, ALU.mult)
            ts(o, t2, 1.0 / 15, None, ALU.mult)
            for n in (13, 11, 9, 7, 5, 3):
                stt(o, o, 1.0 / n, t2, ALU.add, ALU.mult)
            stt(o, o, 1.0, t1, ALU.add, ALU.mult)
            return ts(o, o, 2.0, None, ALU.mult)

        def log_sigmoid(o, x, t1, t2):
            log1p_exp_neg_abs(o, x, t1, t2)
            return stt(o, x, 0.0, o, ALU.min, ALU.subtract)

        ssq = small(16)

        def rstd(n, width, after=()):
            m = ts(ssq[:, 0:n], ssq[:, 0:n], 1.0 / width, EPS, ALU.mult, ALU.add, after=after)
            return G.do(lambda e: e.tensor_tensor(ssq[:, 0:n], ssq[:, 0:n], gate_pow[:, 0:n], ALU.pow),
                        (m, pow_in))

        def row_rms(o, x, junk, after=()):
            A.wait(now(V), now(G))
            for t in range(NT):
                m = act(junk[:, t, :], x[:, t, :], ACT.Square, accum=ssq[:, t:t + 1], after=after)
            r = rstd(NT, D, after=(m,))
            for t in range(NT):
                m = ts(o[:, t, :], x[:, t, :], ssq[:, t:t + 1], None, ALU.mult, after=(r,))
            return m

        def flip_tokens(dst, src, ntile, ready, evac):
            for k in range(0, ntile, 2):
                b = 6 + (k // 2) % 2
                PE.wait(bank_free[b])
                for i in range(2):
                    for t in range(NT):
                        m = flip(ps[:, b, i * T + t * P:i * T + (t + 1) * P], src[:, t, (k + i) * P:(k + i + 1) * P],
                                 after=(ready, const_in), signal=(i == 1 and t == NT - 1))
                for i in range(2):
                    bank_free[b] = evac(k + i, ps[:, b, i * T:(i + 1) * T], m)
            return bank_free[b]

        cst = small(3 * KD)
        call = cols[:, COLS["c"][0]:COLS["c"][0] + 3 * KD]
        sg = sigmoid_into(cst, call, after=(cols_in,))
        m = tt(cst, cst, call, ALU.mult)
        crep = at(135, KD, 32)
        crep2 = small(KD, 32)
        m = vcopy(crep, cst[:, 0:KD].unsqueeze(2).broadcast_to([P, KD, 32]))
        vcopy(crep2[:, :, 0:16], cst[:, KD:2 * KD].unsqueeze(2).broadcast_to([P, KD, 16]))
        crep_ok = vcopy(crep2[:, :, 16:32], cst[:, 2 * KD:3 * KD].unsqueeze(2).broadcast_to([P, KD, 16]))

        def ada(w, c0, ngroup, rep, bias, bank, dst, dst_free=None):
            rows_per = SLOT // (ngroup * W)
            bt = []
            for n in range(ngroup):
                bt.append(load(dst[32 * n:32 * n + 32, :],
                               row(bias, c0 + n * W, W).partition_broadcast(32), after=(dst_free,)))
            PE.wait(bank_free[bank], crep_ok)
            for q in range(KD // rows_per):
                src = w[q * rows_per * P:(q + 1) * rows_per * P, c0:c0 + ngroup * W]
                slot, got, s = take(src.rearrange("(k p) n -> p k n", p=P), (rows_per, ngroup * W))
                for kk in range(rows_per):
                    k = q * rows_per + kk
                    for n in range(ngroup):
                        m = mm(ps[32 * n:32 * n + 32, bank, :], rep[:, k, :], slot[:, kk, n * W:(n + 1) * W],
                               k == 0, k == KD - 1, after=(got,), signal=(n == ngroup - 1 and kk == rows_per - 1))
                freed[s] = m
            n = 32 * ngroup
            bank_free[bank] = tt(dst[0:n, :], ps[0:n, bank, :], dst[0:n, :], ALU.add, after=(m, *bt))
            return bank_free[bank]

        def ada_columns(rowsv, ready, pick, dst_sh, dst_g, g):
            PE.wait(bank_free[7])
            for b in range(4):
                m = flip(ps[:, 7, b * P:(b + 1) * P], rowsv[:, b * P:(b + 1) * P], after=(ready, const_in), signal=True)
            v = ps[:, 7, :].rearrange("p (b n j) -> p n b j", b=4, n=4)
            vcopy(dst_sh.rearrange("p (n b) -> p n b", n=2), v[:, 0:2, :, pick], after=(m,))
            bank_free[7] = m = stt(dst_g.rearrange("p (n b) -> p n b", n=2), v[:, 2:4, :, pick], 1.0,
                                   g.rearrange("p (n b) -> p n b", n=2), ALU.add, ALU.mult)
            return m

        modA = at(114, W)
        mA = ada(dram["w_ada"], 0, 4, crep, "b_ada", 0, modA)
        sh1, gs1 = small(KD), small(KD)
        mod1 = ada_columns(modA, mA, 0, sh1, gs1, part(cols, COLS, "norm_g"))

        XN, HT = at(16, NT, D), at(8, KD, T)
        xn = row_rms(XN, X, at(32, NT, D), after=(x_in,))

        def modulate(dst, sh, gs, ready):
            def evac(k, view, m):
                return act(dst[:, k, :], view, ACT.Identity, scale=gs[:, k:k + 1], bias=sh[:, k:k + 1],
                           after=(m, ready))
            return evac

        h_ok = flip_tokens(HT, XN, KD, xn, modulate(HT, sh1, gs1, mod1))

        turn = [0]

        def natural(lhs, ktiles, w, c0, ready, evac):
            pair = (0, 1) if turn[0] % 2 == 0 else (2, 3)
            turn[0] += 1
            PE.wait(ready, bank_free[pair[0]], bank_free[pair[1]])
            for q in range(ktiles // 4):
                src = w[q * 4 * P:(q + 1) * 4 * P, c0:c0 + W]
                slot, got, s = take(src.rearrange("(k p) n -> p k n", p=P), (4, W))
                for t in range(NT):
                    for kk in range(4):
                        k = 4 * q + kk
                        m = mm(ps[:, pair[t], :], lhs(k, t), slot[:, kk, :], k == 0, k == ktiles - 1,
                               after=(got,), signal=(kk == 3))
                    if q == ktiles // 4 - 1:
                        bank_free[pair[t]] = evac(t, ps[:, pair[t], :], m)
                freed[s] = m

        def transposed(xT, w, c0, ready, evac):
            pair = (0, 1) if turn[0] % 2 == 0 else (2, 3)
            turn[0] += 1
            PE.wait(ready)
            got = []
            for q in range(2):
                src = w[q * 4 * P:(q + 1) * 4 * P, c0:c0 + W]
                got.append(take(src.rearrange("(k p) n -> p k n", p=P), (4, W)))
            for i in range(4):
                b = pair[i // 2]
                if i % 2 == 0:
                    PE.wait(bank_free[b])
                view = ps[:, b, (i % 2) * T:(i % 2 + 1) * T]
                for k in range(KD):
                    slot, ok, s = got[k // 4]
                    m = mm(view, slot[:, k % 4, i * P:(i + 1) * P], xT[:, k, :], k == 0, k == KD - 1,
                           after=(ok,), signal=(k == KD - 1 or (i == 3 and k == 3)))
                    if i == 3 and k % 4 == 3:
                        freed[s] = m
                if i % 2 == 1:
                    for j in (i - 1, i):
                        bank_free[b] = evac(j, ps[:, b, (j % 2) * T:(j % 2 + 1) * T], m)

        hT = lambda k, t: HT[:, k, t * P:(t + 1) * P]

        gi, gf, gF, gt1, gt2 = (at(128 + i, T)[0:MH, :] for i in range(5))
        b_if = part(cols, COLS, "b_if", MH)
        for j in range(2):
            for k in range(KD):
                m = mm(ps[0:MH, 6, j * T:(j + 1) * T], wif[:, k, j * MH:(j + 1) * MH], HT[:, k, :], k == 0, k == KD - 1,
                       after=(h_ok, wif_in, bank_free[6]), signal=(k == KD - 1))
        ts(gi, ps[0:MH, 6, 0:T], b_if[:, 0:1], None, ALU.add, after=(m,))
        bank_free[6] = ts(gf, ps[0:MH, 6, T:2 * T], b_if[:, 1:2], None, ALU.add)
        log_sigmoid(gF, gf, gt1, gt2)
        V.do(lambda e: e.memset(gt1, 0.0))
        V.do(lambda e: e.tensor_tensor_scan(gf, gF, gt1, 0.0, ALU.add, ALU.add))
        tt(gi, gi, gf, ALU.subtract)
        V.do(lambda e: e.tensor_tensor_scan(gF, gi, gt1, 0.0, ALU.max, ALU.max))
        m = tt(gf, gf, gF, ALU.add)
        em = act(gf, gf, ACT.Exp, scale=-1.0, after=(m,))
        negM = ts(gF, gF, -1.0, None, ALU.mult)
        ccol, emcol = small(NT, MH), small(NT, MH)
        PE.wait(bank_free[7])
        for t in range(NT):
            flip(ps[:, 7, t * MH:(t + 1) * MH], gi[:, t * P:(t + 1) * P], after=(negM, em, early_in), signal=True)
            m = flip(ps[:, 7, 8 + t * MH:8 + (t + 1) * MH], gf[:, t * P:(t + 1) * P], signal=True)
        vcopy(ccol, ps[:, 7, 0:8].rearrange("p (t h) -> p t h", t=NT), after=(m,))
        bank_free[7] = cols_ok = vcopy(emcol, ps[:, 7, 8:16].rearrange("p (t h) -> p t h", t=NT))
        ET = at(48, MH, 3 * P)
        selh = part(early, EARLY, "selh", MH).rearrange("p (h m) -> p h m", h=MH)
        et_ok = None
        for h in range(MH):
            if h % 2 == 0:
                PE.wait(bank_free[6])
                for j in range(2):
                    m = mm(ps[:, 6, j * T:(j + 1) * T], selh[:, h + j, :], gF, True, True, signal=True)
            nm = ps[:, 6, (h % 2) * T:(h % 2 + 1) * T]
            tt(ET[:, h, 0:P], nm[:, 0:P], causal, ALU.add, after=(m,))
            vcopy(ET[:, h, P:2 * P], nm[:, P:2 * P])
            bank_free[6] = f = tt(ET[:, h, 2 * P:3 * P], nm[:, P:2 * P], causal, ALU.add)
            act(ET[:, h, 0:2 * P], ET[:, h, 0:2 * P], ACT.Exp, bias=ccol[:, 0, h:h + 1], after=(f,))
            et_ok = act(ET[:, h, 2 * P:3 * P], ET[:, h, 2 * P:3 * P], ACT.Exp, bias=ccol[:, 1, h:h + 1])

        toep = dram["toeplitz"]
        brow = at(133, 2 * T)[0:AH, :]
        m = mm(ps[0:AH, 6, :], table[0:NBUCKET, :], part(early, EARLY, "onehot", NBUCKET), True, True,
               after=(bank_free[6], table_in, early_in), signal=True)
        bank_free[6] = m = tt(brow, ps[0:AH, 6, :], part(early, EARLY, "future", AH), ALU.add, after=(m,))
        m = load(toep.rearrange("(h j) -> h j", h=AH), brow, after=(m,))
        BREV, BIAS = at(94, AH, T), at(54, AH, T)
        brev_in = load(BREV, bass.AP(toep.tensor, 0, [[1, P], [2 * T, AH], [1, T]]), after=(m,))

        def bias_turn():
            for j in range(4):
                b = 4 + j % 2
                m = mm(ps[:, b, :], part(early, EARLY, "mirror"), BREV[:, 2 * j:2 * j + 2, :].rearrange("p a b -> p (a b)"),
                       True, True, after=(brev_in, bank_free[b]), signal=True)
                bank_free[b] = acopy(BIAS[:, 2 * j:2 * j + 2, :].rearrange("p a b -> p (a b)"), ps[:, b, :], after=(m,))
            return bank_free[b]

        lamv = small(2)
        l4 = lam4.rearrange("p (a b) -> p a b", a=4)
        tt(l4[:, 0:4:2, :], l4[:, 0:4:2, :], l4[:, 1:4:2, :], ALU.mult, after=(lam_in,))
        m = reduce(lamv, l4[:, 0:4:2, :], ALU.add)
        m = act(lamv, lamv, ACT.Exp, after=(m,))
        tt(lamv[:, 0:1], lamv[:, 1:2], lamv[:, 0:1], ALU.subtract, after=(m,))
        neglam = lamv[:, 0:1]
        ts(neglam, neglam, LAM_INIT, None, ALU.subtract)

        QT, KT = at(32, KD, T), at(40, KD, T)
        cw = part(cols, COLS, "conv_w").rearrange("p (j c) -> p j c", j=4)
        cb = part(cols, COLS, "conv_b")
        conv_ok = {}

        def conv_evac(base, dst):
            def evac(i, view, m):
                c = base + i
                o = dst[:, c % KD, :]
                f = ts(o, view, cw[:, 3, c:c + 1], cb[:, c:c + 1], ALU.mult, ALU.add, after=(m,))
                for back in (1, 2, 3):
                    f = stt(o[:, back:T], view[:, 0:T - back], cw[:, 3 - back, c:c + 1], o[:, back:T],
                            ALU.mult, ALU.add)
                if i % 2 == 1:
                    two = dst[:, c % KD - 1:c % KD + 1, :]
                    t = TA[:, (c // 2) % 2, :].rearrange("p (a b) -> p a b", a=2)
                    sigmoid_into(t, two)
                    conv_ok[dst is KT] = tt(two, two, t, ALU.mult)
                return f
            return evac

        for n in range(4):
            transposed(HT, dram["w_in"], QM + n * W, h_ok, conv_evac(4 * n, QT if n < 2 else KT))
        qk_ok = now(V)

        HM = at(16, NT, 2 * D)
        v_ok = {}

        def v_evac(n):
            def evac(t, view, m):
                v_ok[n] = acopy(HM[:, t, n * W:(n + 1) * W], view, after=(m,))
                return v_ok[n]
            return evac

        for n in range(4):
            natural(hT, KD, dram["w_in"], VM + n * W, h_ok, v_evac(n))

        PT = [at(114 + 1.5 * i, 3 * P) for i in range(2)]
        den = small(2, NT)
        head_ok = {}

        def mlstm_scores(h):
            for k in range(2):
                m = mm(ps[:, 4, 0:T], KT[:, 2 * h + k, 0:P], QT[:, 2 * h + k, :], k == 0, k == 1,
                       after=(qk_ok, bank_free[4]))
            for k in range(2):
                m = mm(ps[:, 4, T:T + P], KT[:, 2 * h + k, P:T], QT[:, 2 * h + k, P:T], k == 0, k == 1,
                       signal=(k == 1))
            bank_free[4] = stt(PT[h % 2], ps[:, 4, 0:3 * P], MDK ** -0.5, ET[:, h, :], ALU.mult, ALU.mult,
                               after=(m, et_ok))
            return bank_free[4]

        def mlstm_values(h, ready):
            p = PT[h % 2]
            PE.wait(ready, ones_in, bank_free[5], bank_free[6], bank_free[7], v_ok[h])
            v = [HM[:, t, h * W:(h + 1) * W] for t in range(NT)]
            mm(ps[:, 5, :], p[:, 0:P], v[0], True, True)
            mm(ps[:, 6, :], p[:, P:2 * P], v[0], True, False)
            mm(ps[:, 6, :], p[:, 2 * P:3 * P], v[1], False, True)
            mm(ps[:, 7, 0:1], p[:, 0:P], ones[:, 0:1], True, True)
            mm(ps[:, 7, 1:2], p[:, P:2 * P], ones[:, 0:1], True, False)
            m = mm(ps[:, 7, 1:2], p[:, 2 * P:3 * P], ones[:, 0:1], False, True, signal=True)
            d, e = den[:, 0, :], den[:, 1, :]
            ts(d, ps[:, 7, 0:NT], -1.0, None, ALU.mult, after=(m,))
            tt(d, d, ps[:, 7, 0:NT], ALU.max)
            tt(d, d, emcol[:, :, h], ALU.max)
            bank_free[7] = recip(e, d)
            for t in range(NT):
                m = ts(v[t], ps[:, 5 + t, :], e[:, t:t + 1], None, ALU.mult)
                bank_free[5 + t] = m
            head_ok[h] = m

        QMASK, KAT, VAN = at(62, AH, NT, T), at(78, KD, T), at(86, NT, D)
        zq = G.do(lambda e: e.memset(QMASK, 0.0))
        aq_ok, ak_ok, av_ok = {}, {}, {}

        def qa_evac(n):
            def evac(i, view, m):
                h = 4 * n + i
                act(QMASK[0:ADH, h, 0, :], view[0:ADH, :], ACT.Copy, scale=ADH ** -0.5, after=(m, zq))
                aq_ok[h] = act(QMASK[ADH:P, h, 1, :], view[ADH:P, :], ACT.Copy, scale=ADH ** -0.5)
                return aq_ok[h]
            return evac

        def ka_evac(n):
            def evac(i, view, m):
                ak_ok[4 * n + i] = acopy(KAT[:, 4 * n + i, :], view, after=(m,))
                return ak_ok[4 * n + i]
            return evac

        def va_evac(n):
            def evac(t, view, m):
                av_ok[n] = acopy(VAN[:, t, n * W:(n + 1) * W], view, after=(m,))
                return av_ok[n]
            return evac

        r = mlstm_scores(0)
        transposed(HT, dram["w_in"], QA, h_ok, qa_evac(0))
        mlstm_values(0, r)
        r = mlstm_scores(1)
        transposed(HT, dram["w_in"], QA + W, h_ok, qa_evac(1))
        mlstm_values(1, r)
        r = mlstm_scores(2)
        transposed(HT, dram["w_in"], KA, h_ok, ka_evac(0))
        mlstm_values(2, r)
        r = mlstm_scores(3)
        transposed(HT, dram["w_in"], KA + W, h_ok, ka_evac(1))
        mlstm_values(3, r)
        mlstm_done = now(V)
        for n in range(2):
            natural(hT, KD, dram["w_in"], VA + n * W, h_ok, va_evac(n))

        bias_ok = bias_turn()
        HA = at(94, NT, D)
        LG = [at(102 + 3 * i, 2, 3 * P) for i in range(2)]
        AM = [at(108 + 1.5 * i, 3 * P) for i in range(2)]
        AT = [at(111 + 1.5 * i, 3 * P) for i in range(2)]
        mx, sm = small(2, NT), small(2, NT)
        at_free = [None, None]

        def attn_scores(h):
            for m_ in range(2):
                PE.wait(bank_free[4 + m_], aq_ok[h], ak_ok[h])
                q = QMASK[:, h, m_, :]
                mm(ps[:, 4 + m_, 0:T], q[:, P:T], KAT[:, h, :], True, True)
                m = mm(ps[:, 4 + m_, T:T + P], q[:, 0:P], KAT[:, h, 0:P], True, True, signal=True)
            L = LG[h % 2]
            V.wait(now(A))
            tt(L[:, :, 0:T], ps[:, 4:6, 0:T], BIAS[:, h, :].unsqueeze(1).broadcast_to([P, 2, T]), ALU.add,
               after=(m, bias_ok))
            m = tt(L[:, :, T:T + P], ps[:, 4:6, T:T + P], BIAS[:, h, P:T].unsqueeze(1).broadcast_to([P, 2, P]), ALU.add)
            bank_free[4] = bank_free[5] = m
            reduce(mx[:, :, 0], L[:, :, 0:T], ALU.max)
            reduce(mx[:, :, 1], L[:, :, T:T + P], ALU.max)
            m = ts(mx, mx, -1.0, None, ALU.mult)
            for m_ in range(2):
                act(L[:, m_, 0:T], L[:, m_, 0:T], ACT.Exp, bias=mx[:, m_, 0:1], accum=sm[:, m_, 0:1], after=(m,))
                a = act(L[:, m_, T:T + P], L[:, m_, T:T + P], ACT.Exp, bias=mx[:, m_, 1:2], accum=sm[:, m_, 1:2])
            recip(sm, sm, after=(a,))
            ts(sm[:, 1, :], sm[:, 1, :], neglam, None, ALU.mult)
            V.wait(at_free[h % 2])
            am = AM[h % 2]
            for q, (lo, hi) in enumerate(((0, T), (T, T + P))):
                ts(L[:, 1, lo:hi], L[:, 1, lo:hi], sm[:, 1, q:q + 1], None, ALU.mult)
                m = stt(am[:, lo:hi], L[:, 0, lo:hi], sm[:, 0, q:q + 1], L[:, 1, lo:hi], ALU.mult, ALU.add)
            return m

        def attn_values(h, ready):
            am, aT = AM[h % 2], AT[h % 2]
            PE.wait(ready, bank_free[6])
            for j in range(3):
                m = flip(ps[:, 6, j * P:(j + 1) * P], am[:, j * P:(j + 1) * P], signal=True)
            bank_free[6] = at_free[h % 2] = c = acopy(aT, ps[:, 6, 0:3 * P], after=(m,))
            v = [VAN[:, t, h * P:(h + 1) * P] for t in range(NT)]
            PE.wait(c, bank_free[7], av_ok[h // 4])
            mm(ps[:, 7, 0:P], aT[:, 2 * P:3 * P], v[0], True, True)
            mm(ps[:, 7, P:T], aT[:, 0:P], v[0], True, False)
            m = mm(ps[:, 7, P:T], aT[:, P:2 * P], v[1], False, True, signal=True)
            bank_free[7] = acopy(HA[:, :, h * P:(h + 1) * P], ps[:, 7, 0:T].rearrange("p (t e) -> p t e", t=NT),
                                 after=(m,))
            return bank_free[7]

        def o_evac(n):
            def evac(t, view, m):
                e = act(TA[:, t, :], view, ACT.Exp, scale=-1.0, after=(m, now(V)))
                ts(TA[:, t, :], TA[:, t, :], 1.0, None, ALU.add, after=(e,))
                recip(TA[:, t, :], TA[:, t, :])
                hm = HM[:, t, n * W:(n + 1) * W]
                v = tt(hm, hm, TA[:, t, :], ALU.mult)
                act(TA[:, t, :], hm, ACT.Square, accum=ssq[:, NT * n + t:NT * n + t + 1], after=(v,))
                return e
            return evac

        def z_evac(n):
            def evac(t, view, m):
                e = act(TA[:, t, :], view, ACT.Exp, scale=-1.0, after=(m, now(V)))
                ts(TA[:, t, :], TA[:, t, :], 1.0, None, ALU.add, after=(e,))
                recip(TA[:, t, :], TA[:, t, :])
                f = tt(TA[:, t, :], TA[:, t, :], view, ALU.mult)
                hm = HM[:, t, n * W:(n + 1) * W]
                stt(hm, hm, ssq[:, NT * n + t:NT * n + t + 1], TA[:, t, :], ALU.mult, ALU.mult)
                return f
            return evac

        steps = [lambda n=n: natural(hT, KD, dram["w_in"], OM + n * W, h_ok, o_evac(n)) for n in range(4)]
        steps.append(lambda: rstd(NT * MH, MDV, after=(now(A),)))
        steps += [lambda n=n: (V.wait(now(G)), natural(hT, KD, dram["w_in"], ZM + n * W, h_ok, z_evac(n)))
                  for n in range(4)]
        for h in range(AH):
            r = attn_scores(h)
            steps.pop(0)()
            if h == 4:
                steps.pop(0)()
            attn_done = attn_values(h, r)
        attn_pe = now(PE)

        sq = at(102, NT, D)
        assq = small(NT * AH)
        V.wait(attn_done, now(A))
        tt(sq, HA, HA, ALU.mult, after=(attn_pe,))
        m = reduce(assq, sq.rearrange("p t (h e) -> p (t h) e", h=AH), ALU.add)
        m = ts(assq, assq, 1.0 / (2 * ADH), EPS, ALU.mult, ALU.add)
        m = G.do(lambda e: e.tensor_tensor(assq, assq, gate_pow, ALU.pow), (m,))
        HA4 = HA.rearrange("p t (h e) -> p (t h) e", h=AH)
        tt(HA4, HA4, assq.unsqueeze(2).broadcast_to([P, NT * AH, 2 * ADH]), ALU.mult, after=(m,))

        def za_evac(n):
            def evac(t, view, m):
                e = act(TA[:, t, :], view, ACT.Exp, scale=-1.0, after=(m, now(V)))
                ts(TA[:, t, :], TA[:, t, :], 1.0, None, ALU.add, after=(e,))
                recip(TA[:, t, :], TA[:, t, :])
                f = tt(TA[:, t, :], TA[:, t, :], view, ALU.mult)
                ha = HA[:, t, n * W:(n + 1) * W]
                tt(ha, ha, TA[:, t, :], ALU.mult)
                return f
            return evac

        for n in range(2):
            natural(hT, KD, dram["w_in"], ZA + n * W, h_ok, za_evac(n))

        HMT = at(32, 2 * KD, T)
        mg = part(cols, COLS, "mnorm_g")

        def scaled(dst, g):
            def evac(k, view, m):
                return act(dst[:, k, :], view, ACT.Copy, scale=g[:, k:k + 1], after=(m,))
            return evac

        A.wait(attn_pe)
        hmt_ok = flip_tokens(HMT, HM, 2 * KD, now(V), scaled(HMT, mg))
        YM, YA = at(16, NT, D), at(24, NT, D)
        ag = small(KD)
        m = ts(ag, part(cols, COLS, "anorm_g"), 1.0 - LAM_INIT, None, ALU.mult)
        HAT = at(48, KD, T)
        A.wait(m)
        y_ready = {}

        def y_evac(dst, key, n):
            def evac(t, view, m):
                y_ready[key] = acopy(dst[:, t, n * W:(n + 1) * W], view, after=(m,))
                return y_ready[key]
            return evac

        for n in range(2):
            natural(lambda k, t: HMT[:, k, t * P:(t + 1) * P], 2 * KD, dram["w_proj_m"], n * W, hmt_ok,
                    y_evac(YM, "m", n))
        hat_ok = flip_tokens(HAT, HA, KD, now(V), scaled(HAT, ag))
        GATE, FG, G1, SH2, SC2, GG2 = (at(kb, D) for kb in (102, 106, 110, 114, 118, 122))
        modB = at(126, W)
        late_in = load(late, dram["late"], after=(attn_pe, now(A)))
        fg_in = load(FG, row("final_g").partition_broadcast(P), after=(now(V),))

        def spread(src, n, dst, half, ready):
            b = 4 + (n % 2)
            m = mm(ps[:, b, :], sel32[:, n, :], src, True, True, after=(ready, bank_free[b]), signal=True)
            bank_free[b] = acopy(dst[:, half * W:(half + 1) * W], ps[:, b, :], after=(m,))
            return bank_free[b]

        modF = at(128, W)
        m = V.do(lambda e: e.memset(modF, 0.0), (attn_pe,))
        mF = ada(dram["w_ada"], 2 * D, 2, crep, "b_ada", 6, modF, m)
        for i in range(2):
            gate_ok = spread(modF, i, GATE, i, mF)
        modC = at(130, W)
        sh2, gs2, shc, gsc = (small(KD) for _ in range(4))
        mC = ada(dram["w_ada_2"], 0, 4, crep2, "b_ada_2", 5, modC, now(PE))
        ada_columns(modC, mC, 0, sh2, gs2, part(cols, COLS, "pre_mix_g"))
        modc_ok = ada_columns(modC, mC, 16, shc, gsc, part(cols, COLS, "pre_mix_g"))
        mD = ada(dram["w_ada_2"], 2 * D, 4, crep2, "b_ada_2", 6, modB, now(PE))
        for n, (dst, half) in enumerate(((G1, 0), (G1, 1), (SH2, 0), (SH2, 1))):
            rows_ok = spread(modB, n, dst, half, mD)
        modE = at(132, W)
        mE = ada(dram["w_ada_2"], 4 * D, 4, crep2, "b_ada_2", 6, modE, now(PE))
        for n, (dst, half) in enumerate(((SC2, 0), (SC2, 1), (GG2, 0), (GG2, 1))):
            rows_ok = spread(modE, n, dst, half, mE)
        V.wait(rows_ok)
        A.wait(now(V), now(PE))
        for n in range(2):
            natural(lambda k, t: HAT[:, k, t * P:(t + 1) * P], KD, dram["w_proj_a"], n * W, hat_ok,
                    y_evac(YA, "a", n))

        def mix_evac(n, y, first):
            def evac(t, view, m):
                e = act(TA[:, t, :], view, ACT.Exp, scale=-1.0, after=(m, now(V)))
                ts(TA[:, t, :], TA[:, t, :], 1.0, None, ALU.add, after=(e, y_ready["m"], y_ready["a"]))
                recip(TA[:, t, :], TA[:, t, :])
                yy = y[:, t, n * W:(n + 1) * W]
                tt(yy, yy, TA[:, t, :], ALU.mult)
                if not first:
                    ym = YM[:, t, n * W:(n + 1) * W]
                    tt(ym, ym, yy, ALU.add)
                return e
            return evac

        for n in range(2):
            natural(hT, KD, dram["w_in"], GM + n * W, h_ok, mix_evac(n, YM, True))
        for n in range(2):
            natural(hT, KD, dram["w_in"], GA + n * W, h_ok, mix_evac(n, YA, False))
        YT = at(48, KD, T)
        yt_ok = flip_tokens(YT, YM, KD, now(V), lambda k, view, m: acopy(YT[:, k, :], view, after=(m,)))

        def residual_evac(n):
            def evac(t, view, m):
                f = tt(TA[:, t, :], view, GATE[:, n * W:(n + 1) * W], ALU.mult, after=(m, gate_ok))
                xx = X[:, t, n * W:(n + 1) * W]
                tt(xx, xx, TA[:, t, :], ALU.add)
                return f
            return evac

        for n in range(2):
            natural(lambda k, t: YT[:, k, t * P:(t + 1) * P], KD, dram["w_out"], n * W, yt_ok, residual_evac(n))
        m = row_rms(X, X, at(24, NT, D), after=(now(V),))
        for t in range(NT):
            x1 = tt(X[:, t, :], X[:, t, :], FG, ALU.mult, after=(fg_in,))
        if tap:
            tap_sem = load(dram["tap1"].rearrange("(t p) d -> p t d", p=P), X, after=(x1,))

        CX, CN, CT = at(32, NT, D), at(24, NT, D), at(40, KD, T)
        cx_in = load(CX, dram["ctx"].rearrange("(t p) d -> p t d", p=P), after=(now(PE), now(V), now(A)))
        ct_n = row_rms(CN, CX, CN, after=(cx_in,))
        ct_ok = flip_tokens(CT, CN, KD, ct_n, modulate(CT, shc, gsc, modc_ok))
        KC, VC = at(94, NT, W), at(98, NT, W)
        cT = lambda k, t: CT[:, k, t * P:(t + 1) * P]

        def plain(dst):
            def evac(t, view, m):
                return acopy(dst[:, t, :], view, after=(m,))
            return evac

        natural(cT, KD, dram["w_in_2"], K2, ct_ok, plain(KC))
        natural(cT, KD, dram["w_in_2"], V2, ct_ok, plain(VC))
        lgs, lt1, lt2 = small(2 * RH), small(2 * RH), small(2 * RH)
        V.wait(lg_in)
        lg_ok = log_sigmoid(lgs, lg, lt1, lt2)

        def rotary(x, c, s, scratch, after):
            x4 = x.rearrange("p t (h e) -> p t h e", h=RH)
            a, b = x4[:, :, :, 0:64], x4[:, :, :, 64:128]
            bc = [part(late, LATE, n_).rearrange("p (t e) -> p t e", t=NT).unsqueeze(2).broadcast_to([P, NT, RH, 64])
                  for n_ in (c, s)]
            u, v, w_, z = (scratch[:, i, :].rearrange("p (t h e) -> p t h e", t=NT, h=RH) for i in range(4))
            tt(u, a, bc[0], ALU.mult, after=after)
            tt(v, b, bc[1], ALU.mult)
            tt(w_, a, bc[1], ALU.mult)
            tt(z, b, bc[0], ALU.mult)
            tt(a, u, v, ALU.subtract)
            return tt(b, w_, z, ALU.add)

        RS = at(128, 4, W)
        rk = rotary(KC, "cosc", "sinc", RS, (now(A), late_in))
        wfb = small(2, NT, RH)
        wn = part(late, LATE, "wn").rearrange("p (a t) -> p a t", a=2)
        for d in range(2):
            for t in range(NT):
                m = ts(wfb[:, d, t, :], lgs[:, d * RH:(d + 1) * RH], wn[:, d, t:t + 1], None, ALU.mult)
        m = act(wfb, wfb, ACT.Exp, after=(m,))
        wfb = wfb
        m = ts(wfb, wfb, RD ** -0.5, None, ALU.mult, after=(m,))
        KF = [at(128 + 4 * d, NT, W) for d in range(2)]
        SF = at(56, 2, RH * RD)
        kc4 = KC.rearrange("p t (h e) -> p t h e", h=RH)
        for d in range(2):
            m = tt(KF[d].rearrange("p t (h e) -> p t h e", h=RH), kc4,
                   wfb[:, d, :, :].unsqueeze(3).broadcast_to([P, NT, RH, RD]), ALU.mult)
            PE.wait(bank_free[4 + d], m, now(A))
            for h in range(RH):
                for t in range(NT):
                    m = mm(ps[:, 4 + d, h * RD:(h + 1) * RD], KF[d][:, t, h * RD:(h + 1) * RD],
                           VC[:, t, h * RD:(h + 1) * RD], t == 0, t == NT - 1, signal=(t == NT - 1))
            state_ok = bank_free[4 + d] = acopy(SF[:, d, :], ps[:, 4 + d, :], after=(m,))
        WT = at(32, RH, NT * T)
        ahead, behind = part(late, LATE, "ahead"), part(late, LATE, "behind")
        XI = at(76, 2, RH, T)
        for h in range(RH):
            ts(WT[:, h, :], ahead, lgs[:, h:h + 1], None, ALU.mult, after=(now(PE), now(A)))
            m = stt(WT[:, h, :], behind, lgs[:, RH + h:RH + h + 1], WT[:, h, :], ALU.mult, ALU.add)
            act(WT[:, h, :], WT[:, h, :], ACT.Exp, after=(m,))
            act(XI[:, 0, h, :], part(late, LATE, "n1"), ACT.Exp, scale=lgs[:, h:h + 1])
            xi_ok = act(XI[:, 1, h, :], part(late, LATE, "n2"), ACT.Exp, scale=lgs[:, RH + h:RH + h + 1])

        X2N, HT2 = at(16, NT, D), at(8, KD, T)
        xn = row_rms(X2N, X, X2N, after=(x1, now(V)))
        h2_ok = flip_tokens(HT2, X2N, KD, xn, modulate(HT2, sh2, gs2, modc_ok))
        h2T = lambda k, t: HT2[:, k, t * P:(t + 1) * P]
        QX, KX, VX, GX = (at(kb, NT, W) for kb in (16, 20, 24, 28))
        natural(h2T, KD, dram["w_in_2"], Q2, h2_ok, plain(QX))
        q_ok = now(A)
        natural(h2T, KD, dram["w_in_2"], K2, h2_ok, plain(KX))
        k_ok = now(A)
        natural(h2T, KD, dram["w_in_2"], V2, h2_ok, plain(VX))
        vx_ok = now(A)
        rq = rotary(QX, "cosx", "sinx", RS, (q_ok,))
        rk = rotary(KX, "cosx", "sinx", RS, (k_ok,))
        QXT, KXT = at(94, RH, T), at(98, RH, T)
        flip_tokens(QXT, QX, RH, rq, lambda k, view, m: acopy(QXT[:, k, :], view, after=(m,)))
        qkx_ok = flip_tokens(KXT, KX, RH, rk,
                             lambda k, view, m: act(KXT[:, k, :], view, ACT.Copy, scale=RD ** -0.5, after=(m,)))

        def g_evac(t, view, m):
            e = act(GX[:, t, :], view, ACT.Exp, scale=-1.0, after=(m,))
            ts(GX[:, t, :], GX[:, t, :], 1.0, None, ALU.add, after=(e,))
            recip(GX[:, t, :], GX[:, t, :])
            return tt(GX[:, t, :], GX[:, t, :], view, ALU.mult)

        natural(h2T, KD, dram["w_in_2"], G2, h2_ok, g_evac)
        QS = at(102, 2, RH * T)
        for d in range(2):
            qs_ok = tt(QS[:, d, :].rearrange("p (h t) -> p h t", h=RH), QXT, XI[:, d, :, :], ALU.mult,
                       after=(qkx_ok, xi_ok, now(PE)))

        RP = [at(128 + 2 * i, NT, T) for i in range(2)]
        RY = at(132, NT, W)

        def ret_scores(h):
            b = 4 + h % 2
            PE.wait(bank_free[b], qkx_ok)
            for mt in range(NT):
                m = mm(ps[:, b, mt * T:(mt + 1) * T], KXT[:, h, mt * P:(mt + 1) * P], QXT[:, h, :], True, True,
                       signal=True)
            bank_free[b] = tt(RP[h % 2], ps[:, b, :].rearrange("p (a b) -> p a b", a=NT),
                              WT[:, h, :].rearrange("p (a b) -> p a b", a=NT), ALU.mult, after=(m, now(A)))
            return bank_free[b]

        def ret_values(h, ready):
            PE.wait(ready, qs_ok, state_ok, vx_ok)
            if h == 0:
                PE.wait(bank_free[6], bank_free[7])
            hs = slice(h * RD, (h + 1) * RD)
            for nt in range(NT):
                o = ps[:, 6 + nt, hs]
                ns = slice(nt * P, (nt + 1) * P)
                for mt in range(NT):
                    mm(o, RP[h % 2][:, mt, ns], VX[:, mt, hs], mt == 0, False)
                for d in range(2):
                    m = mm(o, QS[:, d, h * T + nt * P:h * T + (nt + 1) * P], SF[:, d, hs], False, d == 1,
                           signal=(d == 1))
            return m

        MIXT = at(48, KD, T)
        CVC, CVU = at(86, RH, T), at(40, RH, T)
        c_ok = {}

        def hold(dst, key):
            def evac(i, view, m):
                c_ok[key] = acopy(dst[:, i, :], view, after=(m,))
                return c_ok[key]
            return evac

        r0 = ret_scores(0)
        transposed(HT2, dram["w_in_2"], CC2, h2_ok, hold(CVC, "c"))
        ret_values(0, r0)
        r1 = ret_scores(1)
        A.wait(now(V))

        def u_evac(i, view, m):
            return tt(CVU[:, i, :], view, CVC[:, i, :], ALU.mult, after=(m, c_ok["c"]))

        transposed(HT2, dram["w_in_2"], CX2, h2_ok, u_evac)
        ret_values(1, r1)
        r2 = ret_scores(2)
        w2, b2 = part(cols, COLS, "conv_w_2").rearrange("p (j c) -> p j c", j=3), part(cols, COLS, "conv_b_2")
        for i in range(4):
            o = MIXT[:, i, :].rearrange("p (r w) -> p r w", w=GRID_W)
            u = CVU[:, i, :].rearrange("p (r w) -> p r w", w=GRID_W)
            ts(MIXT[:, i, :], CVU[:, i, :], w2[:, 1, i:i + 1], b2[:, i:i + 1], ALU.mult, ALU.add)
            stt(o[:, :, 1:], u[:, :, :-1], w2[:, 0, i:i + 1], o[:, :, 1:], ALU.mult, ALU.add)
            conv2 = stt(o[:, :, :-1], u[:, :, 1:], w2[:, 2, i:i + 1], o[:, :, :-1], ALU.mult, ALU.add)

        def b_evac(i, view, m):
            return tt(MIXT[:, i, :], MIXT[:, i, :], view, ALU.mult, after=(m,))

        transposed(HT2, dram["w_in_2"], CB2, h2_ok, b_evac)
        ret_values(2, r2)
        r3 = ret_scores(3)
        m = ret_values(3, r3)
        for t in range(NT):
            ry = bank_free[6 + t] = acopy(RY[:, t, :], ps[:, 6 + t, :], after=(m,))
        RY4 = RY.rearrange("p t (h e) -> p (t h) e", h=RH)
        gmean = small(NT * RH)
        reduce(gmean, RY4, ALU.add, after=(ry,))
        ts(gmean, gmean, 1.0 / RD, None, ALU.mult)
        tt(RY4, RY4, gmean.unsqueeze(2).broadcast_to([P, NT * RH, RD]), ALU.subtract)
        sq4 = at(128, NT * RH, RD)
        tt(sq4, RY4, RY4, ALU.mult, after=(now(PE),))
        m = reduce(ssq[:, 0:NT * RH], sq4, ALU.add)
        r = rstd(NT * RH, RD)
        tt(RY4, RY4, ssq[:, 0:NT * RH].unsqueeze(2).broadcast_to([P, NT * RH, RD]), ALU.mult, after=(r,))
        rg = at(126, W)
        rg_in = load(rg, row("ret_norm_g").partition_broadcast(P), after=(now(PE), now(A)))
        tt(RY, RY, rg.unsqueeze(1).broadcast_to([P, NT, W]), ALU.mult, after=(rg_in,))
        m = tt(RY, RY, GX, ALU.mult)
        mix_ok = flip_tokens(MIXT, RY, RH, m, lambda k, view, m: acopy(MIXT[:, RH + k, :], view, after=(m,)))
        PE.wait(now(V))

        M = at(16, NT, D)

        def m_evac(n):
            def evac(t, view, m):
                return acopy(M[:, t, n * W:(n + 1) * W], view, after=(m,))
            return evac

        for n in range(2):
            natural(lambda k, t: MIXT[:, k, t * P:(t + 1) * P], KD, dram["w_out_2"], n * W, mix_ok, m_evac(n))
        gst = at(128, D)
        pm_in = load(gst, row("post_mix_g").partition_broadcast(P), after=(now(V), now(PE)))
        tt(G1, G1, gst, ALU.mult, after=(pm_in,))
        pf_in = load(gst, row("pre_ffn_g").partition_broadcast(P), after=(now(V),))
        stt(SC2, SC2, 1.0, gst, ALU.add, ALU.mult, after=(pf_in,))
        po_in = load(gst, row("post_ffn_g").partition_broadcast(P), after=(now(V),))
        tt(GG2, GG2, gst, ALU.mult, after=(po_in,))
        row_rms(M, M, at(24, NT, D), after=(now(A), now(V)))
        for t in range(NT):
            tt(M[:, t, :], M[:, t, :], G1, ALU.mult)
            x2 = tt(X[:, t, :], X[:, t, :], M[:, t, :], ALU.add)
        if tap:
            load(dram["tap2"].rearrange("(t p) d -> p t d", p=P), X, after=(x2,))
        H2, H2T = at(24, NT, D), at(8, KD, T)
        row_rms(H2, X, H2, after=(x2,))
        for t in range(NT):
            tt(H2[:, t, :], H2[:, t, :], SC2, ALU.mult)
            hh = tt(H2[:, t, :], H2[:, t, :], SH2, ALU.add)
        h2t_ok = flip_tokens(H2T, H2, KD, hh, lambda k, view, m: acopy(H2T[:, k, :], view, after=(m,)))
        PE.wait(bank_free[0], wr_in, h2t_ok)
        for t in range(NT):
            for k in range(KD):
                m = mm(ps[:, 0, t * NE:(t + 1) * NE], H2T[:, k, t * P:(t + 1) * P], wr[:, k, :], k == 0, k == KD - 1,
                       signal=(k == KD - 1))
        aff, rank, eqs = small(NT, NE), small(NT, NE), small(NT, NE)
        rmax = small(NT)
        tt(aff, ps[:, 0, 0:NT * NE].rearrange("p (t e) -> p t e", t=NT), brt.unsqueeze(1).broadcast_to([P, NT, NE]),
           ALU.add, after=(m, brt_in))
        bank_free[0] = now(V)
        reduce(rmax, aff, ALU.max)
        m = tt(aff, aff, rmax.unsqueeze(2).broadcast_to([P, NT, NE]), ALU.subtract)
        m = act(aff, aff, ACT.Exp, after=(m,))
        reduce(rmax, aff, ALU.add, after=(m,))
        recip(rmax, rmax)
        m = tt(aff, aff, rmax.unsqueeze(2).broadcast_to([P, NT, NE]), ALU.mult)
        PE.wait(bank_free[1])
        for t in range(NT):
            m = flip(ps[0:NE, 1, t * P:(t + 1) * P], aff[:, t, :], after=(m,), signal=True)
        affT = at(126, T)[0:NE, :]
        bank_free[1] = m = acopy(affT, ps[0:NE, 1, 0:T], after=(m, now(V)))
        m = load(dram["affinity"].rearrange("(e t) -> e t", e=NE), affT, after=(m,))
        ROWB = at(32, NE, T)
        rowb = load(ROWB.rearrange("p e t -> p (e t)"), dram["affinity"].partition_broadcast(P),
                    after=(m, now(PE), now(V), now(A)))
        before = part(late, LATE, "before").rearrange("p (t s) -> p t s", t=NT)
        junk = at(132, T)
        for e_ in range(NE):
            for t in range(NT):
                V.do(lambda e, e_=e_, t=t: e.tensor_scalar(junk, ROWB[:, e_, :], aff[:, t, e_:e_ + 1], 0.0,
                                                           ALU.is_gt, ALU.add, accum_out=rank[:, t, e_:e_ + 1]),
                     (rowb,))
                V.do(lambda e, e_=e_, t=t: e.scalar_tensor_tensor(out=junk, in0=ROWB[:, e_, :],
                                                                  scalar=aff[:, t, e_:e_ + 1], in1=before[:, t, :],
                                                                  op0=ALU.is_equal, op1=ALU.mult,
                                                                  accum_out=eqs[:, t, e_:e_ + 1]))
        rank_ok = tt(rank, rank, eqs, ALU.add)

        ACC = at(16, NT, D)
        acc0 = V.do(lambda e: e.memset(ACC, 0.0), (now(A),))
        ONE = small(NT, CAP)
        Z = at(48, NT, P)
        GT = at(49, 2, T)
        XS, XT = at(51, T), at(52, 2, P)
        SG, HD, HTT, YS = at(53, W), at(55, W), at(57, 4, P), at(59, W)
        gz = V.do(lambda e: e.memset(GT, 0.0))
        landed_before = [chunks[0] // RING + (1 if s < chunks[0] % RING else 0) for s in range(RING)]
        first_slot = chunks[0] % RING
        NCH = 3 * KD
        wg, wu, wd = dram["w_gate"], dram["w_up"], dram["w_down"]
        p_use = sem("p_use")

        def chunk_src(e_, c):
            if c < 2 * KD:
                w_ = wg if c < KD else wu
                return w_[e_, (c % KD) * P:(c % KD + 1) * P, :]
            return wd[e_, (c - 2 * KD) * 2 * P:(c - 2 * KD + 1) * 2 * P, :].rearrange("(k p) n -> p k n", p=P)

        def chunk_slot(c):
            s = (first_slot + c) % RING
            return s, (ring[:, s, :] if c < 2 * KD else ring[:, s, :].rearrange("p (k n) -> p k n", k=2))

        def fetch(e, e_, c):
            s, dst = chunk_slot(c)
            e.dma_start(dst, chunk_src(e_, c)).then_inc(landed[s], 16)

        for c in range(RING):
            s, _ = chunk_slot(c)
            SP.wait(freed[s])
            SP.items.append(lambda e, c=c: fetch(e, 0, c))

        def sp_experts(e):
            with e.Fori(0, NE - 1) as i:
                for c in range(NCH):
                    e.wait_ge(p_use, i * NCH + (c + 1))
                    if c + RING < NCH:
                        src = chunk_src_dyn(i, c + RING)
                    else:
                        src = chunk_src_dyn(i + 1, c + RING - NCH)
                    s, dst = chunk_slot((c + RING) % NCH)
                    e.dma_start(dst, src).then_inc(landed[s], 16)
            for c in range(NCH - RING):
                e.wait_ge(p_use, (NE - 1) * NCH + c + 1)
                fetch(e, NE - 1, c + RING)

        def chunk_src_dyn(i, c):
            if c < 2 * KD:
                w_ = wg if c < KD else wu
                return w_[bass.ds(i, 1), (c % KD) * P:(c % KD + 1) * P, :].rearrange("o p n -> p (o n)")
            return wd[bass.ds(i, 1), (c - 2 * KD) * 2 * P:(c - 2 * KD + 1) * 2 * P, :].rearrange(
                "o (k p) n -> p (o k) n", p=P)

        SP.items.append(sp_experts)

        names = ("v_one", "v_gt", "v_hd", "p_gath", "p_xt", "p_ht", "p_dn", "a_xs", "a_xt",
                 "a_sg", "a_ht", "a_y", "v_acc0", "v_acc1", "p_sc0", "p_sc1")
        ev = {n: sem(n) for n in names}

        def prime(e, who):
            for n in names:
                if n[0] == who:
                    e.sem_inc(ev[n], 1)

        SLOTS_BACK = NCH // RING

        def pe_experts(e):
            prime(e, "p")
            with e.Fori(0, NE) as i:
                prev, this = i + 1, i + 2
                e.wait_ge(ev["v_one"], this)
                e.wait_ge(ev["a_xt"], prev)
                e.wait_ge(ev["v_gt"], prev)
                for t in range(NT):
                    for j in range(4):
                        e.matmul(ps[32 * j:32 * j + 32, 0, 0:T], ONE[:, t, :], H2[:, t, j * T:(j + 1) * T],
                                 start=(t == 0), stop=(t == NT - 1), skip_group_check=True)
                for t in range(NT):
                    ins = e.transpose(ps[:, 1, t * P:(t + 1) * P], Z[:, t, :], ident)
                ins.then_inc(ev["p_gath"], 1)
                e.wait_ge(ev["a_xs"], this)
                for b in range(2):
                    ins = e.transpose(ps[:, 0, T + b * P:T + (b + 1) * P], XS[:, b * P:(b + 1) * P], ident)
                ins.then_inc(ev["p_xt"], 1)
                e.wait_ge(ev["a_xt"], this)
                for c in range(2 * KD):
                    k = c % KD
                    if c == 0:
                        e.wait_ge(ev["a_sg"], prev)
                    if c == KD:
                        e.wait_ge(ev["v_hd"], prev)
                    s, slot = chunk_slot(c)
                    e.wait_ge(landed[s], i * (16 * SLOTS_BACK) + 16 * (landed_before[s] + c // RING + 1))
                    for n in range(4):
                        ins = e.matmul(ps[32 * n:32 * n + 32, 2 + c // KD, :],
                                       XT[:, k % 2, 32 * (k // 2):32 * (k // 2) + 32], slot[:, n * W:(n + 1) * W],
                                       start=(k == 0), stop=(k == KD - 1), skip_group_check=True)
                    ins.then_inc(p_use, 1)
                e.wait_ge(ev["v_hd"], this)
                e.wait_ge(ev["a_ht"], prev)
                for b in range(4):
                    ins = e.transpose(ps[:, 4, b * P:(b + 1) * P], HD[:, b * P:(b + 1) * P], ident)
                ins.then_inc(ev["p_ht"], 1)
                e.wait_ge(ev["a_ht"], this)
                e.wait_ge(ev["a_y"], prev)
                for c in range(2 * KD, NCH):
                    s, slot = chunk_slot(c)
                    e.wait_ge(landed[s], i * (16 * SLOTS_BACK) + 16 * (landed_before[s] + c // RING + 1))
                    for kk in range(2):
                        f = 2 * (c - 2 * KD) + kk
                        for nd in range(2):
                            g = 2 * nd + kk
                            ins = e.matmul(ps[32 * g:32 * g + 32, 5, :],
                                           HTT[:, f % 4, 32 * (f // 4):32 * (f // 4) + 32],
                                           slot[:, kk, nd * W:(nd + 1) * W],
                                           start=(c == 2 * KD), stop=(c == NCH - 1), skip_group_check=True)
                    ins.then_inc(p_use, 1)
                e.wait_ge(ev["a_y"], this)
                e.wait_ge(ev["v_gt"], this)
                for t in range(NT):
                    e.wait_ge(ev["v_acc0"], prev) if t == 0 else e.wait_ge(ev["v_acc0"], this)
                    for nd in range(2):
                        ins = e.matmul(ps[:, 6 + nd, :], GT[:, nd, t * P:(t + 1) * P], YS[:, :],
                                       start=True, stop=True, skip_group_check=True)
                    ins.then_inc(ev[f"p_sc{t}"], 1)

        def act_experts(e):
            prime(e, "a")
            with e.Fori(0, NE) as i:
                prev, this = i + 1, i + 2
                e.wait_ge(ev["p_gath"], this)
                e.wait_ge(ev["p_xt"], prev)
                e.activation(XS, ps[:, 0, 0:T], ACT.Copy).then_inc(ev["a_xs"], 1)
                e.wait_ge(ev["p_xt"], this)
                e.activation(XT.rearrange("p a b -> p (a b)"), ps[:, 0, T:2 * T], ACT.Copy).then_inc(ev["a_xt"], 1)
                e.wait_ge(p_use, i * NCH + KD)
                e.wait_ge(ev["v_hd"], prev)
                e.activation(SG, ps[:, 2, :], ACT.Silu).then_inc(ev["a_sg"], 1)
                e.wait_ge(ev["p_ht"], this)
                e.activation(HTT.rearrange("p a b -> p (a b)"), ps[:, 4, :], ACT.Copy).then_inc(ev["a_ht"], 1)
                e.wait_ge(p_use, i * NCH + NCH)
                e.wait_ge(ev["p_sc1"], prev)
                e.activation(YS, ps[:, 5, :], ACT.Copy).then_inc(ev["a_y"], 1)

        def dve_experts(e):
            prime(e, "v")
            with e.Fori(0, NE) as i:
                prev, this = i + 1, i + 2
                e.wait_ge(ev["p_gath"], prev)
                for t in range(NT):
                    r_ = rank[:, t, bass.ds(i, 1)]
                    e.tensor_scalar(ONE[:, t, :], iota[:, 0:CAP], r_, None, ALU.is_equal)
                    ins = e.tensor_scalar(Z[:, t, :], iota, r_, aff[:, t, bass.ds(i, 1)], ALU.is_equal, ALU.mult)
                ins.then_inc(ev["v_one"], 1)
                e.wait_ge(ev["p_gath"], this)
                e.wait_ge(ev["p_sc1"], prev)
                e.tensor_copy(GT[0:64, 0, :], ps[0:64, 1, 0:T])
                e.tensor_copy(GT[64:128, 1, :], ps[64:128, 1, 0:T]).then_inc(ev["v_gt"], 1)
                e.wait_ge(ev["a_sg"], this)
                e.wait_ge(p_use, i * NCH + 2 * KD)
                e.wait_ge(ev["p_ht"], prev)
                e.tensor_tensor(HD, SG, ps[:, 3, :], ALU.mult).then_inc(ev["v_hd"], 1)
                for t in range(NT):
                    e.wait_ge(ev[f"p_sc{t}"], this)
                    e.wait_ge(ev[f"v_acc{t}"], prev)
                    a_ = ACC[:, t, :].rearrange("p (n w) -> p n w", n=2)
                    e.tensor_tensor(a_, a_, ps[:, 6:8, :], ALU.add).then_inc(ev[f"v_acc{t}"], 1)

        for q in (PE, A, V):
            q.wait(rank_ok, acc0, gz, now(A), now(PE))
        PE.items.append(pe_experts)
        A.items.append(act_experts)
        V.items.append(dve_experts)
        acc_done = (ev["v_acc1"], NE + 1)
        G.wait(acc_done)
        for q in (A, V):
            q.wait(acc_done, (ev["v_acc0"], NE + 1))

        OUTT = at(32, NT, D)
        if tap:
            load(dram["tap3"].rearrange("(t p) d -> p t d", p=P), ACC, after=(acc_done,))
        row_rms(OUTT, ACC, OUTT)
        stores = []
        for t in range(NT):
            tt(OUTT[:, t, :], OUTT[:, t, :], GG2, ALU.mult)
            m = tt(OUTT[:, t, :], OUTT[:, t, :], X[:, t, :], ALU.add)
            stores.append(load(out[t * P:(t + 1) * P, :], OUTT[:, t, :], after=(m,)))
        SP.wait(*stores)

        block = ctx.enter_context(nc.Block())

        @block.sync
        def _(e):
            for item in SP.items:
                item(e)

        @block.tensor
        def _(e):
            for item in PE.items:
                item(e)

        @block.vector
        def _(e):
            for item in V.items:
                item(e)

        @block.scalar
        def _(e):
            for item in A.items:
                item(e)

        @block.gpsimd
        def _(e):
            for item in G.items:
                item(e)


def arrange(inputs):
    a = {k: np.asarray(v) for k, v in inputs.items()}

    def col(v):
        v = np.asarray(v)
        v = v.reshape(-1, P)
        return v.T

    pack = {
        "c": col(a["c"]), "c_2": col(a["c_2"]), "c_ctx": col(a["c_ctx_2"]), "conv_w": col(a["conv_w"]),
        "conv_b": col(a["conv_b"]), "norm_g": col(a["norm_g"]), "mnorm_g": col(a["mnorm_g"]),
        "anorm_g": col(a["anorm_g"]), "pre_mix_g": col(a["pre_mix_g_2"]), "conv_w_2": col(a["conv_w_2"]),
        "conv_b_2": col(a["conv_b_2"]),
    }
    cols = np.zeros((P, COLS["all"][1]), np.float32)
    for name, v in pack.items():
        s, n = COLS[name]
        cols[:, s:s + n] = v
    s, n = COLS["b_if"]
    cols[0:MH, s:s + 2] = a["b_if"].reshape(2, MH).T
    rows = np.concatenate([a[n].reshape(-1) for n in (
        "b_ada", "b_ada_2", "final_g", "post_mix_g_2", "pre_ffn_g_2", "post_ffn_g_2", "ret_norm_g_2",
        "b_router_2", "ret_decay_logit_2", "lam_q1", "lam_k1", "lam_q2", "lam_k2")])
    big = {
        "x": a["x"][0], "ctx": a["ctx_2"][0], "w_ada": a["w_ada"][0], "w_in": a["w_in"][0],
        "w_proj_m": a["w_proj_m"][0], "w_proj_a": a["w_proj_a"][0], "w_out": a["w_out"][0],
        "rel_bias": a["rel_bias"], "w_ada_2": a["w_ada_2"][0], "w_in_2": a["w_in_2"][0],
        "w_out_2": a["w_out_2"][0], "w_router": a["w_router_2"][0], "w_gate": a["w_gate_2"][0],
        "w_up": a["w_up_2"][0], "w_down": a["w_down_2"][0], "rows": rows, "cols": cols,
    }
    return {**big, **constants()}


def program(nc, arrays, tap=None):
    dram = {n: nc.dram_tensor(f"in_{n}", v.shape, F32, kind="ExternalInput").ap() for n, v in arrays.items()}
    dram["toeplitz"] = nc.dram_tensor("toeplitz", (AH * 2 * T,), F32, kind="Internal").ap()
    dram["affinity"] = nc.dram_tensor("affinity", (NE * T,), F32, kind="Internal").ap()
    for n in (tap or ()):
        dram[n] = nc.dram_tensor(n, (T, D), F32, kind="ExternalOutput").ap()
    out = nc.dram_tensor("out", (T, D), F32, kind="ExternalOutput").ap()
    build(nc, dram, out, tap)


def kernel(**inputs):
    import concourse.bacc as _bacc
    from concourse.bass_utils import run_bass_kernel_spmd as _run

    arrays = {n: np.ascontiguousarray(v) for n, v in arrange(inputs).items()}
    nc = _bacc.Bacc("TRN2", target_bir_lowering=False, num_devices=1)
    program(nc, arrays)
    r = _run(nc, [{f"in_{n}": v for n, v in arrays.items()}], core_ids=[0])
    return r.results[0]["out"].reshape(1, T, D)
```

```python
from contextlib import ExitStack
import math

import numpy as np
import concourse.bass as bass
from concourse import mybir

F32 = mybir.dt.float32
ALU = mybir.AluOpType
ACT = mybir.ActivationFunctionType
AX = mybir.AxisListType.X

P = 128
T = 256
NT = T // P
D = 1024
KD = D // P
W = 512
MH, MDV, MDK = 4, 512, 256
AH, ADH = 8, 64
RH, RD = 4, 128
NBUCKET, MAXDIST = 32, 128
NE, CAP, DE = 16, 32, 2048
EPS = 1e-6
NEG = -1e30
LAM_INIT = 0.8 - 0.6 * math.exp(0.0)
GRID_W = 64
SLOT = 2048
RING = 8

SPLITS = (1024, 1024, 2048, 2048, 2048, MH, MH, 1024, 1024, 1024, 1024, 1024, 1024)
QM, KM, VM, OM, ZM, IM, FM, QA, KA, VA, ZA, GM, GA = (sum(SPLITS[:i]) for i in range(13))
CB2, CC2, CX2, Q2, K2, V2, G2 = (W * i for i in range(7))

ROWS, COLS, CONST, EARLY, LATE = {}, {}, {}, {}, {}


def _lay(table, *items):
    at = 0
    for name, n in items:
        table[name] = (at, n)
        at += n
    table["all"] = (0, at)


_lay(ROWS, ("b_ada", 3 * D), ("b_ada_2", 6 * D), ("final_g", D), ("post_mix_g", D), ("pre_ffn_g", D),
     ("post_ffn_g", D), ("ret_norm_g", W), ("b_router", NE), ("decay", 2 * RH), ("lam", 4 * ADH))
_lay(COLS, ("c", KD), ("c_2", KD), ("c_ctx", KD), ("conv_w", 4 * 16), ("conv_b", 16), ("norm_g", KD),
     ("mnorm_g", 16), ("anorm_g", KD), ("pre_mix_g", KD), ("conv_w_2", 3 * 4), ("conv_b_2", 4), ("b_if", 2))
_lay(CONST, ("ident", P), ("iota", P), ("causal", P))
_lay(EARLY, ("selh", MH * P), ("onehot", 2 * T), ("future", 2 * T), ("mirror", P))
_lay(LATE, ("ahead", NT * T), ("behind", NT * T), ("before", NT * T), ("n1", T), ("n2", T),
     ("cosx", NT * 64), ("sinx", NT * 64), ("cosc", NT * 64), ("sinc", NT * 64), ("wn", 2 * NT))


def constants():
    one = np.zeros((P, CONST["all"][1]), np.float32)

    def put(a, table, name, v):
        s, n = table[name]
        a[:v.shape[0], s:s + n] = v.reshape(v.shape[0], n)

    p, j = np.arange(P)[:, None], np.arange(P)[None, :]
    put(one, CONST, "ident", (p == j).astype(np.float32))
    put(one, CONST, "iota", np.broadcast_to(j % CAP, (P, P)).astype(np.float32))
    put(one, CONST, "causal", np.where(p <= j, 0.0, NEG).astype(np.float32))
    early = np.zeros((P, EARLY["all"][1]), np.float32)
    selh = np.zeros((MH, MH, P), np.float32)
    for h in range(MH):
        selh[h, h] = 1.0
    put(early, EARLY, "selh", selh)
    dist = T - 1 - np.arange(2 * T)
    exact = NBUCKET // 2
    nf = np.maximum(dist, 1).astype(np.float32)
    large = exact + (np.log(nf / np.float32(exact)) / np.float32(math.log(MAXDIST / exact))
                     * np.float32(NBUCKET - exact)).astype(np.int32)
    bucket = np.where(dist < exact, dist, np.minimum(large, NBUCKET - 1))
    put(early, EARLY, "onehot", ((bucket[None, :] == np.arange(NBUCKET)[:, None]) & (dist >= 0)).astype(np.float32))
    put(early, EARLY, "future", np.broadcast_to(np.where(dist >= 0, 0.0, NEG), (AH, 2 * T)).astype(np.float32))
    put(early, EARLY, "mirror", (p + j == P - 1).astype(np.float32))
    late = np.zeros((P, LATE["all"][1]), np.float32)
    m = (np.arange(NT)[None, :, None] * P + np.arange(P)[:, None, None])
    n = np.arange(T)[None, None, :]
    put(late, LATE, "ahead", np.maximum(n - m, 0).astype(np.float32))
    put(late, LATE, "behind", np.maximum(m - n, 0).astype(np.float32))
    put(late, LATE, "before", (n < m).astype(np.float32))
    put(late, LATE, "n1", np.broadcast_to(np.arange(T) + 1.0, (P, T)).astype(np.float32))
    put(late, LATE, "n2", np.broadcast_to(T - np.arange(T), (P, T)).astype(np.float32))
    half = RD // 2
    inv = (np.float32(1.0) / (np.float32(10000.0) ** (np.arange(half, dtype=np.float32) / np.float32(half)))).astype(np.float32)
    tok = (np.arange(NT)[None, :, None] * P + np.arange(P)[:, None, None]).astype(np.float32)
    for base, c, s in ((T, "cosx", "sinx"), (0, "cosc", "sinc")):
        ang = ((tok + np.float32(base)) * inv[None, None, :]).astype(np.float32)
        put(late, LATE, c, np.cos(ang.astype(np.float64)).astype(np.float32))
        put(late, LATE, s, np.sin(ang.astype(np.float64)).astype(np.float32))
    put(late, LATE, "wn", np.concatenate([T - 1 - tok[:, :, 0], tok[:, :, 0]], axis=1))
    return {"const": one, "early": early, "late": late}


class Queue:

    def __init__(self, sem, chained):
        self.sem, self.chained = sem, chained
        self.items, self.count, self.seen = [], 0, {}

    def wait(self, *marks):
        for mark in marks:
            if mark is None:
                continue
            sem, value = mark
            if self.seen.get(sem.name, 0) < value:
                self.seen[sem.name] = value
                self.items.append(lambda e, s=sem, v=value: e.wait_ge(s, v))

    def do(self, issue, after=(), signal=True):
        self.wait(*after)
        if self.chained and self.count:
            self.wait((self.sem, self.count))
        if not signal:
            self.items.append(issue)
            return None
        self.count += 1
        self.items.append(lambda e: issue(e).then_inc(self.sem, 1))
        return (self.sem, self.count)


def build(nc, dram, out, tap=None):
    ctx = ExitStack()
    with ctx:
        def sem(name):
            return ctx.enter_context(nc.semaphore(name))

        ring = ctx.enter_context(nc.sbuf_tensor("ring", [P, RING, SLOT], F32))
        KB = 256
        arena = ctx.enter_context(nc.sbuf_tensor("arena", [P, 136 * KB], F32))
        keep = ctx.enter_context(nc.sbuf_tensor("keep", [P, 1990], F32))
        ps = ctx.enter_context(nc.psum_tensor("ps", [P, 8, W], F32))

        def at(kb, *shape):
            n = int(np.prod(shape))
            v = arena[:, int(kb * KB):int(kb * KB) + n]
            if len(shape) == 2:
                return v.rearrange("p (a b) -> p a b", a=shape[0])
            if len(shape) == 3:
                return v.rearrange("p (a b c) -> p a b c", a=shape[0], b=shape[1])
            return v

        used = [0]

        def small(*shape):
            n = int(np.prod(shape))
            v = keep[:, used[0]:used[0] + n]
            used[0] += n
            assert used[0] <= 1990
            if len(shape) == 2:
                return v.rearrange("p (a b) -> p a b", a=shape[0])
            if len(shape) == 3:
                return v.rearrange("p (a b c) -> p a b c", a=shape[0], b=shape[1])
            return v

        const, cols = small(CONST["all"][1]), small(COLS["all"][1])
        wr = small(KD, NE)
        early, late = at(118, EARLY["all"][1]), at(62, LATE["all"][1])

        def part(v, table, name, rows=P):
            s, n = table[name]
            return v[0:rows, s:s + n]

        ident, iota = part(const, CONST, "ident"), part(const, CONST, "iota")
        causal = part(const, CONST, "causal")

        PE, V, A, G, SP = (Queue(sem(n), c) for n, c in
                           (("pe", False), ("dve", True), ("act", True), ("pool", True), ("sp", False)))

        def mm(out_, lhsT, rhs, start, stop, after=(), signal=False):
            return PE.do(lambda e: e.matmul(out_, lhsT, rhs, start=start, stop=stop, skip_group_check=True),
                         after, signal)

        def flip(out_, in_, after=(), signal=False):
            k = in_.shape[0]
            return PE.do(lambda e: e.transpose(out_, in_, ident[0:k, 0:k]), after, signal)

        def tt(o, a, b, op, after=()):
            return V.do(lambda e: e.tensor_tensor(o, a, b, op), after)

        def ts(o, a, s1, s2, op0, op1=None, after=()):
            if op1 is None:
                return V.do(lambda e: e.tensor_scalar(o, a, s1, None, op0), after)
            return V.do(lambda e: e.tensor_scalar(o, a, s1, s2, op0, op1), after)

        def stt(o, a, s, b, op0, op1, after=()):
            return V.do(lambda e: e.scalar_tensor_tensor(out=o, in0=a, scalar=s, in1=b, op0=op0, op1=op1), after)

        def recip(o, a, after=()):
            return V.do(lambda e: e.reciprocal(o, a), after)

        def vcopy(o, a, after=()):
            return V.do(lambda e: e.tensor_copy(o, a), after)

        def reduce(o, a, op, after=()):
            return V.do(lambda e: e.tensor_reduce(o, a, AX, op), after)

        def act(o, a, func, scale=1.0, bias=0.0, accum=None, after=()):
            if accum is None:
                return A.do(lambda e: e.activation(o, a, func, bias=bias, scale=scale), after)
            return A.do(lambda e: e.activation(o, a, func, bias=bias, scale=scale, accum_out=accum), after)

        def acopy(o, a, after=()):
            return act(o, a, ACT.Copy, after=after)

        def now(q):
            return (q.sem, q.count)

        loads = [0]

        def load(dst, src, after=(), queue=None):
            s = sem(f"load{loads[0]}")
            loads[0] += 1
            q = queue or G
            q.wait(*after)
            q.items.append(lambda e: e.dma_start(dst, src).then_inc(s, 16))
            return (s, 16)

        landed = [sem(f"landed{i}") for i in range(RING)]
        chunks, freed = [0], [None] * RING

        def take(src, shape):
            s = chunks[0] % RING
            chunks[0] += 1
            dst = ring[:, s, 0:int(np.prod(shape))]
            if len(shape) == 2:
                dst = dst.rearrange("p (a b) -> p a b", a=shape[0])
            SP.wait(freed[s])
            SP.items.append(lambda e: e.dma_start(dst, src).then_inc(landed[s], 16))
            return dst, (landed[s], 16 * ((chunks[0] - 1) // RING + 1)), s

        bank_free = [None] * 8

        rows = dram["rows"]

        def row(name, s=0, n=None):
            a, m = ROWS[name]
            return rows[a + s:a + s + (m if n is None else n)]

        X = at(0, NT, D)
        cols_in = load(cols, dram["cols"], queue=A)
        const_in = load(const, dram["const"], queue=A)
        x_in = load(X, dram["x"].rearrange("(t p) d -> p t d", p=P), queue=A)
        gate_pow = small(16)
        pow_in = G.do(lambda e: e.memset(gate_pow, -0.5))
        ones = small(2)
        ones_in = G.do(lambda e: e.memset(ones, 1.0))

        TA = at(128, 4, W)
        ta_free, ta_turn = [None] * 4, [0]

        def scratch():
            i = ta_turn[0] % 3
            ta_turn[0] += 1
            return TA[:, i, :], i

        def logistic(o, pre, after=()):
            e = act(o, pre, ACT.Exp, scale=-1.0, after=(*after, now(V)))
            ts(o, o, 1.0, None, ALU.add, after=(e,))
            return recip(o, o)

        def log1p_exp_neg_abs(o, x, t1, t2):
            m = stt(t1, x, -1.0, x, ALU.mult, ALU.max)
            m = act(t1, t1, ACT.Exp, scale=-1.0, after=(m,))
            ts(t2, t1, 2.0, None, ALU.add, after=(m,))
            recip(t2, t2)
            tt(t1, t1, t2, ALU.mult)
            tt(t2, t1, t1, ALU.mult)
            ts(o, t2, 1.0 / 15, None, ALU.mult)
            for n in (13, 11, 9, 7, 5, 3):
                stt(o, o, 1.0 / n, t2, ALU.add, ALU.mult)
            stt(o, o, 1.0, t1, ALU.add, ALU.mult)
            return ts(o, o, 2.0, None, ALU.mult)

        def log_sigmoid(o, x, t1, t2):
            log1p_exp_neg_abs(o, x, t1, t2)
            return stt(o, x, 0.0, o, ALU.min, ALU.subtract)

        ssq = small(16)

        def rstd(n, width, after=()):
            m = ts(ssq[:, 0:n], ssq[:, 0:n], 1.0 / width, EPS, ALU.mult, ALU.add, after=after)
            return G.do(lambda e: e.tensor_tensor(ssq[:, 0:n], ssq[:, 0:n], gate_pow[:, 0:n], ALU.pow),
                        (m, pow_in))

        def row_rms(o, x, junk, after=(), gain=None, gain_in=None):
            A.wait(now(V), now(G))
            for t in range(NT):
                m = act(junk[:, t, :], x[:, t, :], ACT.Square, accum=ssq[:, t:t + 1], after=after)
            r = rstd(NT, D, after=(m,))
            for t in range(NT):
                if gain is None:
                    m = ts(o[:, t, :], x[:, t, :], ssq[:, t:t + 1], None, ALU.mult, after=(r,))
                else:
                    m = stt(o[:, t, :], x[:, t, :], ssq[:, t:t + 1], gain, ALU.mult, ALU.mult, after=(r, gain_in))
            return m

        def flip_tokens(dst, src, ntile, ready, evac, first=0):
            for k in range(first, ntile, 2):
                b = 6 + (k // 2) % 2
                PE.wait(bank_free[b])
                for i in range(2):
                    for t in range(NT):
                        m = flip(ps[:, b, i * T + t * P:i * T + (t + 1) * P], src[:, t, (k + i) * P:(k + i + 1) * P],
                                 after=(ready, const_in), signal=(i == 1 and t == NT - 1))
                for i in range(2):
                    bank_free[b] = evac(k + i, ps[:, b, i * T:(i + 1) * T], m)
            return bank_free[b]

        cst = small(3 * KD)
        call = cols[:, COLS["c"][0]:COLS["c"][0] + 3 * KD]
        sg = logistic(cst, call, after=(cols_in,))
        m = tt(cst, cst, call, ALU.mult)
        crep = at(135, KD, 32)
        crep2 = small(KD, 32)
        m = vcopy(crep, cst[:, 0:KD].unsqueeze(2).broadcast_to([P, KD, 32]))
        vcopy(crep2[:, :, 0:16], cst[:, KD:2 * KD].unsqueeze(2).broadcast_to([P, KD, 16]))
        crep_ok = vcopy(crep2[:, :, 16:32], cst[:, 2 * KD:3 * KD].unsqueeze(2).broadcast_to([P, KD, 16]))

        def ada(w, c0, ngroup, rep, bias, bank, dst, dst_free=None, stored=None):
            rows_per = SLOT // (ngroup * W)
            bt = [load(dst[32 * n:32 * n + 32, :], row(bias, c0 + n * W, W).partition_broadcast(32),
                       after=(dst_free,)) for n in range(ngroup)]
            PE.wait(bank_free[bank], crep_ok)
            for q in range(KD // rows_per):
                src = w[q * rows_per * P:(q + 1) * rows_per * P, c0:c0 + ngroup * W]
                slot, got, s = take(src.rearrange("(k p) n -> p k n", p=P), (rows_per, ngroup * W))
                for kk in range(rows_per):
                    k = q * rows_per + kk
                    for n in range(ngroup):
                        m = mm(ps[32 * n:32 * n + 32, bank, :], rep[:, k, :], slot[:, kk, n * W:(n + 1) * W],
                               k == 0, k == KD - 1, after=(got,), signal=(n == ngroup - 1 and kk == rows_per - 1))
                freed[s] = m
                if q < KD // rows_per - 1:
                    yield
            n = 32 * ngroup
            bank_free[bank] = m = tt(dst[0:n, :], ps[0:n, bank, :], dst[0:n, :], ALU.add, after=(m, *bt))
            if stored is not None:
                for n in range(ngroup):
                    m = load(dram["mods"][stored + n * W:stored + (n + 1) * W].unsqueeze(0),
                             dst[32 * n:32 * n + 1, :], after=(m,))
                    mods_in.append(m)
            ada_mark.append(bank_free[bank])
            yield

        mods_in, ada_mark = [], []
        def ada_columns(rowsv, ready, pick, dst_sh, dst_g, g):
            PE.wait(bank_free[7])
            for b in range(4):
                m = flip(ps[:, 7, b * P:(b + 1) * P], rowsv[:, b * P:(b + 1) * P], after=(ready, const_in), signal=True)
            v = ps[:, 7, :].rearrange("p (b n j) -> p n b j", b=4, n=4)
            vcopy(dst_sh.rearrange("p (n b) -> p n b", n=2), v[:, 0:2, :, pick], after=(m,))
            bank_free[7] = m = stt(dst_g.rearrange("p (n b) -> p n b", n=2), v[:, 2:4, :, pick], 1.0,
                                   g.rearrange("p (n b) -> p n b", n=2), ALU.add, ALU.mult)
            return m

        XN, HT = at(16, NT, D), at(8, KD, T)
        modA = at(114, W)
        first_rows = ada(dram["w_ada"], 0, 4, crep, "b_ada", 3, modA)
        next(first_rows)
        xn = row_rms(XN, X, at(32, NT, D), after=(x_in,))
        for _ in first_rows:
            pass
        mA = ada_mark[-1]
        G.wait(mA)
        early_in = load(early, dram["early"])
        table = small(AH)
        table_in = load(table[0:NBUCKET, :], dram["rel_bias"])
        wif = at(126, KD, 2 * MH)
        wif_in = load(wif, dram["w_in"][:, IM:IM + 2 * MH].rearrange("(k p) n -> p k n", p=P))
        lam4 = at(127, 4 * ADH)
        lam_in = load(lam4, row("lam").partition_broadcast(P))
        wr_in = load(wr, dram["w_router"].rearrange("(k p) n -> p k n", p=P))
        brt = small(NE)
        brt_in = load(brt, row("b_router").partition_broadcast(P))
        lg = small(2 * RH)
        lg_in = load(lg, row("decay").partition_broadcast(P))
        sh1, gs1 = small(KD), small(KD)
        mod1 = ada_columns(modA, mA, 0, sh1, gs1, part(cols, COLS, "norm_g"))


        def modulate(dst, sh, gs, ready):
            def evac(k, view, m):
                return act(dst[:, k, :], view, ACT.Identity, scale=gs[:, k:k + 1], bias=sh[:, k:k + 1],
                           after=(m, ready))
            return evac

        h_ok = flip_tokens(HT, XN, KD, xn, modulate(HT, sh1, gs1, mod1))

        turn = [0]

        def next_bank():
            b = turn[0] % 3
            turn[0] += 1
            return b

        def natural(lhs, ktiles, w, c0, ready, evac, order=None):
            pair = (next_bank(), next_bank())
            order = order or [(q, ready) for q in range(ktiles // 4)]
            for at_, (q, ok) in enumerate(order):
                src = w[q * 4 * P:(q + 1) * 4 * P, c0:c0 + W]
                slot, got, s = take(src.rearrange("(k p) n -> p k n", p=P), (4, W))
                for t in range(NT):
                    if at_ == 0:
                        PE.wait(bank_free[pair[t]])
                    for kk in range(4):
                        m = mm(ps[:, pair[t], :], lhs(4 * q + kk, t), slot[:, kk, :], at_ == 0 and kk == 0,
                               at_ == len(order) - 1 and kk == 3, after=(ok, got), signal=(kk == 3))
                    if at_ == len(order) - 1:
                        bank_free[pair[t]] = evac(t, ps[:, pair[t], :], m)
                freed[s] = m

        def by_tile(lhs, w, order, evac, finish):
            got = {}
            for n in range(2):
                for q, _ in order:
                    src = w[q * 4 * P:(q + 1) * 4 * P, n * W:(n + 1) * W]
                    got[n, q] = take(src.rearrange("(k p) n -> p k n", p=P), (4, W))
            for t in range(NT):
                for n in range(2):
                    b = next_bank()
                    PE.wait(bank_free[b])
                    for at_, (q, ok) in enumerate(order):
                        slot, landed_, s = got[n, q]
                        for kk in range(4):
                            m = mm(ps[:, b, :], lhs(4 * q + kk, t), slot[:, kk, :], at_ == 0 and kk == 0,
                                   at_ == 1 and kk == 3, after=(ok, landed_), signal=(kk == 3))
                        freed[s] = m
                    bank_free[b] = evac(t, n, ps[:, b, :], m)
                finish(t)

        def column_rstd(v, width, after=()):
            m = ts(v, v, 1.0 / width, EPS, ALU.mult, ALU.add, after=after)
            return G.do(lambda e: e.tensor_tensor(v, v, gate_pow[:, 0:1], ALU.pow), (m, pow_in))

        def transposed(xT, w, c0, ready, evac):
            PE.wait(ready)
            got = []
            for q in range(2):
                src = w[q * 4 * P:(q + 1) * 4 * P, c0:c0 + W]
                got.append(take(src.rearrange("(k p) n -> p k n", p=P), (4, W)))
            for i in range(4):
                if i % 2 == 0:
                    b = next_bank()
                    PE.wait(bank_free[b])
                view = ps[:, b, (i % 2) * T:(i % 2 + 1) * T]
                for k in range(KD):
                    slot, ok, s = got[k // 4]
                    m = mm(view, slot[:, k % 4, i * P:(i + 1) * P], xT[:, k, :], k == 0, k == KD - 1,
                           after=(ok,), signal=(k == KD - 1 or (i == 3 and k == 3)))
                    if i == 3 and k % 4 == 3:
                        freed[s] = m
                if i % 2 == 1:
                    for j in (i - 1, i):
                        bank_free[b] = evac(j, ps[:, b, (j % 2) * T:(j % 2 + 1) * T], m)

        hT = lambda k, t: HT[:, k, t * P:(t + 1) * P]

        QT, KT = at(32, KD, T), at(40, KD, T)
        cw = part(cols, COLS, "conv_w").rearrange("p (j c) -> p j c", j=4)
        cb = part(cols, COLS, "conv_b")
        conv_ok = {}

        def conv_evac(base, dst):
            def evac(i, view, m):
                c = base + i
                o = dst[:, c % KD, :]
                f = ts(o, view, cw[:, 3, c:c + 1], cb[:, c:c + 1], ALU.mult, ALU.add, after=(m,))
                for back in (1, 2, 3):
                    f = stt(o[:, back:T], view[:, 0:T - back], cw[:, 3 - back, c:c + 1], o[:, back:T],
                            ALU.mult, ALU.add)
                if i % 2 == 1:
                    two = dst[:, c % KD - 1:c % KD + 1, :]
                    conv_ok[dst is KT] = act(two, two, ACT.Silu, after=(f,))
                return f
            return evac

        MODT = [at(86 + 2 * i, W) for i in range(4)]
        sh2, gs2, shc, gsc = (small(KD) for _ in range(4))
        rounds = [ada(dram["w_ada_2"], 0, 4, crep2, "b_ada_2", 3, MODT[0]),
                  ada(dram["w_ada"], 2 * D, 2, crep, "b_ada", 3, MODT[1], None, 0),
                  ada(dram["w_ada_2"], 2 * D, 4, crep2, "b_ada_2", 3, MODT[2], None, D),
                  ada(dram["w_ada_2"], 4 * D, 4, crep2, "b_ada_2", 3, MODT[3], None, 3 * D)]
        spread_rounds = (x for r_ in rounds for x in r_)

        def some_ada(n):
            for _ in range(n):
                next(spread_rounds, None)

        for n in range(4):
            transposed(HT, dram["w_in"], QM + n * W, h_ok, conv_evac(4 * n, QT if n < 2 else KT))
            some_ada(3)
        ada_columns(MODT[0], ada_mark[1], 0, sh2, gs2, part(cols, COLS, "pre_mix_g"))
        modc_ok = ada_columns(MODT[0], ada_mark[1], 16, shc, gsc, part(cols, COLS, "pre_mix_g"))

        gi, gf, gF, gt1, gt2 = (at(128 + i, T)[0:MH, :] for i in range(5))
        b_if = part(cols, COLS, "b_if", MH)
        for j in range(2):
            for k in range(KD):
                m = mm(ps[0:MH, 6, j * T:(j + 1) * T], wif[:, k, j * MH:(j + 1) * MH], HT[:, k, :], k == 0, k == KD - 1,
                       after=(h_ok, wif_in, bank_free[6]), signal=(k == KD - 1))
        ts(gi, ps[0:MH, 6, 0:T], b_if[:, 0:1], None, ALU.add, after=(m,))
        bank_free[6] = ts(gf, ps[0:MH, 6, T:2 * T], b_if[:, 1:2], None, ALU.add)
        log_sigmoid(gF, gf, gt1, gt2)
        V.do(lambda e: e.memset(gt1, 0.0))
        V.do(lambda e: e.tensor_tensor_scan(gf, gF, gt1, 0.0, ALU.add, ALU.add))
        tt(gi, gi, gf, ALU.subtract)
        V.do(lambda e: e.tensor_tensor_scan(gF, gi, gt1, 0.0, ALU.max, ALU.max))
        m = tt(gf, gf, gF, ALU.add)
        em = act(gf, gf, ACT.Exp, scale=-1.0, after=(m,))
        negM = ts(gF, gF, -1.0, None, ALU.mult)
        ccol, emcol = small(NT, MH), small(NT, MH)
        ET = at(48, MH, 3 * P)
        def gate_tables():
            PE.wait(bank_free[7])
            for t in range(NT):
                flip(ps[:, 7, t * MH:(t + 1) * MH], gi[:, t * P:(t + 1) * P], after=(negM, em, early_in), signal=True)
                m = flip(ps[:, 7, 8 + t * MH:8 + (t + 1) * MH], gf[:, t * P:(t + 1) * P], signal=True)
            vcopy(ccol, ps[:, 7, 0:8].rearrange("p (t h) -> p t h", t=NT), after=(m,))
            bank_free[7] = vcopy(emcol, ps[:, 7, 8:16].rearrange("p (t h) -> p t h", t=NT))
            selh = part(early, EARLY, "selh", MH).rearrange("p (h m) -> p h m", h=MH)
            et_ok = None
            for h in range(MH):
                if h % 2 == 0:
                    PE.wait(bank_free[6])
                    for j in range(2):
                        m = mm(ps[:, 6, j * T:(j + 1) * T], selh[:, h + j, :], gF, True, True, signal=True)
                nm = ps[:, 6, (h % 2) * T:(h % 2 + 1) * T]
                tt(ET[:, h, 0:P], nm[:, 0:P], causal, ALU.add, after=(m,))
                vcopy(ET[:, h, P:2 * P], nm[:, P:2 * P])
                bank_free[6] = f = tt(ET[:, h, 2 * P:3 * P], nm[:, P:2 * P], causal, ALU.add)
                act(ET[:, h, 0:2 * P], ET[:, h, 0:2 * P], ACT.Exp, bias=ccol[:, 0, h:h + 1], after=(f,))
                et_ok = act(ET[:, h, 2 * P:3 * P], ET[:, h, 2 * P:3 * P], ACT.Exp, bias=ccol[:, 1, h:h + 1])
            return et_ok

        HM = at(16, NT, 2 * D)
        v_ok = {}

        def v_evac(n):
            def evac(t, view, m):
                v_ok[n] = acopy(HM[:, t, n * W:(n + 1) * W], view, after=(m,))
                return v_ok[n]
            return evac

        PT = [at(114 + 1.5 * i, 3 * P) for i in range(2)]
        den = small(2, NT)
        head_ok = {}

        def mlstm_scores(h):
            for k in range(2):
                m = mm(ps[:, 4, 0:T], KT[:, 2 * h + k, 0:P], QT[:, 2 * h + k, :], k == 0, k == 1,
                       after=(conv_ok[True], conv_ok[False], bank_free[4]))
            for k in range(2):
                m = mm(ps[:, 4, T:T + P], KT[:, 2 * h + k, P:T], QT[:, 2 * h + k, P:T], k == 0, k == 1,
                       signal=(k == 1))
            bank_free[4] = stt(PT[h % 2], ps[:, 4, 0:3 * P], MDK ** -0.5, ET[:, h, :], ALU.mult, ALU.mult,
                               after=(m, et_ok))
            return bank_free[4]

        def mlstm_values(h, ready):
            p = PT[h % 2]
            PE.wait(ready, ones_in, bank_free[5], bank_free[6], bank_free[7], v_ok[h])
            v = [HM[:, t, h * W:(h + 1) * W] for t in range(NT)]
            mm(ps[:, 5, :], p[:, 0:P], v[0], True, True)
            mm(ps[:, 6, :], p[:, P:2 * P], v[0], True, False)
            mm(ps[:, 6, :], p[:, 2 * P:3 * P], v[1], False, True)
            mm(ps[:, 7, 0:1], p[:, 0:P], ones[:, 0:1], True, True)
            mm(ps[:, 7, 1:2], p[:, P:2 * P], ones[:, 0:1], True, False)
            m = mm(ps[:, 7, 1:2], p[:, 2 * P:3 * P], ones[:, 0:1], False, True, signal=True)
            d, e = den[:, 0, :], den[:, 1, :]
            ts(d, ps[:, 7, 0:NT], -1.0, None, ALU.mult, after=(m,))
            tt(d, d, ps[:, 7, 0:NT], ALU.max)
            tt(d, d, emcol[:, :, h], ALU.max)
            bank_free[7] = recip(e, d)
            for t in range(NT):
                m = ts(v[t], ps[:, 5 + t, :], e[:, t:t + 1], None, ALU.mult)
                bank_free[5 + t] = m
            head_ok[h] = m

        QMASK, KAT, VAN = at(62, AH, NT, T), at(78, KD, T), at(86, NT, D)
        zq = G.do(lambda e: e.memset(QMASK, 0.0))
        aq_ok, ak_ok, av_ok = {}, {}, {}

        def qa_evac(n):
            def evac(i, view, m):
                h = 4 * n + i
                act(QMASK[0:ADH, h, 0, :], view[0:ADH, :], ACT.Copy, scale=ADH ** -0.5, after=(m, zq))
                aq_ok[h] = act(QMASK[ADH:P, h, 1, :], view[ADH:P, :], ACT.Copy, scale=ADH ** -0.5)
                return aq_ok[h]
            return evac

        def ka_evac(n):
            def evac(i, view, m):
                ak_ok[4 * n + i] = acopy(KAT[:, 4 * n + i, :], view, after=(m,))
                return ak_ok[4 * n + i]
            return evac

        def va_evac(n):
            def evac(t, view, m):
                av_ok[n] = acopy(VAN[:, t, n * W:(n + 1) * W], view, after=(m,))
                return av_ok[n]
            return evac

        toep = dram["toeplitz"]
        brow = at(133, 2 * T)[0:AH, :]
        m = mm(ps[0:AH, 6, :], table[0:NBUCKET, :], part(early, EARLY, "onehot", NBUCKET), True, True,
               after=(bank_free[6], table_in, early_in), signal=True)
        bank_free[6] = m = tt(brow, ps[0:AH, 6, :], part(early, EARLY, "future", AH), ALU.add, after=(m,))
        m = load(toep.rearrange("(h j) -> h j", h=AH), brow, after=(m,))
        BREV, BIAS = at(94, AH, T), at(54, AH, T)
        brev_in = load(BREV, bass.AP(toep.tensor, 0, [[1, P], [2 * T, AH], [1, T]]), after=(m,))

        def bias_turn():
            for j in range(4):
                b = 4 + j % 2
                m = mm(ps[:, b, :], part(early, EARLY, "mirror"), BREV[:, 2 * j:2 * j + 2, :].rearrange("p a b -> p (a b)"),
                       True, True, after=(brev_in, bank_free[b]), signal=True)
                bank_free[b] = acopy(BIAS[:, 2 * j:2 * j + 2, :].rearrange("p a b -> p (a b)"), ps[:, b, :], after=(m,))
            return bank_free[b]

        lamv = small(2)
        l4 = lam4.rearrange("p (a b) -> p a b", a=4)
        tt(l4[:, 0:4:2, :], l4[:, 0:4:2, :], l4[:, 1:4:2, :], ALU.mult, after=(lam_in,))
        m = reduce(lamv, l4[:, 0:4:2, :], ALU.add)
        m = act(lamv, lamv, ACT.Exp, after=(m,))
        tt(lamv[:, 0:1], lamv[:, 1:2], lamv[:, 0:1], ALU.subtract, after=(m,))
        neglam = lamv[:, 0:1]
        ts(neglam, neglam, LAM_INIT, None, ALU.subtract)

        for j in range(8):
            if 2 <= j <= 5:
                r = mlstm_scores(j - 2)
            if j < 4:
                natural(hT, KD, dram["w_in"], VM + j * W, h_ok, v_evac(j))
                if j == 0:
                    et_ok = gate_tables()
            else:
                n = j % 2
                transposed(HT, dram["w_in"], (QA if j < 6 else KA) + n * W, h_ok, qa_evac(n) if j < 6 else ka_evac(n))
            if 2 <= j <= 5:
                mlstm_values(j - 2, r)
            some_ada(2)

        bias_ok = bias_turn()
        HA = at(94, NT, D)
        LG = [at(102 + 3 * i, 2, 3 * P) for i in range(2)]
        AM = [at(108 + 1.5 * i, 3 * P) for i in range(2)]
        AT = [at(111 + 1.5 * i, 3 * P) for i in range(2)]
        mx, sm = small(2, NT), small(2, NT)
        at_free = [None, None]

        def attn_scores(h):
            for m_ in range(2):
                PE.wait(bank_free[4 + m_], aq_ok[h], ak_ok[h])
                q = QMASK[:, h, m_, :]
                mm(ps[:, 4 + m_, 0:T], q[:, P:T], KAT[:, h, :], True, True)
                m = mm(ps[:, 4 + m_, T:T + P], q[:, 0:P], KAT[:, h, 0:P], True, True, signal=True)
            L = LG[h % 2]
            V.wait(now(A))
            tt(L[:, :, 0:T], ps[:, 4:6, 0:T], BIAS[:, h, :].unsqueeze(1).broadcast_to([P, 2, T]), ALU.add,
               after=(m, bias_ok))
            m = tt(L[:, :, T:T + P], ps[:, 4:6, T:T + P], BIAS[:, h, P:T].unsqueeze(1).broadcast_to([P, 2, P]), ALU.add)
            bank_free[4] = bank_free[5] = m
            reduce(mx[:, :, 0], L[:, :, 0:T], ALU.max)
            reduce(mx[:, :, 1], L[:, :, T:T + P], ALU.max)
            m = ts(mx, mx, -1.0, None, ALU.mult)
            for m_ in range(2):
                act(L[:, m_, 0:T], L[:, m_, 0:T], ACT.Exp, bias=mx[:, m_, 0:1], accum=sm[:, m_, 0:1], after=(m,))
                a = act(L[:, m_, T:T + P], L[:, m_, T:T + P], ACT.Exp, bias=mx[:, m_, 1:2], accum=sm[:, m_, 1:2])
            recip(sm, sm, after=(a,))
            ts(sm[:, 1, :], sm[:, 1, :], neglam, None, ALU.mult)
            V.wait(at_free[h % 2])
            am = AM[h % 2]
            for q, (lo, hi) in enumerate(((0, T), (T, T + P))):
                ts(L[:, 1, lo:hi], L[:, 1, lo:hi], sm[:, 1, q:q + 1], None, ALU.mult)
                m = stt(am[:, lo:hi], L[:, 0, lo:hi], sm[:, 0, q:q + 1], L[:, 1, lo:hi], ALU.mult, ALU.add)
            return m

        def attn_flips(h, ready):
            am, aT = AM[h % 2], AT[h % 2]
            PE.wait(ready, bank_free[6])
            for j in range(3):
                m = flip(ps[:, 6, j * P:(j + 1) * P], am[:, j * P:(j + 1) * P], signal=True)
            bank_free[6] = at_free[h % 2] = acopy(aT, ps[:, 6, 0:3 * P], after=(m,))
            return bank_free[6]

        def attn_values(h, c):
            aT = AT[h % 2]
            v = [VAN[:, t, h * P:(h + 1) * P] for t in range(NT)]
            PE.wait(c, bank_free[7], av_ok[h // 4])
            mm(ps[:, 7, 0:P], aT[:, 2 * P:3 * P], v[0], True, True)
            mm(ps[:, 7, P:T], aT[:, 0:P], v[0], True, False)
            m = mm(ps[:, 7, P:T], aT[:, P:2 * P], v[1], False, True, signal=True)
            bank_free[7] = acopy(HA[:, :, h * P:(h + 1) * P], ps[:, 7, 0:T].rearrange("p (t e) -> p t e", t=NT),
                                 after=(m,))
            return bank_free[7]

        hssq = small(NT * MH)

        def o_evac(n):
            def evac(t, view, m):
                s, i = scratch()
                e = act(s, view, ACT.Sigmoid, after=(m, ta_free[i]))
                hm = HM[:, t, n * W:(n + 1) * W]
                v = tt(hm, hm, s, ALU.mult, after=(e,))
                ta_free[i] = act(s, hm, ACT.Square, accum=hssq[:, NT * n + t:NT * n + t + 1], after=(v,))
                return e
            return evac

        def head_rstd():
            m = ts(hssq, hssq, 1.0 / MDV, EPS, ALU.mult, ALU.add, after=(now(A),))
            V.wait(G.do(lambda e: e.tensor_tensor(hssq, hssq, gate_pow[:, 0:NT * MH], ALU.pow), (m, pow_in)))

        def z_evac(n):
            def evac(t, view, m):
                s, i = scratch()
                e = act(s, view, ACT.Silu, after=(m, ta_free[i]))
                hm = HM[:, t, n * W:(n + 1) * W]
                ta_free[i] = zdone[n] = stt(hm, hm, hssq[:, NT * n + t:NT * n + t + 1], s, ALU.mult, ALU.mult,
                                            after=(e,))
                return e
            return evac

        zdone = {}
        HMT = at(32, 2 * KD, T)
        mg = part(cols, COLS, "mnorm_g")

        def scaled(dst, g):
            def evac(k, view, m):
                return act(dst[:, k, :], view, ACT.Copy, scale=g[:, k:k + 1], after=(m,))
            return evac

        def head_flip(h):
            return flip_tokens(HMT, HM, 4 * (h + 1), zdone[h], scaled(HMT, mg), 4 * h)

        steps = [lambda n=n: natural(hT, KD, dram["w_in"], VA + n * W, h_ok, va_evac(n)) for n in range(2)]
        steps += [lambda n=n: natural(hT, KD, dram["w_in"], OM + n * W, h_ok, o_evac(n)) for n in range(4)]
        steps += [lambda n=n: natural(hT, KD, dram["w_in"], ZM + n * W, h_ok, z_evac(n)) for n in range(3)]
        A.wait(*mods_in)
        ready = turned = None
        for j, step in enumerate(steps):
            if j:
                turned = attn_flips(j - 1, ready)
            if j < AH:
                ready = attn_scores(j)
            if j == 6:
                head_rstd()
            step()
            if j:
                attn_done = attn_values(j - 1, turned)
        attn_pe = now(PE)

        sq = at(102, NT, D)
        assq = small(NT * AH)
        hmt_free = attn_pe
        A.wait(hmt_free)
        head_flip(0)
        V.wait(attn_done)
        tt(sq, HA, HA, ALU.mult, after=(attn_pe,))
        m = reduce(assq, sq.rearrange("p t (h e) -> p (t h) e", h=AH), ALU.add)
        m = ts(assq, assq, 1.0 / (2 * ADH), EPS, ALU.mult, ALU.add)
        m = G.do(lambda e: e.tensor_tensor(assq, assq, gate_pow, ALU.pow), (m,))
        HA4 = HA.rearrange("p t (h e) -> p (t h) e", h=AH)
        tt(HA4, HA4, assq.unsqueeze(2).broadcast_to([P, NT * AH, 2 * ADH]), ALU.mult, after=(m,))

        ha_done = {}

        def za_evac(n):
            def evac(t, view, m):
                s, i = scratch()
                e = act(s, view, ACT.Silu, after=(m, ta_free[i]))
                ha = HA[:, t, n * W:(n + 1) * W]
                ta_free[i] = ha_done[n] = tt(ha, ha, s, ALU.mult, after=(e,))
                return e
            return evac

        natural(hT, KD, dram["w_in"], ZM + 3 * W, h_ok, z_evac(3))
        head_flip(1)
        natural(hT, KD, dram["w_in"], ZA, h_ok, za_evac(0))
        head_flip(2)
        natural(hT, KD, dram["w_in"], ZA + W, h_ok, za_evac(1))
        hmt_ok = head_flip(3)
        YM, YA = at(16, NT, D), at(24, NT, D)
        ag = small(KD)
        m = ts(ag, part(cols, COLS, "anorm_g"), 1.0 - LAM_INIT, None, ALU.mult)
        HAT = at(48, KD, T)
        A.wait(m)
        y_ready = {}

        def y_evac(dst, key, n):
            def evac(t, view, m):
                y_ready[key] = acopy(dst[:, t, n * W:(n + 1) * W], view, after=(m,))
                return y_ready[key]
            return evac

        natural(lambda k, t: HMT[:, k, t * P:(t + 1) * P], 2 * KD, dram["w_proj_m"], 0, hmt_ok, y_evac(YM, "m", 0))
        hat_ok = flip_tokens(HAT, HA, KD, ha_done[1], scaled(HAT, ag))
        natural(lambda k, t: HMT[:, k, t * P:(t + 1) * P], 2 * KD, dram["w_proj_m"], W, hmt_ok, y_evac(YM, "m", 1))
        GATE, FG, G1, SH2, SC2, GG2 = (at(kb, D) for kb in (102, 106, 110, 114, 118, 122))
        rows_free = (attn_pe, now(A), now(V))
        late_in = load(late, dram["late"], after=rows_free)
        rows_in = [load(dst, dram["mods"][i * D:(i + 1) * D].partition_broadcast(P), after=(*rows_free, *mods_in))
                   for i, dst in enumerate((GATE, G1, SH2, SC2, GG2))]
        gate_ok, rows_ok = rows_in[0], rows_in[-1]
        fg_in = load(FG, row("final_g").partition_broadcast(P), after=rows_free)
        CX, CT = at(32, NT, D), at(40, KD, T)
        cx_in = load(CX, dram["ctx"].rearrange("(t p) d -> p t d", p=P), after=(now(PE),))
        for n in range(2):
            natural(lambda k, t: HAT[:, k, t * P:(t + 1) * P], KD, dram["w_proj_a"], n * W, hat_ok,
                    y_evac(YA, "a", n))
        ct_n = row_rms(CX, CX, at(86, NT, D), after=(cx_in,))

        def mix_evac(n, y, first):
            def evac(t, view, m):
                s, i = scratch()
                e = act(s, view, ACT.Sigmoid, after=(m, ta_free[i]))
                yy, ym = y[:, t, n * W:(n + 1) * W], YM[:, t, n * W:(n + 1) * W]
                if first:
                    ta_free[i] = tt(yy, yy, s, ALU.mult, after=(e, y_ready["m"], y_ready["a"]))
                else:
                    tt(s, yy, s, ALU.mult, after=(e, y_ready["m"], y_ready["a"]))
                    ta_free[i] = tt(ym, ym, s, ALU.add)
                return e
            return evac

        for n in range(2):
            natural(hT, KD, dram["w_in"], GM + n * W, h_ok, mix_evac(n, YM, True))
        ct_ok = flip_tokens(CT, CX, KD, ct_n, modulate(CT, shc, gsc, modc_ok))
        for n in range(2):
            natural(hT, KD, dram["w_in"], GA + n * W, h_ok, mix_evac(n, YA, False))
        y_ok = now(V)
        KC, VC = at(94, NT, W), at(98, NT, W)
        cT = lambda k, t: CT[:, k, t * P:(t + 1) * P]

        def plain(dst):
            def evac(t, view, m):
                return acopy(dst[:, t, :], view, after=(m,))
            return evac

        natural(cT, KD, dram["w_in_2"], K2, ct_ok, plain(KC))
        kc_ok = now(A)
        YT = at(48, KD, T)
        yt_ok = flip_tokens(YT, YM, KD, y_ok, lambda k, view, m: acopy(YT[:, k, :], view, after=(m,)))

        X2N, JUNK, x1, x2n = at(16, NT, D), at(24, NT, D), [], []
        xsq = small(NT, 2)

        def residual_evac(t, n, view, m):
            s, i = scratch()
            f = tt(s, view, GATE[:, n * W:(n + 1) * W], ALU.mult, after=(m, gate_ok, ta_free[i]))
            xx = X[:, t, n * W:(n + 1) * W]
            ta_free[i] = tt(xx, xx, s, ALU.add)
            return f

        def normed(t):
            x, v = X[:, t, :], xsq[:, t, :]
            m = act(JUNK[:, t, :], x, ACT.Square, accum=v[:, 0:1], after=(now(V),))
            m = column_rstd(v[:, 0:1], D, (m,))
            m = stt(x, x, v[:, 0:1], FG, ALU.mult, ALU.mult, after=(m, fg_in))
            x1.append(m)
            m = act(JUNK[:, t, :], x, ACT.Square, accum=v[:, 1:2], after=(m,))
            m = column_rstd(v[:, 1:2], D, (m,))
            x2n.append(ts(X2N[:, t, :], x, v[:, 1:2], None, ALU.mult, after=(m,)))

        by_tile(lambda k, t: YT[:, k, t * P:(t + 1) * P], dram["w_out"], [(0, yt_ok), (1, yt_ok)], residual_evac, normed)
        natural(cT, KD, dram["w_in_2"], V2, ct_ok, plain(VC))
        vc_ok = now(A)
        if tap:
            tap_sem = load(dram["tap1"].rearrange("(t p) d -> p t d", p=P), X, after=x1)

        lgs, lt1, lt2 = small(2 * RH), small(2 * RH), small(2 * RH)
        V.wait(lg_in)
        lg_ok = log_sigmoid(lgs, lg, lt1, lt2)

        HT2 = at(8, KD, T)
        xn = x2n[-1]
        h2_ok = flip_tokens(HT2, X2N, KD, xn, modulate(HT2, sh2, gs2, modc_ok))
        h2T = lambda k, t: HT2[:, k, t * P:(t + 1) * P]
        QX, KX, VX, GX = (at(kb, NT, W) for kb in (16, 20, 24, 28))
        natural(h2T, KD, dram["w_in_2"], Q2, h2_ok, plain(QX))
        q_ok = now(A)

        def rotary(x, c, s, scratch, after):
            x4 = x.rearrange("p t (h e) -> p t h e", h=RH)
            a, b = x4[:, :, :, 0:64], x4[:, :, :, 64:128]
            bc = [part(late, LATE, n_).rearrange("p (t e) -> p t e", t=NT).unsqueeze(2).broadcast_to([P, NT, RH, 64])
                  for n_ in (c, s)]
            u, v, w_, z = (scratch[:, i, :].rearrange("p (t h e) -> p t h e", t=NT, h=RH) for i in range(4))
            tt(u, a, bc[0], ALU.mult, after=after)
            tt(v, b, bc[1], ALU.mult)
            tt(w_, a, bc[1], ALU.mult)
            tt(z, b, bc[0], ALU.mult)
            tt(a, u, v, ALU.subtract)
            return tt(b, w_, z, ALU.add)

        RS = at(128, 4, W)
        rk = rotary(KC, "cosc", "sinc", RS, (kc_ok, late_in, *ta_free[0:3]))
        wfb = small(2, NT, RH)
        wn = part(late, LATE, "wn").rearrange("p (a t) -> p a t", a=2)
        for d in range(2):
            for t in range(NT):
                m = ts(wfb[:, d, t, :], lgs[:, d * RH:(d + 1) * RH], wn[:, d, t:t + 1], None, ALU.mult)
        m = act(wfb, wfb, ACT.Exp, after=(m,))
        wfb = wfb
        m = ts(wfb, wfb, RD ** -0.5, None, ALU.mult, after=(m,))
        KF = [at(128 + 4 * d, NT, W) for d in range(2)]
        SF = at(56, 2, RH * RD)
        kc4 = KC.rearrange("p t (h e) -> p t h e", h=RH)
        for d in range(2):
            m = tt(KF[d].rearrange("p t (h e) -> p t h e", h=RH), kc4,
                   wfb[:, d, :, :].unsqueeze(3).broadcast_to([P, NT, RH, RD]), ALU.mult)
            PE.wait(bank_free[4 + d], m, vc_ok)
            for h in range(RH):
                for t in range(NT):
                    m = mm(ps[:, 4 + d, h * RD:(h + 1) * RD], KF[d][:, t, h * RD:(h + 1) * RD],
                           VC[:, t, h * RD:(h + 1) * RD], t == 0, t == NT - 1, signal=(t == NT - 1))
            states_pe = m
            state_ok = bank_free[4 + d] = acopy(SF[:, d, :], ps[:, 4 + d, :], after=(m,))
        WT = at(32, RH, NT * T)
        ahead, behind = part(late, LATE, "ahead"), part(late, LATE, "behind")
        XI = at(76, 2, RH, T)
        for h in range(RH):
            ts(WT[:, h, :], ahead, lgs[:, h:h + 1], None, ALU.mult, after=(ct_ok,))
            m = stt(WT[:, h, :], behind, lgs[:, RH + h:RH + h + 1], WT[:, h, :], ALU.mult, ALU.add)
            act(WT[:, h, :], WT[:, h, :], ACT.Exp, after=(m,))
            act(XI[:, 0, h, :], part(late, LATE, "n1"), ACT.Exp, scale=lgs[:, h:h + 1])
            xi_ok = act(XI[:, 1, h, :], part(late, LATE, "n2"), ACT.Exp, scale=lgs[:, RH + h:RH + h + 1])

        natural(h2T, KD, dram["w_in_2"], K2, h2_ok, plain(KX))
        k_ok = now(A)
        natural(h2T, KD, dram["w_in_2"], V2, h2_ok, plain(VX))
        vx_ok = now(A)
        rq = rotary(QX, "cosx", "sinx", RS, (q_ok, states_pe))
        rk = rotary(KX, "cosx", "sinx", RS, (k_ok,))
        QXT, KXT = at(94, RH, T), at(98, RH, T)
        flip_tokens(QXT, QX, RH, rq, lambda k, view, m: acopy(QXT[:, k, :], view, after=(m,)))
        qkx_ok = flip_tokens(KXT, KX, RH, rk,
                             lambda k, view, m: act(KXT[:, k, :], view, ACT.Copy, scale=RD ** -0.5, after=(m,)))

        def g_evac(t, view, m):
            return act(GX[:, t, :], view, ACT.Silu, after=(m,))

        QS = at(102, 2, RH * T)
        for d in range(2):
            qs_ok = tt(QS[:, d, :].rearrange("p (h t) -> p h t", h=RH), QXT, XI[:, d, :, :], ALU.mult,
                       after=(qkx_ok, xi_ok))

        RP = [at(128 + 2 * i, NT, T) for i in range(2)]
        RY = at(132, NT, W)

        def ret_scores(h):
            b = 4 + h % 2
            PE.wait(bank_free[b], qkx_ok)
            for mt in range(NT):
                m = mm(ps[:, b, mt * T:(mt + 1) * T], KXT[:, h, mt * P:(mt + 1) * P], QXT[:, h, :], True, True,
                       signal=True)
            bank_free[b] = tt(RP[h % 2], ps[:, b, :].rearrange("p (a b) -> p a b", a=NT),
                              WT[:, h, :].rearrange("p (a b) -> p a b", a=NT), ALU.mult, after=(m, state_ok, xi_ok))
            return bank_free[b]

        def ret_values(h, ready):
            PE.wait(ready, qs_ok, state_ok, vx_ok)
            if h == 0:
                PE.wait(bank_free[6], bank_free[7])
            hs = slice(h * RD, (h + 1) * RD)
            for nt in range(NT):
                o = ps[:, 6 + nt, hs]
                ns = slice(nt * P, (nt + 1) * P)
                for mt in range(NT):
                    mm(o, RP[h % 2][:, mt, ns], VX[:, mt, hs], mt == 0, False)
                for d in range(2):
                    m = mm(o, QS[:, d, h * T + nt * P:h * T + (nt + 1) * P], SF[:, d, hs], False, d == 1,
                           signal=(d == 1))
            return m

        MIXT = at(48, KD, T)
        CVC, CVU = at(86, RH, T), at(40, RH, T)
        c_ok = {}

        def hold(dst, key):
            def evac(i, view, m):
                c_ok[key] = acopy(dst[:, i, :], view, after=(m,))
                return c_ok[key]
            return evac

        r = ret_scores(0)
        natural(h2T, KD, dram["w_in_2"], G2, h2_ok, g_evac)
        ret_values(0, r)
        r = ret_scores(1)
        transposed(HT2, dram["w_in_2"], CC2, h2_ok, hold(CVC, "c"))
        ret_values(1, r)
        r = ret_scores(2)

        def u_evac(i, view, m):
            return tt(CVU[:, i, :], view, CVC[:, i, :], ALU.mult, after=(m, c_ok["c"]))

        transposed(HT2, dram["w_in_2"], CX2, h2_ok, u_evac)
        ret_values(2, r)
        r = ret_scores(3)
        w2, b2 = part(cols, COLS, "conv_w_2").rearrange("p (j c) -> p j c", j=3), part(cols, COLS, "conv_b_2")
        for i in range(4):
            o = MIXT[:, i, :].rearrange("p (r w) -> p r w", w=GRID_W)
            u = CVU[:, i, :].rearrange("p (r w) -> p r w", w=GRID_W)
            ts(MIXT[:, i, :], CVU[:, i, :], w2[:, 1, i:i + 1], b2[:, i:i + 1], ALU.mult, ALU.add)
            stt(o[:, :, 1:], u[:, :, :-1], w2[:, 0, i:i + 1], o[:, :, 1:], ALU.mult, ALU.add)
            conv2 = stt(o[:, :, :-1], u[:, :, 1:], w2[:, 2, i:i + 1], o[:, :, :-1], ALU.mult, ALU.add)
        m = ret_values(3, r)
        rg = at(126, W)
        rg_in = load(rg, row("ret_norm_g").partition_broadcast(P), after=(qkx_ok,))
        for t in range(NT):
            ry = bank_free[6 + t] = acopy(RY[:, t, :], ps[:, 6 + t, :], after=(m,))
        RY4 = RY.rearrange("p t (h e) -> p (t h) e", h=RH)
        gmean = small(NT * RH)
        reduce(gmean, RY4, ALU.add, after=(ry,))
        ts(gmean, gmean, 1.0 / RD, None, ALU.mult)
        tt(RY4, RY4, gmean.unsqueeze(2).broadcast_to([P, NT * RH, RD]), ALU.subtract)
        sq4 = at(128, NT * RH, RD)
        tt(sq4, RY4, RY4, ALU.mult)
        m = reduce(ssq[:, 0:NT * RH], sq4, ALU.add)
        r = rstd(NT * RH, RD)
        tt(RY4, RY4, ssq[:, 0:NT * RH].unsqueeze(2).broadcast_to([P, NT * RH, RD]), ALU.mult, after=(r,))
        tt(RY, RY, rg.unsqueeze(1).broadcast_to([P, NT, W]), ALU.mult, after=(rg_in,))
        m = tt(RY, RY, GX, ALU.mult)
        ret_ok, ret_pe = m, now(PE)

        def b_evac(i, view, m):
            return tt(MIXT[:, i, :], MIXT[:, i, :], view, ALU.mult, after=(m,))

        transposed(HT2, dram["w_in_2"], CB2, h2_ok, b_evac)
        conv_done = now(V)
        ACC = at(32, NT, D)
        acc0 = G.do(lambda e: e.memset(ACC, 0.0), (ret_ok, ret_pe))
        mix_ok = flip_tokens(MIXT, RY, RH, ret_ok, lambda k, view, m: acopy(MIXT[:, RH + k, :], view, after=(m,)))

        gst = [at(kb, D) for kb in (68, 86, 90)]
        for i, (name, dst) in enumerate((("post_mix_g", G1), ("pre_ffn_g", SC2), ("post_ffn_g", GG2))):
            gin = load(gst[i], row(name).partition_broadcast(P), after=(conv_done,))
            if i == 1:
                stt(dst, dst, 1.0, gst[i], ALU.add, ALU.mult, after=(gin, rows_ok))
            else:
                tt(dst, dst, gst[i], ALU.mult, after=(gin, rows_ok))

        M = at(16, NT, D)
        msq = small(NT, 2)

        H2, H2T = at(24, NT, D), at(8, KD, T)
        x2, h2 = [], []
        hsq = small(NT)
        aff, rmax = small(NT, NE), small(NT)

        def m_evac(t, n, view, m):
            act(TA[:, t, :], view, ACT.Square, accum=msq[:, t, n:n + 1], after=(m, ret_ok))
            return acopy(M[:, t, n * W:(n + 1) * W], view)

        def second_norms(t):
            x, v, h = X[:, t, :], msq[:, t, 0:1], hsq[:, t:t + 1]
            tt(v, v, msq[:, t, 1:2], ALU.add, after=(now(A),))
            m = column_rstd(v, D)
            stt(M[:, t, :], M[:, t, :], v, G1, ALU.mult, ALU.mult, after=(m,))
            x2.append(tt(x, x, M[:, t, :], ALU.add))
            m = act(H2[:, t, :], x, ACT.Square, accum=h, after=(x2[t],))
            m = column_rstd(h, D, (m,))
            stt(H2[:, t, :], x, h, SC2, ALU.mult, ALU.mult, after=(m,))
            h2.append(tt(H2[:, t, :], H2[:, t, :], SH2, ALU.add))

        def route(t):
            for g in range(2):
                b = 6 + g
                PE.wait(bank_free[b], h2[t])
                for k in range(4):
                    m = flip(ps[:, b, k * P:(k + 1) * P], H2[:, t, (4 * g + k) * P:(4 * g + k + 1) * P], signal=(k == 3))
                bank_free[b] = acopy(H2T[:, 4 * g:4 * g + 4, t * P:(t + 1) * P],
                                     ps[:, b, :].rearrange("p (k n) -> p k n", k=4), after=(m,))
            PE.wait(bank_free[4 + t], wr_in, bank_free[6], bank_free[7])
            for k in range(KD):
                m = mm(ps[:, 4 + t, 0:NE], H2T[:, k, t * P:(t + 1) * P], wr[:, k, :], k == 0, k == KD - 1,
                       signal=(k == KD - 1))
            a_, r_ = aff[:, t, :], rmax[:, t:t + 1]
            bank_free[4 + t] = tt(a_, ps[:, 4 + t, 0:NE], brt, ALU.add, after=(m, brt_in))
            reduce(r_, a_, ALU.max)
            m = ts(a_, a_, r_, None, ALU.subtract)
            m = act(a_, a_, ACT.Exp, accum=r_, after=(m,))
            recip(r_, r_, after=(m,))
            return ts(a_, a_, r_, None, ALU.mult)

        A.wait(mix_ok)
        by_tile(lambda k, t: MIXT[:, k, t * P:(t + 1) * P], dram["w_out_2"], [(1, mix_ok), (0, conv_done)],
                m_evac, second_norms)
        if tap:
            load(dram["tap2"].rearrange("(t p) d -> p t d", p=P), X, after=x2)
        routed = [route(t) for t in range(NT)]
        PE.wait(bank_free[5], *routed)
        for t in range(NT):
            m = flip(ps[0:NE, 5, t * P:(t + 1) * P], aff[:, t, :], signal=True)
        affT, one_row = at(44, T)[0:NE, :], at(45, T)[0:NE, :]
        bank_free[5] = aff_ok = vcopy(affT, ps[0:NE, 5, 0:T], after=(m,))
        before = part(late, LATE, "before").rearrange("p (t s) -> p t s", t=NT)

        ONE = small(NT, CAP)
        Z = at(48, NT, P)
        GT = at(60, 2, T)
        XS, XT = at(51, T), at(52, 2, P)
        SG, HD, HTT, YS = at(53, W), at(55, W), at(57, 4, P), at(46, W)
        gz = G.do(lambda e: e.memset(GT, 0.0), (ret_pe,))
        own, over, same, rank = small(NT), small(NT), small(NT), small(NT)
        junk = at(128, 4, T)
        onesr = at(132, P)
        ones_ok = G.do(lambda e: e.memset(onesr, 1.0), (m, mix_ok))
        RING2 = 12
        extra = [at(74 + 8 * i, SLOT) for i in range(RING2 - RING)]
        order = [(chunks[0] + c) % RING for c in range(RING)] + list(range(RING, RING2))
        landed += [sem(f"landed{i}") for i in range(RING, RING2)]
        landed_before = [chunks[0] // RING + (1 if s < chunks[0] % RING else 0) for s in range(RING)]
        landed_before += [0] * (RING2 - RING)
        NCH = 3 * KD
        wg, wu, wd = dram["w_gate"], dram["w_up"], dram["w_down"]
        wd_chunks = wd.rearrange("e (c k p) n -> (e c) p k n", k=2, p=P)
        p_use = sem("p_use")

        def chunk_src(e_, c):
            if c < 2 * KD:
                w_ = wg if c < KD else wu
                return w_[e_, (c % KD) * P:(c % KD + 1) * P, :]
            return wd[e_, (c - 2 * KD) * 2 * P:(c - 2 * KD + 1) * 2 * P, :].rearrange("(k p) n -> p k n", p=P)

        def chunk_slot(c):
            s = order[c % RING2]
            v = ring[:, s, :] if s < RING else extra[s - RING]
            return s, (v if c < 2 * KD else v.rearrange("p (k n) -> p k n", k=2))

        def fetch(e, e_, c):
            s, dst = chunk_slot(c)
            e.dma_start(dst, chunk_src(e_, c)).then_inc(landed[s], 16)

        for c in range(RING2):
            s, _ = chunk_slot(c)
            SP.wait(*((freed[s],) if s < RING else (ret_pe, ret_ok, conv_done, *x2)))
            SP.items.append(lambda e, c=c: fetch(e, 0, c))

        def sp_experts(e):
            with e.Fori(0, NE - 1) as i:
                for c in range(NCH):
                    nxt = c + RING2
                    src = chunk_src_dyn(i, nxt) if nxt < NCH else chunk_src_dyn(i + 1, nxt - NCH)
                    s, dst = chunk_slot(nxt % NCH)
                    e.wait_ge(p_use, i * NCH + (c + 1))
                    e.dma_start(dst, src).then_inc(landed[s], 16)
            for c in range(NCH - RING2):
                e.wait_ge(p_use, (NE - 1) * NCH + c + 1)
                fetch(e, NE - 1, c + RING2)

        def chunk_src_dyn(i, c):
            if c < 2 * KD:
                w_ = wg if c < KD else wu
                return w_[bass.ds(i, 1), (c % KD) * P:(c % KD + 1) * P, :].rearrange("o p n -> p (o n)")
            return wd_chunks[bass.ds(i * KD + (c - 2 * KD), 1), :, :, :].rearrange("o p k n -> p (o k) n")

        SP.items.append(sp_experts)

        names = ("v_sel", "p_row", "v_r0", "v_r1", "v_r2", "v_one", "v_gt", "v_hd", "p_gath", "p_xt", "p_ht", "p_dn", "a_xs", "a_xt",
                 "a_sg", "a_ht", "a_y", "v_acc0", "v_acc1", "p_sc0", "p_sc1")
        ev = {n: sem(n) for n in names}

        def prime(e, who):
            for n in names:
                if n[0] == who:
                    e.sem_inc(ev[n], 1)

        SLOTS_BACK = NCH // RING2

        def pe_experts(e):
            prime(e, "p")
            with e.Fori(0, NE) as i:
                prev, this = i + 1, i + 2
                e.wait_ge(ev["v_sel"], this)
                e.wait_ge(ev["v_gt"], prev)
                e.matmul(ps[:, 1, T:2 * T], onesr[0:NE, :], one_row, start=True, stop=True,
                         skip_group_check=True).then_inc(ev["p_row"], 1)
                e.wait_ge(ev["v_one"], this)
                e.wait_ge(ev["a_xt"], prev)
                for t in range(NT):
                    for j in range(4):
                        e.matmul(ps[32 * j:32 * j + 32, 0, 0:T], ONE[:, t, :], H2[:, t, j * T:(j + 1) * T],
                                 start=(t == 0), stop=(t == NT - 1), skip_group_check=True)
                for t in range(NT):
                    ins = e.transpose(ps[:, 1, t * P:(t + 1) * P], Z[:, t, :], ident)
                ins.then_inc(ev["p_gath"], 1)
                e.wait_ge(ev["a_xs"], this)
                for b in range(2):
                    ins = e.transpose(ps[:, 0, T + b * P:T + (b + 1) * P], XS[:, b * P:(b + 1) * P], ident)
                ins.then_inc(ev["p_xt"], 1)
                e.wait_ge(ev["a_xt"], this)
                for c in range(2 * KD):
                    k = c % KD
                    if c == 0:
                        e.wait_ge(ev["a_sg"], prev)
                    if c == KD:
                        e.wait_ge(ev["v_hd"], prev)
                    s, slot = chunk_slot(c)
                    e.wait_ge(landed[s], i * (16 * SLOTS_BACK) + 16 * (landed_before[s] + c // RING2 + 1))
                    for n in range(4):
                        ins = e.matmul(ps[32 * n:32 * n + 32, 2 + c // KD, :],
                                       XT[:, k % 2, 32 * (k // 2):32 * (k // 2) + 32], slot[:, n * W:(n + 1) * W],
                                       start=(k == 0), stop=(k == KD - 1), skip_group_check=True)
                    ins.then_inc(p_use, 1)
                e.wait_ge(ev["v_hd"], this)
                e.wait_ge(ev["a_ht"], prev)
                for b in range(4):
                    ins = e.transpose(ps[:, 4, b * P:(b + 1) * P], HD[:, b * P:(b + 1) * P], ident)
                ins.then_inc(ev["p_ht"], 1)
                e.wait_ge(ev["a_ht"], this)
                e.wait_ge(ev["a_y"], prev)
                for c in range(2 * KD, NCH):
                    s, slot = chunk_slot(c)
                    e.wait_ge(landed[s], i * (16 * SLOTS_BACK) + 16 * (landed_before[s] + c // RING2 + 1))
                    for kk in range(2):
                        f = 2 * (c - 2 * KD) + kk
                        for nd in range(2):
                            g = 2 * nd + kk
                            ins = e.matmul(ps[32 * g:32 * g + 32, 5, :],
                                           HTT[:, f % 4, 32 * (f // 4):32 * (f // 4) + 32],
                                           slot[:, kk, nd * W:(nd + 1) * W],
                                           start=(c == 2 * KD), stop=(c == NCH - 1), skip_group_check=True)
                    ins.then_inc(p_use, 1)
                e.wait_ge(ev["a_y"], this)
                e.wait_ge(ev["v_gt"], this)
                for t in range(NT):
                    e.wait_ge(ev["v_acc0"], prev) if t == 0 else e.wait_ge(ev["v_acc0"], this)
                    for nd in range(2):
                        ins = e.matmul(ps[:, 6 + nd, :], GT[:, nd, t * P:(t + 1) * P], YS[:, :],
                                       start=True, stop=True, skip_group_check=True)
                    ins.then_inc(ev[f"p_sc{t}"], 1)

        def act_experts(e):
            prime(e, "a")
            with e.Fori(0, NE) as i:
                prev, this = i + 1, i + 2
                e.wait_ge(ev["p_gath"], this)
                e.wait_ge(ev["p_xt"], prev)
                e.activation(XS, ps[:, 0, 0:T], ACT.Copy).then_inc(ev["a_xs"], 1)
                e.wait_ge(ev["p_xt"], this)
                e.activation(XT.rearrange("p a b -> p (a b)"), ps[:, 0, T:2 * T], ACT.Copy).then_inc(ev["a_xt"], 1)
                e.wait_ge(p_use, i * NCH + KD)
                e.wait_ge(ev["v_hd"], prev)
                e.activation(SG, ps[:, 2, :], ACT.Silu).then_inc(ev["a_sg"], 1)
                e.wait_ge(ev["p_ht"], this)
                e.activation(HTT.rearrange("p a b -> p (a b)"), ps[:, 4, :], ACT.Copy).then_inc(ev["a_ht"], 1)
                e.wait_ge(p_use, i * NCH + NCH)
                e.wait_ge(ev["p_sc1"], prev)
                e.activation(YS, ps[:, 5, :], ACT.Copy).then_inc(ev["a_y"], 1)

        def dve_experts(e):
            prime(e, "v")
            with e.Fori(0, NE) as i:
                prev, this = i + 1, i + 2
                e.wait_ge(ev["p_row"], prev)
                e.tensor_scalar(one_row, affT, ident[0:NE, bass.ds(i, 1)], None, ALU.mult).then_inc(ev["v_sel"], 1)
                e.wait_ge(ev["p_row"], this)
                e.wait_ge(ev["p_gath"], prev)
                row_ = ps[:, 1, T:2 * T]
                for t in range(NT):
                    ins = e.scalar_tensor_tensor(out=junk[:, t, 0:P], in0=row_[:, t * P:(t + 1) * P], scalar=1.0,
                                                 in1=ident, op0=ALU.mult, op1=ALU.mult, accum_out=own[:, t:t + 1])
                ins.then_inc(ev["v_r0"], 1)
                e.wait_ge(ev["v_r0"], this)
                for t in range(NT):
                    e.tensor_scalar(junk[:, t, :], row_, own[:, t:t + 1], 0.0, ALU.is_gt, ALU.add,
                                    accum_out=over[:, t:t + 1])
                    ins = e.scalar_tensor_tensor(out=junk[:, 2 + t, :], in0=row_, scalar=own[:, t:t + 1],
                                                 in1=before[:, t, :], op0=ALU.is_equal, op1=ALU.mult,
                                                 accum_out=same[:, t:t + 1])
                ins.then_inc(ev["v_r1"], 1)
                e.wait_ge(ev["v_r1"], this)
                e.tensor_tensor(rank, over, same, ALU.add).then_inc(ev["v_r2"], 1)
                e.wait_ge(ev["v_r2"], this)
                for t in range(NT):
                    e.tensor_scalar(ONE[:, t, :], iota[:, 0:CAP], rank[:, t:t + 1], None, ALU.is_equal)
                    ins = e.tensor_scalar(Z[:, t, :], iota, rank[:, t:t + 1], own[:, t:t + 1], ALU.is_equal, ALU.mult)
                ins.then_inc(ev["v_one"], 1)
                e.wait_ge(ev["p_gath"], this)
                e.wait_ge(ev["p_sc1"], prev)
                e.tensor_copy(GT[0:64, 0, :], ps[0:64, 1, 0:T])
                e.tensor_copy(GT[64:128, 1, :], ps[64:128, 1, 0:T]).then_inc(ev["v_gt"], 1)
                e.wait_ge(ev["a_sg"], this)
                e.wait_ge(p_use, i * NCH + 2 * KD)
                e.wait_ge(ev["p_ht"], prev)
                e.tensor_tensor(HD, SG, ps[:, 3, :], ALU.mult).then_inc(ev["v_hd"], 1)
                for t in range(NT):
                    e.wait_ge(ev[f"p_sc{t}"], this)
                    e.wait_ge(ev[f"v_acc{t}"], prev)
                    a_ = ACC[:, t, :].rearrange("p (n w) -> p n w", n=2)
                    e.tensor_tensor(a_, a_, ps[:, 6:8, :], ALU.add).then_inc(ev[f"v_acc{t}"], 1)

        for q in (PE, A, V):
            q.wait(aff_ok, acc0, gz, ones_ok, now(A), now(PE))
        PE.items.append(pe_experts)
        A.items.append(act_experts)
        V.items.append(dve_experts)
        acc_done = (ev["v_acc1"], NE + 1)
        G.wait(acc_done)
        for q in (A, V):
            q.wait(acc_done, (ev["v_acc0"], NE + 1))

        OUTT = at(16, NT, D)
        if tap:
            load(dram["tap3"].rearrange("(t p) d -> p t d", p=P), ACC, after=(acc_done,))
        stores = []
        osq = small(NT)
        for t in range(NT):
            m = act(OUTT[:, t, :], ACC[:, t, :], ACT.Square, accum=osq[:, t:t + 1])
            m = column_rstd(osq[:, t:t + 1], D, (m,))
            stt(OUTT[:, t, :], ACC[:, t, :], osq[:, t:t + 1], GG2, ALU.mult, ALU.mult, after=(m,))
            m = tt(OUTT[:, t, :], OUTT[:, t, :], X[:, t, :], ALU.add)
            stores.append(load(out[t * P:(t + 1) * P, :], OUTT[:, t, :], after=(m,)))
        SP.wait(*stores)

        block = ctx.enter_context(nc.Block())

        @block.sync
        def _(e):
            for item in SP.items:
                item(e)

        @block.tensor
        def _(e):
            for item in PE.items:
                item(e)

        @block.vector
        def _(e):
            for item in V.items:
                item(e)

        @block.scalar
        def _(e):
            for item in A.items:
                item(e)

        @block.gpsimd
        def _(e):
            for item in G.items:
                item(e)


def arrange(inputs):
    a = {k: np.asarray(v) for k, v in inputs.items()}

    def col(v):
        v = np.asarray(v)
        v = v.reshape(-1, P)
        return v.T

    pack = {
        "c": col(a["c"]), "c_2": col(a["c_2"]), "c_ctx": col(a["c_ctx_2"]), "conv_w": col(a["conv_w"]),
        "conv_b": col(a["conv_b"]), "norm_g": col(a["norm_g"]), "mnorm_g": col(a["mnorm_g"]),
        "anorm_g": col(a["anorm_g"]), "pre_mix_g": col(a["pre_mix_g_2"]), "conv_w_2": col(a["conv_w_2"]),
        "conv_b_2": col(a["conv_b_2"]),
    }
    cols = np.zeros((P, COLS["all"][1]), np.float32)
    for name, v in pack.items():
        s, n = COLS[name]
        cols[:, s:s + n] = v
    s, n = COLS["b_if"]
    cols[0:MH, s:s + 2] = a["b_if"].reshape(2, MH).T
    rows = np.concatenate([a[n].reshape(-1) for n in (
        "b_ada", "b_ada_2", "final_g", "post_mix_g_2", "pre_ffn_g_2", "post_ffn_g_2", "ret_norm_g_2",
        "b_router_2", "ret_decay_logit_2", "lam_q1", "lam_k1", "lam_q2", "lam_k2")])
    big = {
        "x": a["x"][0], "ctx": a["ctx_2"][0], "w_ada": a["w_ada"][0], "w_in": a["w_in"][0],
        "w_proj_m": a["w_proj_m"][0], "w_proj_a": a["w_proj_a"][0], "w_out": a["w_out"][0],
        "rel_bias": a["rel_bias"], "w_ada_2": a["w_ada_2"][0], "w_in_2": a["w_in_2"][0],
        "w_out_2": a["w_out_2"][0], "w_router": a["w_router_2"][0], "w_gate": a["w_gate_2"][0],
        "w_up": a["w_up_2"][0], "w_down": a["w_down_2"][0], "rows": rows, "cols": cols,
    }
    return {**big, **constants()}


def program(nc, arrays, tap=None):
    dram = {n: nc.dram_tensor(f"in_{n}", v.shape, F32, kind="ExternalInput").ap() for n, v in arrays.items()}
    dram["toeplitz"] = nc.dram_tensor("toeplitz", (AH * 2 * T,), F32, kind="Internal").ap()
    dram["mods"] = nc.dram_tensor("mods", (5 * D,), F32, kind="Internal").ap()
    for n in (tap or ()):
        dram[n] = nc.dram_tensor(n, (T, D), F32, kind="ExternalOutput").ap()
    out = nc.dram_tensor("out", (T, D), F32, kind="ExternalOutput").ap()
    build(nc, dram, out, tap)


def kernel(**inputs):
    import concourse.bacc as _bacc
    from concourse.bass_utils import run_bass_kernel_spmd as _run

    arrays = {n: np.ascontiguousarray(v) for n, v in arrange(inputs).items()}
    nc = _bacc.Bacc("TRN2", target_bir_lowering=False, num_devices=1)
    program(nc, arrays)
    r = _run(nc, [{f"in_{n}": v for n, v in arrays.items()}], core_ids=[0])
    return r.results[0]["out"].reshape(1, T, D)
```

```python
from contextlib import ExitStack
import math

import numpy as np
import concourse.bass as bass
from concourse import mybir

F32 = mybir.dt.float32
F32R = mybir.dt.float32r
ALU = mybir.AluOpType
ACT = mybir.ActivationFunctionType
AX = mybir.AxisListType.X

P = 128
T = 256
NT = T // P
D = 1024
KD = D // P
W = 512
MH, MDV, MDK = 4, 512, 256
AH, ADH = 8, 64
RH, RD = 4, 128
NBUCKET, MAXDIST = 32, 128
NE, CAP, DE = 16, 32, 2048
EPS = 1e-6
NEG = -1e30
LAM_INIT = 0.8 - 0.6 * math.exp(0.0)
GRID_W = 64
SLOT = 2048
RING = 4
HALF = SLOT // 2
NHALF = 3

SPLITS = (1024, 1024, 2048, 2048, 2048, MH, MH, 1024, 1024, 1024, 1024, 1024, 1024)
QM, KM, VM, OM, ZM, IM, FM, QA, KA, VA, ZA, GM, GA = (sum(SPLITS[:i]) for i in range(13))
CB2, CC2, CX2, Q2, K2, V2, G2 = (W * i for i in range(7))

ROWS, COLS, CONST, EARLY, LATE = {}, {}, {}, {}, {}


def _lay(table, *items):
    at = 0
    for name, n in items:
        table[name] = (at, n)
        at += n
    table["all"] = (0, at)


_lay(ROWS, ("b_ada", 3 * D), ("b_ada_2", 6 * D), ("final_g", D), ("post_mix_g", D), ("pre_ffn_g", D),
     ("post_ffn_g", D), ("ret_norm_g", W), ("b_router", NE), ("decay", 2 * RH), ("lam", 4 * ADH))
_lay(COLS, ("c", KD), ("c_2", KD), ("c_ctx", KD), ("conv_w", 4 * 16), ("conv_b", 16), ("norm_g", KD),
     ("mnorm_g", 16), ("anorm_g", KD), ("pre_mix_g", KD), ("conv_w_2", 3 * 4), ("conv_b_2", 4), ("b_if", 2))
_lay(CONST, ("ident", P), ("iota", P), ("causal", P))
_lay(EARLY, ("selh", MH * P), ("onehot", 2 * T), ("future", 2 * T), ("mirror", P))
_lay(LATE, ("before", NT * T), ("ahead", NT * T), ("behind", NT * T), ("n1", T), ("n2", T),
     ("cosx", NT * 64), ("sinx", NT * 64), ("cosc", NT * 64), ("sinc", NT * 64), ("wn", 2 * NT))


def constants():
    one = np.zeros((P, CONST["all"][1]), np.float32)

    def put(a, table, name, v):
        s, n = table[name]
        a[:v.shape[0], s:s + n] = v.reshape(v.shape[0], n)

    p, j = np.arange(P)[:, None], np.arange(P)[None, :]
    put(one, CONST, "ident", (p == j).astype(np.float32))
    put(one, CONST, "iota", np.broadcast_to(j % CAP, (P, P)).astype(np.float32))
    put(one, CONST, "causal", np.where(p <= j, 0.0, NEG).astype(np.float32))
    early = np.zeros((P, EARLY["all"][1]), np.float32)
    selh = np.zeros((MH, MH, P), np.float32)
    for h in range(MH):
        selh[h, h] = 1.0
    put(early, EARLY, "selh", selh)
    dist = T - 1 - np.arange(2 * T)
    exact = NBUCKET // 2
    nf = np.maximum(dist, 1).astype(np.float32)
    large = exact + (np.log(nf / np.float32(exact)) / np.float32(math.log(MAXDIST / exact))
                     * np.float32(NBUCKET - exact)).astype(np.int32)
    bucket = np.where(dist < exact, dist, np.minimum(large, NBUCKET - 1))
    put(early, EARLY, "onehot", ((bucket[None, :] == np.arange(NBUCKET)[:, None]) & (dist >= 0)).astype(np.float32))
    put(early, EARLY, "future", np.broadcast_to(np.where(dist >= 0, 0.0, NEG), (AH, 2 * T)).astype(np.float32))
    put(early, EARLY, "mirror", (p + j == P - 1).astype(np.float32))
    late = np.zeros((P, LATE["all"][1]), np.float32)
    m = (np.arange(NT)[None, :, None] * P + np.arange(P)[:, None, None])
    n = np.arange(T)[None, None, :]
    put(late, LATE, "ahead", np.maximum(n - m, 0).astype(np.float32))
    put(late, LATE, "behind", np.maximum(m - n, 0).astype(np.float32))
    put(late, LATE, "before", (n < m).astype(np.float32))
    put(late, LATE, "n1", np.broadcast_to(np.arange(T) + 1.0, (P, T)).astype(np.float32))
    put(late, LATE, "n2", np.broadcast_to(T - np.arange(T), (P, T)).astype(np.float32))
    half = RD // 2
    inv = (np.float32(1.0) / (np.float32(10000.0) ** (np.arange(half, dtype=np.float32) / np.float32(half)))).astype(np.float32)
    tok = (np.arange(NT)[None, :, None] * P + np.arange(P)[:, None, None]).astype(np.float32)
    for base, c, s in ((T, "cosx", "sinx"), (0, "cosc", "sinc")):
        ang = ((tok + np.float32(base)) * inv[None, None, :]).astype(np.float32)
        put(late, LATE, c, np.cos(ang.astype(np.float64)).astype(np.float32))
        put(late, LATE, s, np.sin(ang.astype(np.float64)).astype(np.float32))
    put(late, LATE, "wn", np.concatenate([T - 1 - tok[:, :, 0], tok[:, :, 0]], axis=1))
    return {"const": one, "early": early, "late": late}


class Queue:

    def __init__(self, sem, chained):
        self.sem, self.chained = sem, chained
        self.items, self.count, self.seen = [], 0, {}

    def wait(self, *marks):
        for mark in marks:
            if mark is None:
                continue
            sem, value = mark
            if self.seen.get(sem.name, 0) < value:
                self.seen[sem.name] = value
                self.items.append(lambda e, s=sem, v=value: e.wait_ge(s, v))

    def reserve(self):
        self.count += 1
        self.items.append(None)
        return len(self.items) - 1, (self.sem, self.count)

    def fill(self, place, issue, after):
        index, mark = place
        waits = [w for w in after if w is not None]

        def item(e):
            for s, v in waits:
                e.wait_ge(s, v)
            issue(e).then_inc(self.sem, 1)

        self.items[index] = item
        return mark

    def do(self, issue, after=(), signal=True):
        self.wait(*after)
        if self.chained and self.count:
            self.wait((self.sem, self.count))
        if not signal:
            self.items.append(issue)
            return None
        self.count += 1
        self.items.append(lambda e: issue(e).then_inc(self.sem, 1))
        return (self.sem, self.count)


def build(nc, dram, out, tap=None):
    ctx = ExitStack()
    with ctx:
        def sem(name):
            return ctx.enter_context(nc.semaphore(name))

        ring = ctx.enter_context(nc.sbuf_tensor("ring", [P, RING, SLOT], F32))
        KB = 256
        arena = ctx.enter_context(nc.sbuf_tensor("arena", [P, 128 * KB], F32))
        parts = ctx.enter_context(nc.sbuf_tensor("parts", [P, 2 * NHALF * HALF + 2 * KD * T + 4 * KD * MH], F32R))
        keep = ctx.enter_context(nc.sbuf_tensor("keep", [P, 1880], F32))
        ps = ctx.enter_context(nc.psum_tensor("ps", [P, 8, W], F32))

        def at(kb, *shape):
            n = int(np.prod(shape))
            v = arena[:, int(kb * KB):int(kb * KB) + n]
            assert kb * KB + n <= 128 * KB
            if len(shape) == 2:
                return v.rearrange("p (a b) -> p a b", a=shape[0])
            if len(shape) == 3:
                return v.rearrange("p (a b c) -> p a b c", a=shape[0], b=shape[1])
            return v

        used = [0]

        def small(*shape):
            n = int(np.prod(shape))
            v = keep[:, used[0]:used[0] + n]
            used[0] += n
            assert used[0] <= 1880
            if len(shape) == 2:
                return v.rearrange("p (a b) -> p a b", a=shape[0])
            if len(shape) == 3:
                return v.rearrange("p (a b c) -> p a b c", a=shape[0], b=shape[1])
            return v

        const, cols = small(CONST["all"][1]), small(COLS["all"][1])
        wr = small(KD, NE)
        early, late = at(110, EARLY["all"][1]), at(54, LATE["all"][1])

        def part(v, table, name, rows=P):
            s, n = table[name]
            return v[0:rows, s:s + n]

        ident, iota = part(const, CONST, "ident"), part(const, CONST, "iota")
        causal = part(const, CONST, "causal")

        PE, V, A, G, SP = (Queue(sem(n), c) for n, c in
                           (("pe", False), ("dve", True), ("act", True), ("pool", True), ("sp", False)))

        def mm(out_, lhsT, rhs, start, stop, after=(), signal=False):
            return PE.do(lambda e: e.matmul(out_, lhsT, rhs, start=start, stop=stop, skip_group_check=True),
                         after, signal)

        def flip(out_, in_, after=(), signal=False):
            k = in_.shape[0]
            return PE.do(lambda e: e.transpose(out_, in_, ident[0:k, 0:k]), after, signal)

        def tt(o, a, b, op, after=()):
            return V.do(lambda e: e.tensor_tensor(o, a, b, op), after)

        def ts(o, a, s1, s2, op0, op1=None, after=()):
            if op1 is None:
                return V.do(lambda e: e.tensor_scalar(o, a, s1, None, op0), after)
            return V.do(lambda e: e.tensor_scalar(o, a, s1, s2, op0, op1), after)

        def stt(o, a, s, b, op0, op1, after=()):
            return V.do(lambda e: e.scalar_tensor_tensor(out=o, in0=a, scalar=s, in1=b, op0=op0, op1=op1), after)

        def recip(o, a, after=()):
            return V.do(lambda e: e.reciprocal(o, a), after)

        def vcopy(o, a, after=()):
            return V.do(lambda e: e.tensor_copy(o, a), after)

        def reduce(o, a, op, after=()):
            return V.do(lambda e: e.tensor_reduce(o, a, AX, op), after)

        def act(o, a, func, scale=1.0, bias=0.0, accum=None, after=()):
            if accum is None:
                return A.do(lambda e: e.activation(o, a, func, bias=bias, scale=scale), after)
            return A.do(lambda e: e.activation(o, a, func, bias=bias, scale=scale, accum_out=accum), after)

        def acopy(o, a, after=()):
            return act(o, a, ACT.Copy, after=after)

        def now(q):
            return (q.sem, q.count)

        loads = [0]

        def load(dst, src, after=(), queue=None):
            s = sem(f"load{loads[0]}")
            loads[0] += 1
            q = queue or G
            q.wait(*after)
            q.items.append(lambda e: e.dma_start(dst, src).then_inc(s, 16))
            return (s, 16)

        landed = [sem(f"landed{i}") for i in range(RING)]
        chunks, freed = [0], [None] * RING

        def take(src, shape):
            s = chunks[0] % RING
            chunks[0] += 1
            dst = ring[:, s, 0:int(np.prod(shape))]
            if len(shape) == 2:
                dst = dst.rearrange("p (a b) -> p a b", a=shape[0])
            SP.wait(freed[s])
            SP.items.append(lambda e: e.dma_start(dst, src).then_inc(landed[s], 16))
            return dst, (landed[s], 16 * ((chunks[0] - 1) // RING + 1)), s

        bank_free = [None] * 8

        rows = dram["rows"]

        def row(name, s=0, n=None):
            a, m = ROWS[name]
            return rows[a + s:a + s + (m if n is None else n)]

        X = at(0, NT, D)
        cols_in = load(cols, dram["cols"], queue=A)
        const_in = load(const, dram["const"], queue=A)
        x_in = load(X, dram["x"].rearrange("(t p) d -> p t d", p=P), queue=A)
        gate_pow = small(16)
        pow_in = G.do(lambda e: e.memset(gate_pow, -0.5))
        ones = small(2)
        ones_in = G.do(lambda e: e.memset(ones, 1.0))

        TA = at(120, 4, W)
        ta_free, ta_turn = [None] * 4, [0]

        def scratch():
            i = ta_turn[0] % 3
            ta_turn[0] += 1
            return TA[:, i, :], i

        def logistic(o, pre, after=()):
            e = act(o, pre, ACT.Exp, scale=-1.0, after=(*after, now(V)))
            ts(o, o, 1.0, None, ALU.add, after=(e,))
            return recip(o, o)

        def turn_pair(dst, scale=1.0):
            def evac(k, view, m):
                return act(dst[:, k:k + 2, :].rearrange("p a b -> p (a b)"), view, ACT.Copy, scale=scale, after=(m,))
            return evac

        def log_sigmoid(o, x, t1, t2):
            m = stt(t1, x, -1.0, x, ALU.mult, ALU.max)
            m = act(t1, t1, ACT.Exp, scale=-1.0, after=(m,))
            yield
            ts(t2, t1, 2.0, None, ALU.add, after=(m,))
            recip(t2, t2)
            yield
            tt(t1, t1, t2, ALU.mult)
            tt(t2, t1, t1, ALU.mult)
            ts(o, t2, 1.0 / 15, None, ALU.mult)
            for n in (13, 11, 9, 7, 5, 3):
                stt(o, o, 1.0 / n, t2, ALU.add, ALU.mult)
            yield
            stt(o, o, 1.0, t1, ALU.add, ALU.mult)
            ts(o, o, 2.0, None, ALU.mult)
            stt(o, x, 0.0, o, ALU.min, ALU.subtract)

        ssq = small(16)

        def rstd(n, width, after=()):
            m = ts(ssq[:, 0:n], ssq[:, 0:n], 1.0 / width, EPS, ALU.mult, ALU.add, after=after)
            return G.do(lambda e: e.tensor_tensor(ssq[:, 0:n], ssq[:, 0:n], gate_pow[:, 0:n], ALU.pow),
                        (m, pow_in))

        def row_rms(o, x, junk, after=(), gain=None, gain_in=None):
            A.wait(now(V), now(G))
            for t in range(NT):
                m = act(junk[:, t, :], x[:, t, :], ACT.Square, accum=ssq[:, t:t + 1], after=after)
            r = rstd(NT, D, after=(m,))
            for t in range(NT):
                if gain is None:
                    m = ts(o[:, t, :], x[:, t, :], ssq[:, t:t + 1], None, ALU.mult, after=(r,))
                else:
                    m = stt(o[:, t, :], x[:, t, :], ssq[:, t:t + 1], gain, ALU.mult, ALU.mult, after=(r, gain_in))
            return m

        def flip_tokens(dst, src, ntile, ready, evac, first=0, pairs=False):
            for k in range(first, ntile, 2):
                b = 6 + (k // 2) % 2
                PE.wait(bank_free[b])
                for i in range(2):
                    for t in range(NT):
                        m = flip(ps[:, b, i * T + t * P:i * T + (t + 1) * P], src[:, t, (k + i) * P:(k + i + 1) * P],
                                 after=(ready, const_in), signal=(i == 1 and t == NT - 1))
                for i in range(0, 2, 1 + pairs):
                    bank_free[b] = evac(k + i, ps[:, b, i * T:(i + 1 + pairs) * T], m)
            return bank_free[b]

        cst = small(3 * KD)
        call = cols[:, COLS["c"][0]:COLS["c"][0] + 3 * KD]
        sg = logistic(cst, call, after=(cols_in,))
        m = tt(cst, cst, call, ALU.mult)
        crep = at(127, KD, 32)
        crep2 = small(KD, 32)
        m = vcopy(crep, cst[:, 0:KD].unsqueeze(2).broadcast_to([P, KD, 32]))
        vcopy(crep2[:, :, 0:16], cst[:, KD:2 * KD].unsqueeze(2).broadcast_to([P, KD, 16]))
        crep_ok = vcopy(crep2[:, :, 16:32], cst[:, 2 * KD:3 * KD].unsqueeze(2).broadcast_to([P, KD, 16]))

        lg, lgs, lt1, lt2 = (small(2 * RH) for _ in range(4))
        V.wait(load(lg, row("decay").partition_broadcast(P)))
        for _ in log_sigmoid(lgs, lg, lt1, lt2):
            pass

        def ada(w, c0, ngroup, rep, bias, bank, dst, stored=None):
            rows_per = SLOT // (ngroup * W)
            bt = [load(dst[32 * n:32 * n + 32, :], row(bias, c0 + n * W, W).partition_broadcast(32),
                       after=(now(PE),)) for n in range(ngroup)]
            PE.wait(bank_free[bank], crep_ok)
            for q in range(KD // rows_per):
                src = w[q * rows_per * P:(q + 1) * rows_per * P, c0:c0 + ngroup * W]
                slot, got, s = take(src.rearrange("(k p) n -> p k n", p=P), (rows_per, ngroup * W))
                for kk in range(rows_per):
                    k = q * rows_per + kk
                    for n in range(ngroup):
                        m = mm(ps[32 * n:32 * n + 32, bank, :], rep[:, k, :], slot[:, kk, n * W:(n + 1) * W],
                               k == 0, k == KD - 1, after=(got,), signal=(n == ngroup - 1 and kk == rows_per - 1))
                freed[s] = m
                if q < KD // rows_per - 1:
                    yield
            n = 32 * ngroup
            bank_free[bank] = m = tt(dst[0:n, :], ps[0:n, bank, :], dst[0:n, :], ALU.add, after=(m, *bt))
            if stored is not None:
                for n in range(ngroup):
                    m = load(dram["mods"][stored + n * W:stored + (n + 1) * W].unsqueeze(0),
                             dst[32 * n:32 * n + 1, :], after=(m,))
                    mods_in.append(m)
            ada_mark.append(bank_free[bank])
            yield

        mods_in, ada_mark = [], []
        def ada_columns(rowsv, ready, pick, dst_sh, dst_g, g):
            PE.wait(bank_free[7])
            for b in range(4):
                m = flip(ps[:, 7, b * P:(b + 1) * P], rowsv[:, b * P:(b + 1) * P], after=(ready, const_in), signal=True)
            v = ps[:, 7, :].rearrange("p (b n j) -> p n b j", b=4, n=4)
            vcopy(dst_sh.rearrange("p (n b) -> p n b", n=2), v[:, 0:2, :, pick], after=(m,))
            bank_free[7] = m = stt(dst_g.rearrange("p (n b) -> p n b", n=2), v[:, 2:4, :, pick], 1.0,
                                   g.rearrange("p (n b) -> p n b", n=2), ALU.add, ALU.mult)
            return m

        XN = at(8, NT, D)
        modA = at(106, W)
        first_rows = ada(dram["w_ada"], 0, 4, crep, "b_ada", 3, modA)
        next(first_rows)
        xn = row_rms(XN, X, at(24, NT, D), after=(x_in,))
        for _ in first_rows:
            pass
        mA = ada_mark[-1]
        G.wait(mA)
        early_in = load(early, dram["early"])
        table = small(AH)
        table_in = load(table[0:NBUCKET, :], dram["rel_bias"])
        wif = at(118, KD, 2 * MH)
        wif_in = load(wif, dram["w_in"][:, IM:IM + 2 * MH].rearrange("(k p) n -> p k n", p=P))
        lam4 = at(119, 4 * ADH)
        lam_in = load(lam4, row("lam").partition_broadcast(P))
        wr_in = load(wr, dram["w_router"].rearrange("(k p) n -> p k n", p=P))
        brt = small(NE)
        brt_in = load(brt, row("b_router").partition_broadcast(P))
        sh1, gs1 = small(KD), small(KD)
        mod1 = ada_columns(modA, mA, 0, sh1, gs1, part(cols, COLS, "norm_g"))


        o = 2 * NHALF * HALF
        WHI, WLO = ([parts[:, (2 * i + j) * HALF:(2 * i + j + 1) * HALF] for i in range(NHALF)] for j in range(2))
        HTH, HTL = (parts[:, o + j * KD * T:o + (j + 1) * KD * T].rearrange("p (k t) -> p k t", k=KD) for j in range(2))
        o += 2 * KD * T
        WIF = [parts[:, o + j * 2 * KD * MH:o + (j + 1) * 2 * KD * MH].rearrange("p (k n) -> p k n", k=KD) for j in range(2)]
        hTs = (HTH, HTL)

        def split(hi, lo, v, after=(), on_vector=False):
            h = (vcopy if on_vector else acopy)(hi, v, after=after)
            return tt(lo, v, hi.bitcast(F32), ALU.subtract, after=(h,))

        def modulate(dst, sh, gs, ready):
            def evac(k, view, m):
                return act(dst[:, k, :], view, ACT.Identity, scale=gs[:, k:k + 1], bias=sh[:, k:k + 1],
                           after=(m, ready))
            return evac

        def modulate_split(sh, gs, ready):
            def evac(k, view, m):
                s_, i = scratch_pair(k)
                o = s_[:, (k % 2) * T:(k % 2 + 1) * T]
                e = act(o, view, ACT.Identity, scale=gs[:, k:k + 1], bias=sh[:, k:k + 1], after=(m, ready, ta_free[i]))
                if k % 2 == 1:
                    two = [v[:, k - 1:k + 1, :].rearrange("p a b -> p (a b)") for v in hTs]
                    ta_free[i] = h_parts[0] = split(*two, s_, (e,), on_vector=(k % 4 == 3))
                return e
            return evac

        pair_now, h_parts = [None], [None]

        def scratch_pair(k):
            if k % 2 == 0:
                pair_now[0] = scratch()
            return pair_now[0]

        turn = [0]

        def next_bank():
            b = turn[0] % 3
            turn[0] += 1
            return b

        def mm3(out_, lhsT, rhs, start, stop, after=(), signal=False):
            (ah, al), (bh, bl) = lhsT, rhs
            mm(out_, ah, bh, start, False, after)
            mm(out_, ah, bl, False, False)
            return mm(out_, al, bh, False, stop, signal=signal)

        kept, half_free, halves = [], [None] * NHALF, [0]

        def keep_places(n):
            while len(kept) < n:
                kept.append((A.reserve(), V.reserve()))

        def split_half(v, got):
            keep_places(1)
            place_a, place_v = kept.pop(0)
            i = halves[0] % NHALF
            halves[0] += 1
            a, free = v.shape[1], half_free[i]
            hi, lo = (x[i].rearrange("p (a b) -> p a b", a=a) for x in (WHI, WLO))
            h = A.fill(place_a, lambda e: e.activation(hi, v, ACT.Copy), (got, free))
            m = V.fill(place_v, lambda e: e.tensor_tensor(lo, v, hi.bitcast(F32), ALU.subtract), (h,))
            return hi, lo, m, i

        side = []

        def side_step():
            if side and next(side[0], "done") == "done":
                side.pop(0)

        def side_rest():
            while side:
                side_step()

        def natural(w, c0, ready, evac, more=True):
            pair = (next_bank(), next_bank())
            n_half = KD // 2
            for c in range(n_half):
                if c % 2 == 0:
                    src = w[2 * c * P:(2 * c + 4) * P, c0:c0 + W]
                    slot, got, s = take(src.rearrange("(k p) n -> p k n", p=P), (4, W))
                hi, lo, ok, i = split_half(slot[:, 2 * (c % 2):2 * (c % 2) + 2, :], got)
                if c % 2 == 1:
                    freed[s] = ok
                keep_places(2 if more else min(2, n_half - 1 - c))
                for t in range(NT):
                    if c == 0:
                        PE.wait(bank_free[pair[t]])
                    for kk in range(2):
                        k, ts_ = 2 * c + kk, slice(t * P, (t + 1) * P)
                        m = mm3(ps[:, pair[t], :], (HTH[:, k, ts_], HTL[:, k, ts_]), (hi[:, kk, :], lo[:, kk, :]),
                                k == 0, k == KD - 1, after=(ready, ok), signal=(kk == 1))
                    if c == n_half - 1:
                        bank_free[pair[t]] = evac(t, ps[:, pair[t], :], m)
                half_free[i] = m
                side_step()

        def transposed(w, c0, ready, evac, more=True):
            for i in range(4):
                if i % 2 == 0:
                    src = w[:, c0 + i * P:c0 + (i + 2) * P]
                    slot, got, s = take(src.rearrange("(k p) n -> p k n", p=P), (KD, 2 * P))
                    b = next_bank()
                hi, lo, ok, buf = split_half(slot[:, :, (i % 2) * P:(i % 2 + 1) * P], got)
                if i % 2 == 1:
                    freed[s] = ok
                keep_places(2 if more else min(2, 3 - i))
                PE.wait(bank_free[b] if i % 2 == 0 else None)
                for k in range(KD):
                    m = mm3(ps[:, b, (i % 2) * T:(i % 2 + 1) * T], (hi[:, k, :], lo[:, k, :]),
                            (HTH[:, k, :], HTL[:, k, :]), k == 0, k == KD - 1, after=(ready, ok), signal=(k == KD - 1))
                half_free[buf] = m
                if i % 2 == 1:
                    for j in (i - 1, i):
                        bank_free[b] = evac(j, ps[:, b, (j % 2) * T:(j % 2 + 1) * T], m)
                side_step()

        def plain_natural(lhs, ktiles, w, c0, ready, evac):
            pair = (next_bank(), next_bank())
            order = [(q, ready) for q in range(ktiles // 4)]
            for at_, (q, ok) in enumerate(order):
                src = w[q * 4 * P:(q + 1) * 4 * P, c0:c0 + W]
                slot, got, s = take(src.rearrange("(k p) n -> p k n", p=P), (4, W))
                for t in range(NT):
                    if at_ == 0:
                        PE.wait(bank_free[pair[t]])
                    for kk in range(4):
                        m = mm(ps[:, pair[t], :], lhs(4 * q + kk, t), slot[:, kk, :], at_ == 0 and kk == 0,
                               at_ == len(order) - 1 and kk == 3, after=(ok, got), signal=(kk == 3))
                    if at_ == len(order) - 1:
                        bank_free[pair[t]] = evac(t, ps[:, pair[t], :], m)
                freed[s] = m

        keep_places(2)
        flip_tokens(HTH, XN, KD, xn, modulate_split(sh1, gs1, mod1))
        h_ok = h_parts[0]

        def by_tile(lhs, w, order, evac, finish):
            got = {}
            for n in range(2):
                for q, _ in order:
                    src = w[q * 4 * P:(q + 1) * 4 * P, n * W:(n + 1) * W]
                    got[n, q] = take(src.rearrange("(k p) n -> p k n", p=P), (4, W))
            for t in range(NT):
                for n in range(2):
                    b = next_bank()
                    PE.wait(bank_free[b])
                    for at_, (q, ok) in enumerate(order):
                        slot, landed_, s = got[n, q]
                        ok = ok() if callable(ok) else ok
                        for kk in range(4):
                            m = mm(ps[:, b, :], lhs(4 * q + kk, t), slot[:, kk, :], at_ == 0 and kk == 0,
                                   at_ == 1 and kk == 3, after=(ok, landed_), signal=(kk == 3))
                        freed[s] = m
                    bank_free[b] = evac(t, n, ps[:, b, :], m)
                finish(t)

        def column_rstd(v, width, after=()):
            m = ts(v, v, 1.0 / width, EPS, ALU.mult, ALU.add, after=after)
            return G.do(lambda e: e.tensor_tensor(v, v, gate_pow[:, 0:1], ALU.pow), (m, pow_in))

        QT, KT = at(24, KD, T), at(32, KD, T)
        cw = part(cols, COLS, "conv_w").rearrange("p (j c) -> p j c", j=4)
        cb = part(cols, COLS, "conv_b")
        conv_ok, held = {}, []

        def conv_evac(base, dst):
            def evac(i, view, m):
                if i % 2 == 0:
                    return held.append(view)
                views, c = (held.pop(), view), base + i - 1
                for v, j in zip(views, (c, c + 1)):
                    f = act(dst[:, j % KD, :], v, ACT.Identity, scale=cw[:, 3, j:j + 1], bias=cb[:, j:j + 1], after=(m,))
                for v, j in zip(views, (c, c + 1)):
                    o = dst[:, j % KD, :]
                    for back in (1, 2, 3):
                        f = stt(o[:, back:T], v[:, 0:T - back], cw[:, 3 - back, j:j + 1], o[:, back:T],
                                ALU.mult, ALU.add, after=(f,))
                two = dst[:, c % KD:c % KD + 2, :]
                conv_ok[dst is KT] = act(two, two, ACT.Silu, after=(f,))
                return f
            return evac

        MODT = [at(kb, W) for kb in (78, 80, 40, 42)]
        sh2, gs2, shc, gsc = (small(KD) for _ in range(4))
        rounds = [ada(dram["w_ada_2"], 0, 4, crep2, "b_ada_2", 3, MODT[0]),
                  ada(dram["w_ada"], 2 * D, 2, crep, "b_ada", 3, MODT[1], 0),
                  ada(dram["w_ada_2"], 2 * D, 4, crep2, "b_ada_2", 3, MODT[2], D),
                  ada(dram["w_ada_2"], 4 * D, 4, crep2, "b_ada_2", 3, MODT[3], 3 * D)]
        spread_rounds = (x for r_ in rounds for x in r_)

        def some_ada(n):
            for _ in range(n):
                next(spread_rounds, None)

        for n in range(4):
            transposed(dram["w_in"], QM + n * W, h_ok, conv_evac(4 * n, QT if n < 2 else KT))
            if n == 1:
                wif_ok = split(*WIF, wif, (wif_in,))
            some_ada(1)
        gi, gf, gF, gt1, gt2 = (at(120 + i, T)[0:MH, :] for i in range(5))
        b_if = part(cols, COLS, "b_if", MH)
        for j in range(2):
            for k in range(KD):
                js = slice(j * MH, (j + 1) * MH)
                m = mm3(ps[0:MH, 6, j * T:(j + 1) * T], [w_[:, k, js] for w_ in WIF], (HTH[:, k, :], HTL[:, k, :]),
                        k == 0, k == KD - 1, after=(wif_ok, bank_free[6]), signal=(k == KD - 1))
        ts(gi, ps[0:MH, 6, 0:T], b_if[:, 0:1], None, ALU.add, after=(m,))
        bank_free[6] = ts(gf, ps[0:MH, 6, T:2 * T], b_if[:, 1:2], None, ALU.add)
        gates = {}

        def gate_rows():
            yield from log_sigmoid(gF, gf, gt1, gt2)
            yield
            V.do(lambda e: e.memset(gt1, 0.0))
            V.do(lambda e: e.tensor_tensor_scan(gf, gF, gt1, 0.0, ALU.add, ALU.add))
            tt(gi, gi, gf, ALU.subtract)
            yield
            V.do(lambda e: e.tensor_tensor_scan(gF, gi, gt1, 0.0, ALU.max, ALU.max))
            m = tt(gf, gf, gF, ALU.add)
            gates["exp"] = act(gf, gf, ACT.Exp, scale=-1.0, after=(m,))
            gates["rows"] = ts(gF, gF, -1.0, None, ALU.mult)

        side.append(gate_rows())
        ccol, emcol = small(NT, MH), small(NT, MH)
        ET = at(40, MH, 3 * P)

        def gate_tables():
            PE.wait(bank_free[7])
            for t in range(NT):
                flip(ps[:, 7, t * MH:(t + 1) * MH], gi[:, t * P:(t + 1) * P], after=(gates["rows"], gates["exp"], early_in),
                     signal=True)
                m = flip(ps[:, 7, 8 + t * MH:8 + (t + 1) * MH], gf[:, t * P:(t + 1) * P], signal=True)
            vcopy(ccol, ps[:, 7, 0:8].rearrange("p (t h) -> p t h", t=NT), after=(m,))
            bank_free[7] = vcopy(emcol, ps[:, 7, 8:16].rearrange("p (t h) -> p t h", t=NT))
            selh = part(early, EARLY, "selh", MH).rearrange("p (h m) -> p h m", h=MH)
            et_ok = None
            for h in range(MH):
                if h % 2 == 0:
                    PE.wait(bank_free[6])
                    for j in range(2):
                        m = mm(ps[:, 6, j * T:(j + 1) * T], selh[:, h + j, :], gF, True, True, signal=True)
                nm = ps[:, 6, (h % 2) * T:(h % 2 + 1) * T]
                tt(ET[:, h, 0:P], nm[:, 0:P], causal, ALU.add, after=(m,))
                vcopy(ET[:, h, P:2 * P], nm[:, P:2 * P])
                bank_free[6] = f = tt(ET[:, h, 2 * P:3 * P], nm[:, P:2 * P], causal, ALU.add)
                act(ET[:, h, 0:2 * P], ET[:, h, 0:2 * P], ACT.Exp, bias=ccol[:, 0, h:h + 1], after=(f,))
                et_ok = act(ET[:, h, 2 * P:3 * P], ET[:, h, 2 * P:3 * P], ACT.Exp, bias=ccol[:, 1, h:h + 1])
            return et_ok

        HM = at(8, NT, 2 * D)
        v_ok = {}

        def v_evac(n):
            def evac(t, view, m):
                v_ok[n] = acopy(HM[:, t, n * W:(n + 1) * W], view, after=(m,))
                return v_ok[n]
            return evac

        PT = [at(106 + 1.5 * i, 3 * P) for i in range(2)]
        den = small(2, NT)
        head_ok = {}

        def mlstm_scores(h):
            for k in range(2):
                m = mm(ps[:, 4, 0:T], KT[:, 2 * h + k, 0:P], QT[:, 2 * h + k, :], k == 0, k == 1,
                       after=(conv_ok[True], conv_ok[False], bank_free[4]))
            for k in range(2):
                m = mm(ps[:, 4, T:T + P], KT[:, 2 * h + k, P:T], QT[:, 2 * h + k, P:T], k == 0, k == 1,
                       signal=(k == 1))
            bank_free[4] = stt(PT[h % 2], ps[:, 4, 0:3 * P], MDK ** -0.5, ET[:, h, :], ALU.mult, ALU.mult,
                               after=(m, et_ok))
            return bank_free[4]

        def mlstm_values(h, ready):
            p = PT[h % 2]
            PE.wait(ready, ones_in, bank_free[5], bank_free[6], bank_free[7], v_ok[h])
            v = [HM[:, t, h * W:(h + 1) * W] for t in range(NT)]
            mm(ps[:, 5, :], p[:, 0:P], v[0], True, True)
            mm(ps[:, 6, :], p[:, P:2 * P], v[0], True, False)
            mm(ps[:, 6, :], p[:, 2 * P:3 * P], v[1], False, True)
            mm(ps[:, 7, 0:1], p[:, 0:P], ones[:, 0:1], True, True)
            mm(ps[:, 7, 1:2], p[:, P:2 * P], ones[:, 0:1], True, False)
            m = mm(ps[:, 7, 1:2], p[:, 2 * P:3 * P], ones[:, 0:1], False, True, signal=True)
            d, e = den[:, 0, :], den[:, 1, :]
            ts(d, ps[:, 7, 0:NT], -1.0, None, ALU.mult, after=(m,))
            tt(d, d, ps[:, 7, 0:NT], ALU.max)
            tt(d, d, emcol[:, :, h], ALU.max)
            bank_free[7] = recip(e, d)
            for t in range(NT):
                m = ts(v[t], ps[:, 5 + t, :], e[:, t:t + 1], None, ALU.mult)
                bank_free[5 + t] = m
            head_ok[h] = m

        QMASK, KAT, VAN = at(54, AH, NT, T), at(70, KD, T), at(78, NT, D)
        zq = G.do(lambda e: e.memset(QMASK, 0.0))
        aq_ok, ak_ok, av_ok = {}, {}, {}

        def qa_evac(n):
            def evac(i, view, m):
                h = 4 * n + i
                act(QMASK[0:ADH, h, 0, :], view[0:ADH, :], ACT.Copy, scale=ADH ** -0.5, after=(m, zq))
                aq_ok[h] = act(QMASK[ADH:P, h, 1, :], view[ADH:P, :], ACT.Copy, scale=ADH ** -0.5)
                return aq_ok[h]
            return evac

        def ka_evac(n):
            def evac(i, view, m):
                ak_ok[4 * n + i] = acopy(KAT[:, 4 * n + i, :], view, after=(m,))
                return ak_ok[4 * n + i]
            return evac

        def va_evac(n):
            def evac(t, view, m):
                av_ok[n] = acopy(VAN[:, t, n * W:(n + 1) * W], view, after=(m,))
                return av_ok[n]
            return evac

        toep = dram["toeplitz"]
        brow = at(125, 2 * T)[0:AH, :]
        m = mm(ps[0:AH, 6, :], table[0:NBUCKET, :], part(early, EARLY, "onehot", NBUCKET), True, True,
               after=(bank_free[6], table_in, early_in), signal=True)
        bank_free[6] = m = tt(brow, ps[0:AH, 6, :], part(early, EARLY, "future", AH), ALU.add, after=(m,))
        m = load(toep.rearrange("(h j) -> h j", h=AH), brow, after=(m,))
        BREV, BIAS = at(86, AH, T), at(46, AH, T)
        brev_in = load(BREV, bass.AP(toep.tensor, 0, [[1, P], [2 * T, AH], [1, T]]), after=(m,))

        def bias_turn():
            for j in range(4):
                b = 4 + j % 2
                m = mm(ps[:, b, :], part(early, EARLY, "mirror"), BREV[:, 2 * j:2 * j + 2, :].rearrange("p a b -> p (a b)"),
                       True, True, after=(brev_in, bank_free[b]), signal=True)
                bank_free[b] = acopy(BIAS[:, 2 * j:2 * j + 2, :].rearrange("p a b -> p (a b)"), ps[:, b, :], after=(m,))
            return bank_free[b]

        lamv = small(2)
        l4 = lam4.rearrange("p (a b) -> p a b", a=4)
        tt(l4[:, 0:4:2, :], l4[:, 0:4:2, :], l4[:, 1:4:2, :], ALU.mult, after=(lam_in,))
        m = reduce(lamv, l4[:, 0:4:2, :], ALU.add)
        m = act(lamv, lamv, ACT.Exp, after=(m,))
        tt(lamv[:, 0:1], lamv[:, 1:2], lamv[:, 0:1], ALU.subtract, after=(m,))
        neglam = lamv[:, 0:1]
        ts(neglam, neglam, LAM_INIT, None, ALU.subtract)

        for j in range(8):
            if 3 <= j <= 6:
                r = mlstm_scores(j - 3)
            if j < 4:
                natural(dram["w_in"], VM + j * W, h_ok, v_evac(j))
                if j == 1:
                    side_rest()
                    et_ok = gate_tables()
            else:
                n = j % 2
                transposed(dram["w_in"], (QA if j < 6 else KA) + n * W, h_ok, qa_evac(n) if j < 6 else ka_evac(n))
            if 3 <= j <= 6:
                mlstm_values(j - 3, r)
            some_ada(1)

        ada_columns(MODT[0], ada_mark[1], 0, sh2, gs2, part(cols, COLS, "pre_mix_g"))
        modc_ok = ada_columns(MODT[0], ada_mark[1], 16, shc, gsc, part(cols, COLS, "pre_mix_g"))

        bias_ok = bias_turn()
        HA = at(86, NT, D)
        LG = [at(94 + 3 * i, 2, 3 * P) for i in range(2)]
        AM = [at(100 + 1.5 * i, 3 * P) for i in range(2)]
        AT = [at(103 + 1.5 * i, 3 * P) for i in range(2)]
        mx, sm = small(2, NT), small(2, NT)
        at_free = [None, None]

        def attn_scores(h):
            for m_ in range(2):
                PE.wait(bank_free[4 + m_], aq_ok[h], ak_ok[h])
                q = QMASK[:, h, m_, :]
                mm(ps[:, 4 + m_, 0:T], q[:, P:T], KAT[:, h, :], True, True)
                m = mm(ps[:, 4 + m_, T:T + P], q[:, 0:P], KAT[:, h, 0:P], True, True, signal=True)
            L = LG[h % 2]
            V.wait(now(A))
            tt(L[:, :, 0:T], ps[:, 4:6, 0:T], BIAS[:, h, :].unsqueeze(1).broadcast_to([P, 2, T]), ALU.add,
               after=(m, bias_ok))
            m = tt(L[:, :, T:T + P], ps[:, 4:6, T:T + P], BIAS[:, h, P:T].unsqueeze(1).broadcast_to([P, 2, P]), ALU.add)
            bank_free[4] = bank_free[5] = m
            yield
            reduce(mx[:, :, 0], L[:, :, 0:T], ALU.max)
            reduce(mx[:, :, 1], L[:, :, T:T + P], ALU.max)
            m = ts(mx, mx, -1.0, None, ALU.mult)
            for m_ in range(2):
                act(L[:, m_, 0:T], L[:, m_, 0:T], ACT.Exp, bias=mx[:, m_, 0:1], accum=sm[:, m_, 0:1], after=(m,))
                a = act(L[:, m_, T:T + P], L[:, m_, T:T + P], ACT.Exp, bias=mx[:, m_, 1:2], accum=sm[:, m_, 1:2])
            yield
            recip(sm, sm, after=(a,))
            ts(sm[:, 1, :], sm[:, 1, :], neglam, None, ALU.mult)
            V.wait(at_free[h % 2])
            am = AM[h % 2]
            for q, (lo, hi) in enumerate(((0, T), (T, T + P))):
                ts(L[:, 1, lo:hi], L[:, 1, lo:hi], sm[:, 1, q:q + 1], None, ALU.mult)
                m = stt(am[:, lo:hi], L[:, 0, lo:hi], sm[:, 0, q:q + 1], L[:, 1, lo:hi], ALU.mult, ALU.add)
            attn_ready[h] = m

        attn_ready = {}

        def attn_flips(h, ready):
            am, aT = AM[h % 2], AT[h % 2]
            PE.wait(ready, bank_free[6])
            for j in range(3):
                m = flip(ps[:, 6, j * P:(j + 1) * P], am[:, j * P:(j + 1) * P], signal=True)
            bank_free[6] = at_free[h % 2] = acopy(aT, ps[:, 6, 0:3 * P], after=(m,))
            return bank_free[6]

        def attn_values(h, c):
            aT = AT[h % 2]
            v = [VAN[:, t, h * P:(h + 1) * P] for t in range(NT)]
            PE.wait(c, bank_free[7], av_ok[h // 4])
            mm(ps[:, 7, 0:P], aT[:, 2 * P:3 * P], v[0], True, True)
            mm(ps[:, 7, P:T], aT[:, 0:P], v[0], True, False)
            m = mm(ps[:, 7, P:T], aT[:, P:2 * P], v[1], False, True, signal=True)
            bank_free[7] = acopy(HA[:, :, h * P:(h + 1) * P], ps[:, 7, 0:T].rearrange("p (t e) -> p t e", t=NT),
                                 after=(m,))
            return bank_free[7]

        hssq = small(NT * MH)

        def o_evac(n):
            def evac(t, view, m):
                s, i = scratch()
                e = act(s, view, ACT.Sigmoid, after=(m, ta_free[i]))
                hm = HM[:, t, n * W:(n + 1) * W]
                v = tt(hm, hm, s, ALU.mult, after=(e,))
                ta_free[i] = act(s, hm, ACT.Square, accum=hssq[:, NT * n + t:NT * n + t + 1], after=(v,))
                return e
            return evac

        def head_rstd():
            m = ts(hssq, hssq, 1.0 / MDV, EPS, ALU.mult, ALU.add, after=(now(A),))
            V.wait(G.do(lambda e: e.tensor_tensor(hssq, hssq, gate_pow[:, 0:NT * MH], ALU.pow), (m, pow_in)))

        def z_evac(n):
            def evac(t, view, m):
                s, i = scratch()
                e = act(s, view, ACT.Silu, after=(m, ta_free[i]))
                hm = HM[:, t, n * W:(n + 1) * W]
                ta_free[i] = zdone[n] = stt(hm, hm, hssq[:, NT * n + t:NT * n + t + 1], s, ALU.mult, ALU.mult,
                                            after=(e,))
                return e
            return evac

        zdone = {}
        HMT = at(24, 2 * KD, T)
        mg = part(cols, COLS, "mnorm_g")

        def scaled(dst, g):
            def evac(k, view, m):
                return act(dst[:, k, :], view, ACT.Copy, scale=g[:, k:k + 1], after=(m,))
            return evac

        def head_flip(h):
            return flip_tokens(HMT, HM, 4 * (h + 1), zdone[h], scaled(HMT, mg), 4 * h)

        steps = [lambda n=n: natural(dram["w_in"], VA + n * W, h_ok, va_evac(n)) for n in range(2)]
        steps += [lambda n=n: natural(dram["w_in"], OM + n * W, h_ok, o_evac(n)) for n in range(4)]
        steps += [lambda n=n: natural(dram["w_in"], ZM + n * W, h_ok, z_evac(n)) for n in range(3)]
        A.wait(*mods_in, modc_ok)
        attn_turned = {}

        def attn_maps(j):
            if j:
                attn_turned[j - 1] = attn_flips(j - 1, attn_ready[j - 1])
            if j < AH:
                yield from attn_scores(j)

        for j, step in enumerate(steps):
            side.append(attn_maps(j))
            if j == 6:
                head_rstd()
            step()
            side_rest()
            if j < AH:
                some_ada(2)
            if j:
                attn_done = attn_values(j - 1, attn_turned[j - 1])
        attn_pe = now(PE)

        sq = at(94, NT, D)
        assq = small(NT * AH)
        hmt_free = attn_pe
        for q in (A, V):
            q.wait(hmt_free)
        head_flip(0)
        HA4 = HA.rearrange("p t (h e) -> p (t h) e", h=AH)

        def attn_norm():
            tt(sq, HA, HA, ALU.mult, after=(attn_done, attn_pe))
            yield
            m = reduce(assq, sq.rearrange("p t (h e) -> p (t h) e", h=AH), ALU.add)
            m = ts(assq, assq, 1.0 / (2 * ADH), EPS, ALU.mult, ALU.add)
            m = G.do(lambda e: e.tensor_tensor(assq, assq, gate_pow, ALU.pow), (m,))
            yield
            tt(HA4, HA4, assq.unsqueeze(2).broadcast_to([P, NT * AH, 2 * ADH]), ALU.mult, after=(m,))

        side.append(attn_norm())
        ha_done = {}

        def za_evac(n):
            def evac(t, view, m):
                s, i = scratch()
                e = act(s, view, ACT.Silu, after=(m, ta_free[i]))
                ha = HA[:, t, n * W:(n + 1) * W]
                ta_free[i] = ha_done[n] = tt(ha, ha, s, ALU.mult, after=(e,))
                return e
            return evac

        natural(dram["w_in"], ZM + 3 * W, h_ok, z_evac(3))
        side_rest()
        head_flip(1)
        natural(dram["w_in"], ZA, h_ok, za_evac(0))
        head_flip(2)
        natural(dram["w_in"], ZA + W, h_ok, za_evac(1), more=False)
        hmt_ok = head_flip(3)
        YM, YA = at(8, NT, D), at(16, NT, D)
        ag = small(KD)
        m = ts(ag, part(cols, COLS, "anorm_g"), 1.0 - LAM_INIT, None, ALU.mult)
        HAT = at(40, KD, T)
        A.wait(m, *mods_in)
        y_ready = {}

        def y_evac(dst, key, n):
            def evac(t, view, m):
                y_ready[key] = acopy(dst[:, t, n * W:(n + 1) * W], view, after=(m,))
                return y_ready[key]
            return evac

        plain_natural(lambda k, t: HMT[:, k, t * P:(t + 1) * P], 2 * KD, dram["w_proj_m"], 0, hmt_ok, y_evac(YM, "m", 0))
        hat_ok = flip_tokens(HAT, HA, KD, ha_done[1], scaled(HAT, ag))
        plain_natural(lambda k, t: HMT[:, k, t * P:(t + 1) * P], 2 * KD, dram["w_proj_m"], W, hmt_ok, y_evac(YM, "m", 1))
        GATE, FG, G1, SH2, SC2, GG2 = (at(kb, D) for kb in (94, 98, 102, 106, 110, 114))
        rows_free = (attn_pe, now(A), now(V))
        late_in = load(late, dram["late"], after=rows_free)
        rows_in = [load(dst, dram["mods"][i * D:(i + 1) * D].partition_broadcast(P), after=(*rows_free, *mods_in))
                   for i, dst in enumerate((GATE, G1, SH2, SC2, GG2))]
        gate_ok, rows_ok = rows_in[0], rows_in[-1]
        fg_in = load(FG, row("final_g").partition_broadcast(P), after=rows_free)
        CX, CT = at(24, NT, D), at(32, KD, T)
        cx_in = load(CX, dram["ctx"].rearrange("(t p) d -> p t d", p=P), after=(now(PE),))
        for n in range(2):
            if n == 1:
                keep_places(2)
            plain_natural(lambda k, t: HAT[:, k, t * P:(t + 1) * P], KD, dram["w_proj_a"], n * W, hat_ok,
                    y_evac(YA, "a", n))
        ct_n = row_rms(CX, CX, at(78, NT, D), after=(cx_in,))

        def mix_evac(n, y, first):
            def evac(t, view, m):
                s, i = scratch()
                e = act(s, view, ACT.Sigmoid, after=(m, ta_free[i]))
                yy, ym = y[:, t, n * W:(n + 1) * W], YM[:, t, n * W:(n + 1) * W]
                if first:
                    ta_free[i] = tt(yy, yy, s, ALU.mult, after=(e, y_ready["m"], y_ready["a"]))
                else:
                    tt(s, yy, s, ALU.mult, after=(e, y_ready["m"], y_ready["a"]))
                    ta_free[i] = tt(ym, ym, s, ALU.add)
                return e
            return evac

        for n in range(2):
            natural(dram["w_in"], GM + n * W, h_ok, mix_evac(n, YM, True))
        ct_ok = flip_tokens(CT, CX, KD, ct_n, modulate(CT, shc, gsc, modc_ok))
        for n in range(2):
            natural(dram["w_in"], GA + n * W, h_ok, mix_evac(n, YA, False), more=(n == 0))
        y_ok = now(V)
        KC, VC = at(86, NT, W), at(90, NT, W)
        cT = lambda k, t: CT[:, k, t * P:(t + 1) * P]

        def plain(dst):
            def evac(t, view, m):
                return acopy(dst[:, t, :], view, after=(m,))
            return evac

        plain_natural(cT, KD, dram["w_in_2"], K2, ct_ok, plain(KC))
        kc_ok = now(A)
        YT = at(40, KD, T)
        yt_ok = flip_tokens(YT, YM, KD, y_ok, turn_pair(YT), pairs=True)

        X2N, JUNK, x1, x2n = at(8, NT, D), at(16, NT, D), [], []
        xsq = small(NT, 2)

        def residual_evac(t, n, view, m):
            s, i = scratch()
            f = tt(s, view, GATE[:, n * W:(n + 1) * W], ALU.mult, after=(m, gate_ok, ta_free[i]))
            xx = X[:, t, n * W:(n + 1) * W]
            ta_free[i] = tt(xx, xx, s, ALU.add)
            return f

        def normed(t):
            x, v = X[:, t, :], xsq[:, t, :]
            m = act(JUNK[:, t, :], x, ACT.Square, accum=v[:, 0:1], after=(now(V),))
            m = column_rstd(v[:, 0:1], D, (m,))
            m = stt(x, x, v[:, 0:1], FG, ALU.mult, ALU.mult, after=(m, fg_in))
            x1.append(m)
            m = act(JUNK[:, t, :], x, ACT.Square, accum=v[:, 1:2], after=(m,))
            m = column_rstd(v[:, 1:2], D, (m,))
            x2n.append(ts(X2N[:, t, :], x, v[:, 1:2], None, ALU.mult, after=(m,)))

        by_tile(lambda k, t: YT[:, k, t * P:(t + 1) * P], dram["w_out"], [(0, yt_ok), (1, yt_ok)], residual_evac, normed)
        plain_natural(cT, KD, dram["w_in_2"], V2, ct_ok, plain(VC))
        vc_ok = now(A)
        if tap:
            tap_sem = load(dram["tap1"].rearrange("(t p) d -> p t d", p=P), X, after=x1)

        xn = x2n[-1]
        keep_places(2)
        flip_tokens(HTH, X2N, KD, xn, modulate_split(sh2, gs2, modc_ok))
        h2_ok = h_parts[0]
        QX, KX, VX, GX = (at(kb, NT, W) for kb in (8, 12, 16, 20))
        def rotary(x, c, s, scratch, after):
            x4 = x.rearrange("p t (h e) -> p t h e", h=RH)
            a, b = x4[:, :, :, 0:64], x4[:, :, :, 64:128]
            bc = [part(late, LATE, n_).rearrange("p (t e) -> p t e", t=NT).unsqueeze(2).broadcast_to([P, NT, RH, 64])
                  for n_ in (c, s)]
            u, v, w_, z = (scratch[:, i, :].rearrange("p (t h e) -> p t h e", t=NT, h=RH) for i in range(4))
            tt(u, a, bc[0], ALU.mult, after=after)
            tt(v, b, bc[1], ALU.mult)
            yield
            tt(w_, a, bc[1], ALU.mult)
            tt(z, b, bc[0], ALU.mult)
            yield
            tt(a, u, v, ALU.subtract)
            rotated.append(tt(b, w_, z, ALU.add))

        RS = at(120, 4, W)
        rotated = []
        wfb = small(2, NT, RH)
        wn = part(late, LATE, "wn").rearrange("p (a t) -> p a t", a=2)
        KF = [at(120 + 4 * d, NT, W) for d in range(2)]
        SF = at(48, 2, RH * RD)
        kc4 = KC.rearrange("p t (h e) -> p t h e", h=RH)
        WT = at(24, RH, NT * T)
        ahead, behind = part(late, LATE, "ahead"), part(late, LATE, "behind")
        XI = at(68, 2, RH, T)
        ret = {}

        def context_states():
            yield from rotary(KC, "cosc", "sinc", RS, (kc_ok, late_in, *ta_free[0:3]))
            yield
            for d in range(2):
                for t in range(NT):
                    m = ts(wfb[:, d, t, :], lgs[:, d * RH:(d + 1) * RH], wn[:, d, t:t + 1], None, ALU.mult)
            m = act(wfb, wfb, ACT.Exp, after=(m,))
            m = ts(wfb, wfb, RD ** -0.5, None, ALU.mult, after=(m,))
            for d in range(2):
                m = tt(KF[d].rearrange("p t (h e) -> p t h e", h=RH), kc4,
                       wfb[:, d, :, :].unsqueeze(3).broadcast_to([P, NT, RH, RD]), ALU.mult)
                PE.wait(bank_free[4 + d], m, vc_ok)
                for h in range(RH):
                    for t in range(NT):
                        m = mm(ps[:, 4 + d, h * RD:(h + 1) * RD], KF[d][:, t, h * RD:(h + 1) * RD],
                               VC[:, t, h * RD:(h + 1) * RD], t == 0, t == NT - 1, signal=(t == NT - 1))
                ret["states_pe"] = m
                ret["state"] = bank_free[4 + d] = acopy(SF[:, d, :], ps[:, 4 + d, :], after=(m,))
                yield

        def decay_tables():
            for h in range(RH):
                ts(WT[:, h, :], ahead, lgs[:, h:h + 1], None, ALU.mult, after=(ct_ok,))
                m = stt(WT[:, h, :], behind, lgs[:, RH + h:RH + h + 1], WT[:, h, :], ALU.mult, ALU.add)
                act(WT[:, h, :], WT[:, h, :], ACT.Exp, after=(m,))
                act(XI[:, 0, h, :], part(late, LATE, "n1"), ACT.Exp, scale=lgs[:, h:h + 1])
                ret["xi"] = act(XI[:, 1, h, :], part(late, LATE, "n2"), ACT.Exp, scale=lgs[:, RH + h:RH + h + 1])
                yield

        side.extend((context_states(), decay_tables()))
        natural(dram["w_in_2"], Q2, h2_ok, plain(QX))
        q_ok = now(A)
        side.append(rotary(QX, "cosx", "sinx", RS, (q_ok,)))

        natural(dram["w_in_2"], K2, h2_ok, plain(KX))
        k_ok = now(A)
        side.append(rotary(KX, "cosx", "sinx", RS, (k_ok,)))
        MIXT = at(40, KD, T)
        CVC, CVU = at(78, RH, T), at(32, RH, T)
        c_ok = {}

        def hold(dst, key):
            def evac(i, view, m):
                c_ok[key] = acopy(dst[:, i, :], view, after=(m,))
                return c_ok[key]
            return evac

        transposed(dram["w_in_2"], CC2, h2_ok, hold(CVC, "c"))
        natural(dram["w_in_2"], V2, h2_ok, plain(VX))
        vx_ok = now(A)
        side_rest()
        states_pe, state_ok, xi_ok = ret["states_pe"], ret["state"], ret["xi"]
        V.wait(states_pe)
        rq, rk = rotated[1], rotated[2]
        QXT, KXT = at(86, RH, T), at(90, RH, T)
        flip_tokens(QXT, QX, RH, rq, turn_pair(QXT), pairs=True)
        qkx_ok = flip_tokens(KXT, KX, RH, rk,
                             turn_pair(KXT, RD ** -0.5), pairs=True)

        def g_evac(t, view, m):
            return act(GX[:, t, :], view, ACT.Silu, after=(m,))

        QS = at(94, 2, RH * T)
        for d in range(2):
            qs_ok = tt(QS[:, d, :].rearrange("p (h t) -> p h t", h=RH), QXT, XI[:, d, :, :], ALU.mult,
                       after=(qkx_ok, xi_ok))

        RP = [at(120 + 2 * i, NT, T) for i in range(2)]
        RY = at(124, NT, W)

        def ret_scores(h):
            b = 4 + h % 2
            PE.wait(bank_free[b], qkx_ok)
            for mt in range(NT):
                m = mm(ps[:, b, mt * T:(mt + 1) * T], KXT[:, h, mt * P:(mt + 1) * P], QXT[:, h, :], True, True,
                       signal=True)
            bank_free[b] = tt(RP[h % 2], ps[:, b, :].rearrange("p (a b) -> p a b", a=NT),
                              WT[:, h, :].rearrange("p (a b) -> p a b", a=NT), ALU.mult, after=(m, state_ok, xi_ok))
            return bank_free[b]

        def ret_values(h, ready):
            PE.wait(ready, qs_ok, state_ok, vx_ok)
            if h == 0:
                PE.wait(bank_free[6], bank_free[7])
            hs = slice(h * RD, (h + 1) * RD)
            for nt in range(NT):
                o = ps[:, 6 + nt, hs]
                ns = slice(nt * P, (nt + 1) * P)
                for mt in range(NT):
                    mm(o, RP[h % 2][:, mt, ns], VX[:, mt, hs], mt == 0, False)
                for d in range(2):
                    m = mm(o, QS[:, d, h * T + nt * P:h * T + (nt + 1) * P], SF[:, d, hs], False, d == 1,
                           signal=(d == 1))
            return m

        r = ret_scores(0)
        natural(dram["w_in_2"], G2, h2_ok, g_evac)
        ret_values(0, r)
        r = ret_scores(1)

        def u_evac(i, view, m):
            return tt(CVU[:, i, :], view, CVC[:, i, :], ALU.mult, after=(m, c_ok["c"]))

        transposed(dram["w_in_2"], CX2, h2_ok, u_evac)
        ret_values(1, r)
        r = ret_scores(2)
        w2, b2 = part(cols, COLS, "conv_w_2").rearrange("p (j c) -> p j c", j=3), part(cols, COLS, "conv_b_2")
        for i in range(4):
            o = MIXT[:, i, :].rearrange("p (r w) -> p r w", w=GRID_W)
            u = CVU[:, i, :].rearrange("p (r w) -> p r w", w=GRID_W)
            ts(MIXT[:, i, :], CVU[:, i, :], w2[:, 1, i:i + 1], b2[:, i:i + 1], ALU.mult, ALU.add)
            stt(o[:, :, 1:], u[:, :, :-1], w2[:, 0, i:i + 1], o[:, :, 1:], ALU.mult, ALU.add)
            conv2 = stt(o[:, :, :-1], u[:, :, 1:], w2[:, 2, i:i + 1], o[:, :, :-1], ALU.mult, ALU.add)
        ret_values(2, r)
        r = ret_scores(3)
        m = ret_values(3, r)
        rg = at(118, W)
        rg_in = load(rg, row("ret_norm_g").partition_broadcast(P), after=(qkx_ok,))
        gst = [at(kb, D) for kb in (68, 72, 36)]
        gains = (("post_mix_g", G1), ("pre_ffn_g", SC2), ("post_ffn_g", GG2))
        gins = [load(g, row(name).partition_broadcast(P), after=(qs_ok,)) for g, (name, _) in zip(gst, gains)]
        for t in range(NT):
            ry = bank_free[6 + t] = acopy(RY[:, t, :], ps[:, 6 + t, :], after=(m,))
        gmean = small(NT * RH)
        RY4, sq4 = RY.rearrange("p t (h e) -> p (t h) e", h=RH), at(120, NT * RH, RD)
        ret_done = []

        def group_norm():
            reduce(gmean, RY4, ALU.add, after=(ry,))
            ts(gmean, gmean, 1.0 / RD, None, ALU.mult)
            tt(RY4, RY4, gmean.unsqueeze(2).broadcast_to([P, NT * RH, RD]), ALU.subtract)
            yield
            tt(sq4, RY4, RY4, ALU.mult)
            m = reduce(ssq[:, 0:NT * RH], sq4, ALU.add)
            yield
            r = rstd(NT * RH, RD)
            tt(RY4, RY4, ssq[:, 0:NT * RH].unsqueeze(2).broadcast_to([P, NT * RH, RD]), ALU.mult, after=(r,))
            yield
            tt(RY, RY, rg.unsqueeze(1).broadcast_to([P, NT, W]), ALU.mult, after=(rg_in,))
            m = tt(RY, RY, GX, ALU.mult)
            ret_done.append(m)

        ret_pe = now(PE)
        side.append(group_norm())

        def b_evac(i, view, m):
            return tt(MIXT[:, i, :], MIXT[:, i, :], view, ALU.mult, after=(m,))

        transposed(dram["w_in_2"], CB2, h2_ok, b_evac, more=False)
        conv_done = bank_free[(turn[0] - 1) % 3]
        side_rest()
        ret_ok = ret_done[0]
        ACC = at(24, NT, D)
        acc0 = G.do(lambda e: e.memset(ACC, 0.0), (ret_ok, ret_pe))
        mix_ok = {}

        def flip_mixed():
            if not mix_ok:
                mix_ok[0] = flip_tokens(MIXT, RY, RH, ret_ok, turn_pair(MIXT[:, RH:, :]), pairs=True)
            return mix_ok[0]


        for i, (_, dst) in enumerate(gains):
            if i == 1:
                stt(dst, dst, 1.0, gst[i], ALU.add, ALU.mult, after=(gins[i], rows_ok))
            else:
                gains_ok = tt(dst, dst, gst[i], ALU.mult, after=(gins[i], rows_ok))
        M = at(8, NT, D)
        msq = small(NT, 2)

        H2, H2T = at(16, NT, D), at(40, KD, T)
        x2, h2 = [], []
        hsq = small(NT)
        aff, rmax = small(NT, NE), small(NT)

        def m_evac(t, n, view, m):
            act(TA[:, t, :], view, ACT.Square, accum=msq[:, t, n:n + 1], after=(m, ret_ok))
            return acopy(M[:, t, n * W:(n + 1) * W], view)

        def second_norms(t):
            x, v, h = X[:, t, :], msq[:, t, 0:1], hsq[:, t:t + 1]
            tt(v, v, msq[:, t, 1:2], ALU.add, after=(now(A),))
            m = column_rstd(v, D)
            stt(M[:, t, :], M[:, t, :], v, G1, ALU.mult, ALU.mult, after=(m,))
            x2.append(tt(x, x, M[:, t, :], ALU.add))
            m = act(H2[:, t, :], x, ACT.Square, accum=h, after=(x2[t],))
            m = column_rstd(h, D, (m,))
            stt(H2[:, t, :], x, h, SC2, ALU.mult, ALU.mult, after=(m,))
            h2.append(tt(H2[:, t, :], H2[:, t, :], SH2, ALU.add))

        def route(t):
            for g in range(2):
                b = 6 + g
                PE.wait(bank_free[b], h2[t])
                for k in range(4):
                    m = flip(ps[:, b, k * P:(k + 1) * P], H2[:, t, (4 * g + k) * P:(4 * g + k + 1) * P], signal=(k == 3))
                bank_free[b] = acopy(H2T[:, 4 * g:4 * g + 4, t * P:(t + 1) * P],
                                     ps[:, b, :].rearrange("p (k n) -> p k n", k=4), after=(m,))
            PE.wait(bank_free[4 + t], wr_in, bank_free[6], bank_free[7])
            for k in range(KD):
                m = mm(ps[:, 4 + t, 0:NE], H2T[:, k, t * P:(t + 1) * P], wr[:, k, :], k == 0, k == KD - 1,
                       signal=(k == KD - 1))
            a_, r_ = aff[:, t, :], rmax[:, t:t + 1]
            bank_free[4 + t] = tt(a_, ps[:, 4 + t, 0:NE], brt, ALU.add, after=(m, brt_in))
            reduce(r_, a_, ALU.max)
            m = ts(a_, a_, r_, None, ALU.subtract)
            m = act(a_, a_, ACT.Exp, accum=r_, after=(m,))
            recip(r_, r_, after=(m,))
            return ts(a_, a_, r_, None, ALU.mult)

        by_tile(lambda k, t: MIXT[:, k, t * P:(t + 1) * P], dram["w_out_2"], [(0, conv_done), (1, flip_mixed)],
                m_evac, second_norms)
        if tap:
            load(dram["tap2"].rearrange("(t p) d -> p t d", p=P), X, after=x2)
        routed = [route(t) for t in range(NT)]
        PE.wait(bank_free[5], *routed)
        for t in range(NT):
            m = flip(ps[0:NE, 5, t * P:(t + 1) * P], aff[:, t, :], signal=True)
        affT, one_row = at(36, T)[0:NE, :], at(37, T)[0:NE, :]
        bank_free[5] = aff_ok = vcopy(affT, ps[0:NE, 5, 0:T], after=(m,))
        before = part(late, LATE, "before").rearrange("p (t s) -> p t s", t=NT)

        ONE = small(NT, CAP)
        Z = at(40, NT, P)
        GT = at(52, 2, T)
        XS, XT = at(43, T), at(44, 2, P)
        SG, HD, HTT, YS = at(45, W), at(47, W), at(49, 4, P), at(38, W)
        gz = G.do(lambda e: e.memset(GT, 0.0), (ret_pe,))
        own, over, same, rank = small(NT), small(NT), small(NT), small(NT)
        junk = at(120, 4, T)
        onesr = at(124, P)
        ones_ok = G.do(lambda e: e.memset(onesr, 1.0), (m, mix_ok[0]))
        RING2 = 12
        more_slots = ((56, ret_ok), (66, gains_ok), (82, ret_pe), (90, ret_pe), (74, conv_done), (8, x2[1]), (98, x2[1]),
                      (106, h2[1]))
        extra = [at(kb, SLOT) for kb, _ in more_slots]
        early_slots = list(range(RING, RING + 5))
        order = (early_slots + [(chunks[0] + c) % RING for c in range(RING)]
                 + list(range(RING + len(early_slots), RING2)))
        landed += [sem(f"landed{i}") for i in range(RING, RING2)]
        landed_before = [chunks[0] // RING + (1 if s < chunks[0] % RING else 0) for s in range(RING)]
        landed_before += [0] * (RING2 - RING)
        NCH = 3 * KD
        wg, wu, wd = dram["w_gate"], dram["w_up"], dram["w_down"]
        wd_chunks = wd.rearrange("e (c k p) n -> (e c) p k n", k=2, p=P)
        p_use = sem("p_use")

        def chunk_src(e_, c):
            if c < 2 * KD:
                w_ = wg if c < KD else wu
                return w_[e_, (c % KD) * P:(c % KD + 1) * P, :]
            return wd[e_, (c - 2 * KD) * 2 * P:(c - 2 * KD + 1) * 2 * P, :].rearrange("(k p) n -> p k n", p=P)

        def chunk_slot(c):
            s = order[c % RING2]
            v = ring[:, s, :] if s < RING else extra[s - RING]
            return s, (v if c < 2 * KD else v.rearrange("p (k n) -> p k n", k=2))

        def fetch(e, e_, c):
            s, dst = chunk_slot(c)
            e.dma_start(dst, chunk_src(e_, c)).then_inc(landed[s], 16)

        for c in range(RING2):
            s, _ = chunk_slot(c)
            SP.wait(*((freed[s],) if s < RING else (ret_pe, ret_ok, more_slots[s - RING][1])))
            SP.items.append(lambda e, c=c: fetch(e, 0, c))

        def sp_experts(e):
            with e.Fori(0, NE - 1) as i:
                for c in range(NCH):
                    nxt = c + RING2
                    src = chunk_src_dyn(i, nxt) if nxt < NCH else chunk_src_dyn(i + 1, nxt - NCH)
                    s, dst = chunk_slot(nxt % NCH)
                    e.wait_ge(p_use, i * NCH + (c + 1))
                    e.dma_start(dst, src).then_inc(landed[s], 16)
            for c in range(NCH - RING2):
                e.wait_ge(p_use, (NE - 1) * NCH + c + 1)
                fetch(e, NE - 1, c + RING2)

        def chunk_src_dyn(i, c):
            if c < 2 * KD:
                w_ = wg if c < KD else wu
                return w_[bass.ds(i, 1), (c % KD) * P:(c % KD + 1) * P, :].rearrange("o p n -> p (o n)")
            return wd_chunks[bass.ds(i * KD + (c - 2 * KD), 1), :, :, :].rearrange("o p k n -> p (o k) n")

        SP.items.append(sp_experts)

        names = ("v_sel", "p_row", "v_r0", "v_r1", "v_r2", "v_one", "v_gt", "v_hd", "p_gath", "p_xt", "p_ht", "p_dn", "a_xs", "a_xt",
                 "a_sg", "a_ht", "a_y", "v_acc0", "v_acc1", "p_sc0", "p_sc1")
        ev = {n: sem(n) for n in names}

        def prime(e, who):
            for n in names:
                if n[0] == who:
                    e.sem_inc(ev[n], 1)

        SLOTS_BACK = NCH // RING2

        def pe_experts(e):
            prime(e, "p")
            with e.Fori(0, NE) as i:
                prev, this = i + 1, i + 2
                e.wait_ge(ev["v_sel"], this)
                e.wait_ge(ev["v_gt"], prev)
                e.matmul(ps[:, 1, T:2 * T], onesr[0:NE, :], one_row, start=True, stop=True,
                         skip_group_check=True).then_inc(ev["p_row"], 1)
                e.wait_ge(ev["v_one"], this)
                e.wait_ge(ev["a_xt"], prev)
                for t in range(NT):
                    for j in range(4):
                        e.matmul(ps[32 * j:32 * j + 32, 0, 0:T], ONE[:, t, :], H2[:, t, j * T:(j + 1) * T],
                                 start=(t == 0), stop=(t == NT - 1), skip_group_check=True)
                for t in range(NT):
                    ins = e.transpose(ps[:, 1, t * P:(t + 1) * P], Z[:, t, :], ident)
                ins.then_inc(ev["p_gath"], 1)
                e.wait_ge(ev["a_xs"], this)
                for b in range(2):
                    ins = e.transpose(ps[:, 0, T + b * P:T + (b + 1) * P], XS[:, b * P:(b + 1) * P], ident)
                ins.then_inc(ev["p_xt"], 1)
                e.wait_ge(ev["a_xt"], this)
                for c in range(2 * KD):
                    k = c % KD
                    if c == 0:
                        e.wait_ge(ev["a_sg"], prev)
                    if c == KD:
                        e.wait_ge(ev["v_hd"], prev)
                    s, slot = chunk_slot(c)
                    e.wait_ge(landed[s], i * (16 * SLOTS_BACK) + 16 * (landed_before[s] + c // RING2 + 1))
                    for n in range(4):
                        ins = e.matmul(ps[32 * n:32 * n + 32, 2 + c // KD, :],
                                       XT[:, k % 2, 32 * (k // 2):32 * (k // 2) + 32], slot[:, n * W:(n + 1) * W],
                                       start=(k == 0), stop=(k == KD - 1), skip_group_check=True)
                    ins.then_inc(p_use, 1)
                e.wait_ge(ev["v_hd"], this)
                e.wait_ge(ev["a_ht"], prev)
                for b in range(4):
                    ins = e.transpose(ps[:, 4, b * P:(b + 1) * P], HD[:, b * P:(b + 1) * P], ident)
                ins.then_inc(ev["p_ht"], 1)
                e.wait_ge(ev["a_ht"], this)
                e.wait_ge(ev["a_y"], prev)
                for c in range(2 * KD, NCH):
                    s, slot = chunk_slot(c)
                    e.wait_ge(landed[s], i * (16 * SLOTS_BACK) + 16 * (landed_before[s] + c // RING2 + 1))
                    for kk in range(2):
                        f = 2 * (c - 2 * KD) + kk
                        for nd in range(2):
                            g = 2 * nd + kk
                            ins = e.matmul(ps[32 * g:32 * g + 32, 5, :],
                                           HTT[:, f % 4, 32 * (f // 4):32 * (f // 4) + 32],
                                           slot[:, kk, nd * W:(nd + 1) * W],
                                           start=(c == 2 * KD), stop=(c == NCH - 1), skip_group_check=True)
                    ins.then_inc(p_use, 1)
                e.wait_ge(ev["a_y"], this)
                e.wait_ge(ev["v_gt"], this)
                for t in range(NT):
                    e.wait_ge(ev["v_acc0"], prev) if t == 0 else e.wait_ge(ev["v_acc0"], this)
                    for nd in range(2):
                        ins = e.matmul(ps[:, 6 + nd, :], GT[:, nd, t * P:(t + 1) * P], YS[:, :],
                                       start=True, stop=True, skip_group_check=True)
                    ins.then_inc(ev[f"p_sc{t}"], 1)

        def act_experts(e):
            prime(e, "a")
            with e.Fori(0, NE) as i:
                prev, this = i + 1, i + 2
                e.wait_ge(ev["p_gath"], this)
                e.wait_ge(ev["p_xt"], prev)
                e.activation(XS, ps[:, 0, 0:T], ACT.Copy).then_inc(ev["a_xs"], 1)
                e.wait_ge(ev["p_xt"], this)
                e.activation(XT.rearrange("p a b -> p (a b)"), ps[:, 0, T:2 * T], ACT.Copy).then_inc(ev["a_xt"], 1)
                e.wait_ge(p_use, i * NCH + KD)
                e.wait_ge(ev["v_hd"], prev)
                e.activation(SG, ps[:, 2, :], ACT.Silu).then_inc(ev["a_sg"], 1)
                e.wait_ge(ev["p_ht"], this)
                e.activation(HTT.rearrange("p a b -> p (a b)"), ps[:, 4, :], ACT.Copy).then_inc(ev["a_ht"], 1)
                e.wait_ge(p_use, i * NCH + NCH)
                e.wait_ge(ev["p_sc1"], prev)
                e.activation(YS, ps[:, 5, :], ACT.Copy).then_inc(ev["a_y"], 1)

        def dve_experts(e):
            prime(e, "v")
            with e.Fori(0, NE) as i:
                prev, this = i + 1, i + 2
                e.wait_ge(ev["p_row"], prev)
                e.tensor_scalar(one_row, affT, ident[0:NE, bass.ds(i, 1)], None, ALU.mult).then_inc(ev["v_sel"], 1)
                e.wait_ge(ev["p_row"], this)
                e.wait_ge(ev["p_gath"], prev)
                row_ = ps[:, 1, T:2 * T]
                for t in range(NT):
                    ins = e.scalar_tensor_tensor(out=junk[:, t, 0:P], in0=row_[:, t * P:(t + 1) * P], scalar=1.0,
                                                 in1=ident, op0=ALU.mult, op1=ALU.mult, accum_out=own[:, t:t + 1])
                ins.then_inc(ev["v_r0"], 1)
                e.wait_ge(ev["v_r0"], this)
                for t in range(NT):
                    e.tensor_scalar(junk[:, t, :], row_, own[:, t:t + 1], 0.0, ALU.is_gt, ALU.add,
                                    accum_out=over[:, t:t + 1])
                    ins = e.scalar_tensor_tensor(out=junk[:, 2 + t, :], in0=row_, scalar=own[:, t:t + 1],
                                                 in1=before[:, t, :], op0=ALU.is_equal, op1=ALU.mult,
                                                 accum_out=same[:, t:t + 1])
                ins.then_inc(ev["v_r1"], 1)
                e.wait_ge(ev["v_r1"], this)
                e.tensor_tensor(rank, over, same, ALU.add).then_inc(ev["v_r2"], 1)
                e.wait_ge(ev["v_r2"], this)
                for t in range(NT):
                    e.tensor_scalar(ONE[:, t, :], iota[:, 0:CAP], rank[:, t:t + 1], None, ALU.is_equal)
                    ins = e.tensor_scalar(Z[:, t, :], iota, rank[:, t:t + 1], own[:, t:t + 1], ALU.is_equal, ALU.mult)
                ins.then_inc(ev["v_one"], 1)
                e.wait_ge(ev["p_gath"], this)
                e.wait_ge(ev["p_sc1"], prev)
                e.tensor_copy(GT[0:64, 0, :], ps[0:64, 1, 0:T])
                e.tensor_copy(GT[64:128, 1, :], ps[64:128, 1, 0:T]).then_inc(ev["v_gt"], 1)
                e.wait_ge(ev["a_sg"], this)
                e.wait_ge(p_use, i * NCH + 2 * KD)
                e.wait_ge(ev["p_ht"], prev)
                e.tensor_tensor(HD, SG, ps[:, 3, :], ALU.mult).then_inc(ev["v_hd"], 1)
                for t in range(NT):
                    e.wait_ge(ev[f"p_sc{t}"], this)
                    e.wait_ge(ev[f"v_acc{t}"], prev)
                    a_ = ACC[:, t, :].rearrange("p (n w) -> p n w", n=2)
                    e.tensor_tensor(a_, a_, ps[:, 6:8, :], ALU.add).then_inc(ev[f"v_acc{t}"], 1)

        for q in (PE, A, V):
            q.wait(aff_ok, acc0, gz, ones_ok, now(A), now(PE))
        PE.items.append(pe_experts)
        A.items.append(act_experts)
        V.items.append(dve_experts)
        acc_done = (ev["v_acc1"], NE + 1)
        G.wait(acc_done)
        for q in (A, V):
            q.wait(acc_done, (ev["v_acc0"], NE + 1))

        OUTT = at(16, NT, D)
        if tap:
            load(dram["tap3"].rearrange("(t p) d -> p t d", p=P), ACC, after=(acc_done,))
        stores = []
        osq = small(NT)
        for t in range(NT):
            m = act(OUTT[:, t, :], ACC[:, t, :], ACT.Square, accum=osq[:, t:t + 1])
            m = column_rstd(osq[:, t:t + 1], D, (m,))
            stt(OUTT[:, t, :], ACC[:, t, :], osq[:, t:t + 1], GG2, ALU.mult, ALU.mult, after=(m,))
            m = tt(OUTT[:, t, :], OUTT[:, t, :], X[:, t, :], ALU.add)
            stores.append(load(out[t * P:(t + 1) * P, :], OUTT[:, t, :], after=(m,)))
        SP.wait(*stores)

        block = ctx.enter_context(nc.Block())

        @block.sync
        def _(e):
            for item in SP.items:
                item(e)

        @block.tensor
        def _(e):
            for item in PE.items:
                item(e)

        @block.vector
        def _(e):
            for item in V.items:
                item(e)

        @block.scalar
        def _(e):
            for item in A.items:
                item(e)

        @block.gpsimd
        def _(e):
            for item in G.items:
                item(e)


def arrange(inputs):
    a = {k: np.asarray(v) for k, v in inputs.items()}

    def col(v):
        v = np.asarray(v)
        v = v.reshape(-1, P)
        return v.T

    pack = {
        "c": col(a["c"]), "c_2": col(a["c_2"]), "c_ctx": col(a["c_ctx_2"]), "conv_w": col(a["conv_w"]),
        "conv_b": col(a["conv_b"]), "norm_g": col(a["norm_g"]), "mnorm_g": col(a["mnorm_g"]),
        "anorm_g": col(a["anorm_g"]), "pre_mix_g": col(a["pre_mix_g_2"]), "conv_w_2": col(a["conv_w_2"]),
        "conv_b_2": col(a["conv_b_2"]),
    }
    cols = np.zeros((P, COLS["all"][1]), np.float32)
    for name, v in pack.items():
        s, n = COLS[name]
        cols[:, s:s + n] = v
    s, n = COLS["b_if"]
    cols[0:MH, s:s + 2] = a["b_if"].reshape(2, MH).T
    rows = np.concatenate([a[n].reshape(-1) for n in (
        "b_ada", "b_ada_2", "final_g", "post_mix_g_2", "pre_ffn_g_2", "post_ffn_g_2", "ret_norm_g_2",
        "b_router_2", "ret_decay_logit_2", "lam_q1", "lam_k1", "lam_q2", "lam_k2")])
    big = {
        "x": a["x"][0], "ctx": a["ctx_2"][0], "w_ada": a["w_ada"][0], "w_in": a["w_in"][0],
        "w_proj_m": a["w_proj_m"][0], "w_proj_a": a["w_proj_a"][0], "w_out": a["w_out"][0],
        "rel_bias": a["rel_bias"], "w_ada_2": a["w_ada_2"][0], "w_in_2": a["w_in_2"][0],
        "w_out_2": a["w_out_2"][0], "w_router": a["w_router_2"][0], "w_gate": a["w_gate_2"][0],
        "w_up": a["w_up_2"][0], "w_down": a["w_down_2"][0], "rows": rows, "cols": cols,
    }
    return {**big, **constants()}


def program(nc, arrays, tap=None):
    dram = {n: nc.dram_tensor(f"in_{n}", v.shape, F32, kind="ExternalInput").ap() for n, v in arrays.items()}
    dram["toeplitz"] = nc.dram_tensor("toeplitz", (AH * 2 * T,), F32, kind="Internal").ap()
    dram["mods"] = nc.dram_tensor("mods", (5 * D,), F32, kind="Internal").ap()
    for n in (tap or ()):
        dram[n] = nc.dram_tensor(n, (T, D), F32, kind="ExternalOutput").ap()
    out = nc.dram_tensor("out", (T, D), F32, kind="ExternalOutput").ap()
    build(nc, dram, out, tap)


def kernel(**inputs):
    import concourse.bacc as _bacc
    from concourse.bass_utils import run_bass_kernel_spmd as _run

    arrays = {n: np.ascontiguousarray(v) for n, v in arrange(inputs).items()}
    nc = _bacc.Bacc("TRN2", target_bir_lowering=False, num_devices=1)
    program(nc, arrays)
    r = _run(nc, [{f"in_{n}": v for n, v in arrays.items()}], core_ids=[0])
    return r.results[0]["out"].reshape(1, T, D)
```
